# Optimizing a Trainium2 kernel written in Bass

```python
import jax, jax.numpy as jnp
from jax import lax
import numpy as np

D_MODEL = 1024
BATCH = 1
SEQ = 2048
DEPTH = 1

D_MIX = D_MODEL
D_REC = D_MIX // 2
D_ATT = D_MIX - D_REC
N_LRU_BLOCKS = 8
LRU_BLOCK = D_REC // N_LRU_BLOCKS
LRU_C = 8.0
CONV_WIDTH = 4
HEAD_DIM = 64
N_HEADS = D_ATT // HEAD_DIM
DILATED_PATTERNS = ((128, 1), (512, 4), (2048, 16))
ROPE_THETA = 10000.0
NORM_EPS = 1e-6
NEG_INF = -1e30
D_IN_PROJ = 2 * D_REC + 4 * D_ATT
SPLIT_IDX = (D_REC, 2 * D_REC, 2 * D_REC + D_ATT, 2 * D_REC + 2 * D_ATT, 2 * D_REC + 3 * D_ATT)


def rms_norm(x, g):
    xf = x.astype(jnp.float32)
    y = xf * lax.rsqrt(jnp.mean(xf * xf, axis=-1, keepdims=True) + NORM_EPS)
    return (y * g.astype(jnp.float32)).astype(x.dtype)

def rotary(x, positions):
    half = HEAD_DIM // 2
    inv_freq = ROPE_THETA ** (-jnp.arange(half, dtype=jnp.float32) / half)
    ang = positions.astype(jnp.float32)[..., None] * inv_freq
    cos = jnp.cos(ang)[:, :, None, :]
    sin = jnp.sin(ang)[:, :, None, :]
    xf = x.astype(jnp.float32)
    x1, x2 = xf[..., :half], xf[..., half:]
    out = jnp.concatenate([x1 * cos - x2 * sin, x2 * cos + x1 * sin], axis=-1)
    return out.astype(x.dtype)

def causal_depthwise_conv(x, w, b):
    S = x.shape[1]
    xp = jnp.pad(x, ((0, 0), (CONV_WIDTH - 1, 0), (0, 0)))
    return sum(xp[:, k:k + S, :] * w[k] for k in range(CONV_WIDTH)) + b

def rg_lru(x, w_a, b_a, w_x, b_x, lam):
    B, S, C = x.shape
    xb = x.reshape(B, S, N_LRU_BLOCKS, LRU_BLOCK)
    r = jax.nn.sigmoid(jnp.einsum('bshi,hij->bshj', xb, w_a).reshape(B, S, C) + b_a)
    i = jax.nn.sigmoid(jnp.einsum('bshi,hij->bshj', xb, w_x).reshape(B, S, C) + b_x)
    log_a = -LRU_C * r.astype(jnp.float32) * jax.nn.softplus(-lam.astype(jnp.float32))
    a = jnp.exp(log_a)
    mult = jnp.sqrt(-jnp.expm1(2.0 * log_a))
    u = mult * (i * x).astype(jnp.float32)

    def combine(left, right):
        a_l, b_l = left
        a_r, b_r = right
        return a_l * a_r, a_r * b_l + b_r

    _, h = lax.associative_scan(combine, (a, u), axis=1)
    return h.astype(x.dtype)

def dilated_attention(q, k, v, window, dilation):
    B, H, S, Dh = q.shape
    L = S // dilation
    blk = window // dilation
    n_blk = -(-L // blk)
    pad = n_blk * blk - L

    def to_blocks(t):
        t = t.reshape(B, H, L, dilation, Dh).transpose(0, 1, 3, 2, 4)
        t = jnp.pad(t, ((0, 0), (0, 0), (0, 0), (0, pad), (0, 0)))
        return t.reshape(B, H, dilation, n_blk, blk, Dh)

    def with_prev(t):
        prev = jnp.pad(t, ((0, 0), (0, 0), (0, 0), (1, 0), (0, 0), (0, 0)))[:, :, :, :-1]
        return jnp.concatenate([prev, t], axis=4)

    qb = to_blocks(q)
    kc = with_prev(to_blocks(k))
    vc = with_prev(to_blocks(v))
    scores = jnp.einsum('bhrnqd,bhrnkd->bhrnqk', qb, kc, preferred_element_type=jnp.float32)
    qi = jnp.arange(blk)[:, None]
    ki = jnp.arange(2 * blk)[None, :]
    dist = qi + blk - ki
    blk_idx = jnp.arange(n_blk)[:, None, None]
    valid = ((dist >= 0) & (dist <= blk))[None] & (blk_idx * blk + ki[None] - blk >= 0)
    scores = jnp.where(valid, scores, NEG_INF)
    m = jnp.max(scores, axis=-1, keepdims=True)
    p = jnp.exp(scores - m)
    denom = jnp.sum(p, axis=-1, keepdims=True)
    out = jnp.einsum('bhrnqk,bhrnkd->bhrnqd', p, vc.astype(jnp.float32)) / denom
    lse = (m + jnp.log(denom))[..., 0]

    def from_blocks(t):
        t = t.reshape(B, H, dilation, n_blk * blk, *t.shape[5:])[:, :, :, :L]
        t = jnp.moveaxis(t, 2, 3)
        return t.reshape(B, H, S, *t.shape[4:])

    return from_blocks(out), from_blocks(lse)

def first_inputs(seed: int = 0) -> dict:
    key = jax.random.key(seed)
    ks = jax.random.split(key, 20)
    D = D_MODEL
    nrm = lambda k, shape, fan_in: jax.random.normal(k, shape, jnp.float32) * fan_in ** -0.5
    x = jax.random.normal(ks[0], (BATCH, SEQ, D), jnp.float32)
    c = jax.random.normal(ks[1], (BATCH, D), jnp.float32)
    offsets = jax.random.randint(ks[2], (BATCH, 1), 0, 4096, dtype=jnp.int32)
    positions = offsets + jnp.arange(SEQ, dtype=jnp.int32)[None, :]
    w_ada = nrm(ks[3], (DEPTH, D, 3 * D), D) * 0.5
    b_ada = 0.02 * jax.random.normal(ks[4], (DEPTH, 3 * D), jnp.float32)
    norm_pre = 1.0 + 0.1 * jax.random.normal(ks[5], (DEPTH, D), jnp.float32)
    norm_post = 1.0 + 0.1 * jax.random.normal(ks[6], (DEPTH, D), jnp.float32)
    w_in = nrm(ks[7], (DEPTH, D, D_IN_PROJ), D)
    conv_w = nrm(ks[8], (DEPTH, CONV_WIDTH, D_REC), CONV_WIDTH)
    conv_b = 0.02 * jax.random.normal(ks[9], (DEPTH, D_REC), jnp.float32)
    w_rg_a = nrm(ks[10], (DEPTH, N_LRU_BLOCKS, LRU_BLOCK, LRU_BLOCK), LRU_BLOCK)
    b_rg_a = 0.02 * jax.random.normal(ks[11], (DEPTH, D_REC), jnp.float32)
    w_rg_x = nrm(ks[12], (DEPTH, N_LRU_BLOCKS, LRU_BLOCK, LRU_BLOCK), LRU_BLOCK)
    b_rg_x = 0.02 * jax.random.normal(ks[13], (DEPTH, D_REC), jnp.float32)
    a_c = jax.random.uniform(ks[14], (DEPTH, D_REC), jnp.float32, 0.9, 0.999)
    a_base = a_c ** (1.0 / LRU_C)
    lru_lambda = jnp.log(a_base) - jnp.log1p(-a_base)
    norm_rec = 1.0 + 0.1 * jax.random.normal(ks[15], (DEPTH, D_REC), jnp.float32)
    norm_att = 1.0 + 0.1 * jax.random.normal(ks[16], (DEPTH, D_ATT), jnp.float32)
    w_out = nrm(ks[17], (DEPTH, D_MIX, D), D_MIX)
    return {'x': x, 'c': c, 'positions': positions, 'w_ada': w_ada, 'b_ada': b_ada,
            'norm_pre': norm_pre, 'norm_post': norm_post, 'w_in': w_in, 'conv_w': conv_w,
            'conv_b': conv_b, 'w_rg_a': w_rg_a, 'b_rg_a': b_rg_a, 'w_rg_x': w_rg_x,
            'b_rg_x': b_rg_x, 'lru_lambda': lru_lambda, 'norm_rec': norm_rec,
            'norm_att': norm_att, 'w_out': w_out}

def first_block(x, c, positions, w_ada, b_ada, norm_pre, norm_post, w_in, conv_w, conv_b,
              w_rg_a, b_rg_a, w_rg_x, b_rg_x, lru_lambda, norm_rec, norm_att, w_out):
    B, S, _ = x.shape
    for l in range(DEPTH):
        mod = jnp.einsum('bd,de->be', jax.nn.silu(c), w_ada[l]) + b_ada[l]
        shift, scale, gate = jnp.split(mod, 3, axis=-1)
        h = rms_norm(x, norm_pre[l]) * (1.0 + scale[:, None, :]) + shift[:, None, :]

        proj = jnp.einsum('bsd,de->bse', h, w_in[l])
        xa, ga, q, k, v, gb = jnp.split(proj, SPLIT_IDX, axis=-1)

        xa = causal_depthwise_conv(xa, conv_w[l], conv_b[l])
        ya = rg_lru(xa, w_rg_a[l], b_rg_a[l], w_rg_x[l], b_rg_x[l], lru_lambda[l]) * jax.nn.silu(ga)
        ya = rms_norm(ya, norm_rec[l])

        heads = lambda t: t.reshape(B, S, N_HEADS, HEAD_DIM)
        qh = (rotary(heads(q), positions) * HEAD_DIM ** -0.5).transpose(0, 2, 1, 3)
        kh = rotary(heads(k), positions).transpose(0, 2, 1, 3)
        vh = heads(v).transpose(0, 2, 1, 3)
        outs, lses = zip(*[dilated_attention(qh, kh, vh, w, d) for (w, d) in DILATED_PATTERNS])
        wts = jax.nn.softmax(jnp.stack(lses, axis=0), axis=0)
        att = jnp.einsum('pbhs,pbhsd->bhsd', wts, jnp.stack(outs, axis=0))
        yb = att.transpose(0, 2, 1, 3).reshape(B, S, D_ATT).astype(x.dtype) * jax.nn.silu(gb)
        yb = rms_norm(yb, norm_att[l])

        mix = jnp.einsum('bse,ed->bsd', jnp.concatenate([ya, yb], axis=-1), w_out[l])
        x = x + gate[:, None, :] * rms_norm(mix, norm_post[l])
    return x


DEPTH_2 = 2

GRID_W = 64
CTX_LEN = 256
BRANCH = 256
MIX_WIDTH = 4 * BRANCH
CONV_K = 3
ATT_HEADS = 4
ATT_KV_HEADS = 2
Q_BLOCK = 128
HG_HEADS = 4
HG_DK = BRANCH // HG_HEADS
HG_DV = BRANCH // HG_HEADS
HG_CHUNK = 64
FN_GROUPS = 4
FN_DIM = BRANCH // FN_GROUPS
EPS = 1e-6

IN_SPLITS = (256, 256, 256, 256,
             256, 128, 128, 256,
             256, 256, 256, 256, 256,
             256, 256)
IN_COLS = 3584


def rms_norm_2(x, g):
    xf = x.astype(jnp.float32)
    y = xf * lax.rsqrt(jnp.mean(xf * xf, axis=-1, keepdims=True) + EPS)
    return (y * g.astype(jnp.float32)).astype(x.dtype)

def split_cols(t):
    points = [int(p) for p in np.cumsum(IN_SPLITS)[:-1]]
    return jnp.split(t, points, axis=-1)

def axial_rope_tables(rows, dtype):
    r, cidx = jnp.meshgrid(jnp.arange(rows), jnp.arange(GRID_W), indexing="ij")
    r = r.reshape(-1).astype(jnp.float32)
    cidx = cidx.reshape(-1).astype(jnp.float32)
    n_pairs = HEAD_DIM // 4
    freqs = ROPE_THETA ** (-jnp.arange(n_pairs, dtype=jnp.float32) / n_pairs)
    ang = jnp.concatenate([r[:, None] * freqs, cidx[:, None] * freqs], axis=-1)
    return jnp.cos(ang).astype(dtype), jnp.sin(ang).astype(dtype)

def apply_rope(x, cos, sin):
    x1, x2 = x[..., 0::2], x[..., 1::2]
    return jnp.stack([x1 * cos - x2 * sin, x1 * sin + x2 * cos], axis=-1).reshape(x.shape)

def to_heads(t, n_heads):
    b, n, _ = t.shape
    return t.reshape(b, n, n_heads, -1).transpose(0, 2, 1, 3)

def from_heads(t):
    b, h, n, d = t.shape
    return t.transpose(0, 2, 1, 3).reshape(b, n, h * d)

def short_conv(u, w):
    up = jnp.pad(u, ((0, 0), (1, 1), (0, 0)))
    return up[:, :-2] * w[0] + up[:, 1:-1] * w[1] + up[:, 2:] * w[2]

def attend(qb, k, v):
    s = jnp.einsum("bhgqd,bhkd->bhgqk", qb, k).astype(jnp.float32) * (HEAD_DIM ** -0.5)
    p = jax.nn.softmax(s, axis=-1).astype(v.dtype)
    return jnp.einsum("bhgqk,bhkd->bhgqd", p, v)

def gqa_branch(q_l, k_l, v_l, q_c, k_c, v_c, q_g, k_g, cos, sin, need_ctx):
    b, n, _ = q_l.shape
    g = ATT_HEADS // ATT_KV_HEADS
    ql = apply_rope(rms_norm_2(to_heads(q_l, ATT_HEADS), q_g), cos, sin)
    kl = apply_rope(rms_norm_2(to_heads(k_l, ATT_KV_HEADS), k_g), cos, sin)
    vl = to_heads(v_l, ATT_KV_HEADS)
    kc = rms_norm_2(to_heads(k_c, ATT_KV_HEADS), k_g)
    vc = to_heads(v_c, ATT_KV_HEADS)
    k_all = jnp.concatenate([kl, kc], axis=2)
    v_all = jnp.concatenate([vl, vc], axis=2)
    nb = n // Q_BLOCK
    qb = ql.reshape(b, ATT_KV_HEADS, g, nb, Q_BLOCK, HEAD_DIM).transpose(3, 0, 1, 2, 4, 5)
    ob = lax.map(lambda blk: attend(blk, k_all, v_all), qb)
    o_lat = ob.transpose(1, 0, 4, 2, 3, 5).reshape(b, n, ATT_HEADS * HEAD_DIM)
    o_ctx = None
    if need_ctx:
        nc = q_c.shape[1]
        qc = rms_norm_2(to_heads(q_c, ATT_HEADS), q_g).reshape(b, ATT_KV_HEADS, g, nc, HEAD_DIM)
        oc = attend(qc, kc, vc)
        o_ctx = oc.transpose(0, 3, 1, 2, 4).reshape(b, nc, ATT_HEADS * HEAD_DIM)
    return o_lat, o_ctx

def hgrn_lower_bounds(lb_param):
    p = jax.nn.softmax(lb_param.astype(jnp.float32), axis=1)
    cs = jnp.cumsum(p, axis=1)
    return cs - cs[:, :1]

def hgrn_gates(fx, lb):
    fx = fx.astype(jnp.float32)
    log_f = jnp.logaddexp(jnp.log(lb), jnp.log1p(-lb) + jax.nn.log_sigmoid(fx))
    k = (1.0 - lb) * jax.nn.sigmoid(-fx)
    return log_f, k

def hgrn_scan(q, k, v, log_f, s0, with_output):
    b, h, t, _ = q.shape
    n = t // HG_CHUNK

    def chunks(a):
        return a.astype(jnp.float32).reshape(b, h, n, HG_CHUNK, a.shape[-1]).transpose(2, 0, 1, 3, 4)

    causal = jnp.tril(jnp.ones((HG_CHUNK, HG_CHUNK), dtype=bool))[:, :, None]

    def step(state, inp):
        qc, kc, vc, lf = inp
        a = jnp.cumsum(lf, axis=2)
        a_last = a[:, :, -1:, :]
        s_new = jnp.exp(a_last)[:, :, 0, :, None] * state + jnp.einsum(
            "bhsk,bhsv->bhkv", kc * jnp.exp(a_last - a), vc)
        if not with_output:
            return s_new, None
        inter = jnp.einsum("bhtk,bhkv->bhtv", qc * jnp.exp(a), state)
        diff = a[:, :, :, None, :] - a[:, :, None, :, :]
        dec = jnp.exp(jnp.where(causal, diff, -jnp.inf))
        scores = jnp.einsum("bhtk,bhsk,bhtsk->bhts", qc, kc, dec)
        intra = jnp.einsum("bhts,bhsv->bhtv", scores, vc)
        return s_new, inter + intra

    s_fin, out = lax.scan(step, s0, (chunks(q), chunks(k), chunks(v), chunks(log_f)))
    if with_output:
        out = out.transpose(1, 2, 0, 3, 4).reshape(b, h, t, v.shape[-1])
    return s_fin, out

def hgrn_branch(q_l, ff_l, fb_l, i_l, q_c, ff_c, fb_c, i_c, lb, hg_g, need_ctx):
    b = q_l.shape[0]
    ql = to_heads(jax.nn.silu(q_l), HG_HEADS)
    il = to_heads(i_l, HG_HEADS)
    qc = to_heads(jax.nn.silu(q_c), HG_HEADS)
    ic = to_heads(i_c, HG_HEADS)
    o_lat, o_ctx = 0.0, 0.0
    for d, (f_l, f_c) in enumerate(((ff_l, ff_c), (fb_l, fb_c))):
        flip = (lambda a: a[:, :, ::-1]) if d == 1 else (lambda a: a)
        logf_l, k_l = hgrn_gates(f_l, lb[d])
        logf_c, k_c = hgrn_gates(f_c, lb[d])
        s0 = jnp.zeros((b, HG_HEADS, HG_DK, HG_DV), jnp.float32)
        s_ctx, oc = hgrn_scan(flip(qc), flip(to_heads(k_c, HG_HEADS)), flip(ic),
                              flip(to_heads(logf_c, HG_HEADS)), s0, need_ctx)
        _, ol = hgrn_scan(flip(ql), flip(to_heads(k_l, HG_HEADS)), flip(il),
                          flip(to_heads(logf_l, HG_HEADS)), s_ctx, True)
        o_lat = o_lat + flip(ol)
        if need_ctx:
            o_ctx = o_ctx + flip(oc)
    gain = hg_g.reshape(HG_HEADS, 1, HG_DV)
    out_l = from_heads(rms_norm_2(o_lat, gain)).astype(q_l.dtype)
    out_c = from_heads(rms_norm_2(o_ctx, gain)).astype(q_l.dtype) if need_ctx else None
    return out_l, out_c

def fourier_mix(u):
    b, t, _ = u.shape
    uf = u.astype(jnp.float32).reshape(b, t, FN_GROUPS, FN_DIM)
    y = jnp.fft.fft2(uf, axes=(1, 3), norm="ortho").real
    return y.reshape(b, t, BRANCH).astype(u.dtype)

def mix_stream(parts, conv_w):
    cb, cc, cv, cz, _, _, _, az, _, _, _, _, hz, fu, fz = parts
    y_conv = cb * short_conv(cc * cv, conv_w) * jax.nn.silu(cz)
    y_four = fourier_mix(fu) * jax.nn.silu(fz)
    return y_conv, y_four, jax.nn.silu(az), jax.nn.silu(hz)

def hybrid_layer(h, hc, c_act, cc_act, norm_g, w_mod, b_mod, w_in, conv_w, q_g, k_g, lb, hg_g,
                 w_out, cos, sin, need_ctx):
    shift, scale, gate = jnp.split((c_act @ w_mod + b_mod)[:, None, :], 3, axis=-1)
    shift_c, scale_c, gate_c = jnp.split(cc_act @ w_mod + b_mod, 3, axis=-1)
    lat = split_cols((rms_norm_2(h, norm_g) * (1.0 + scale) + shift) @ w_in)
    cx = split_cols((rms_norm_2(hc, norm_g) * (1.0 + scale_c) + shift_c) @ w_in)

    att_l, att_c = gqa_branch(lat[4], lat[5], lat[6], cx[4], cx[5], cx[6], q_g, k_g, cos, sin, need_ctx)
    hg_l, hg_c = hgrn_branch(lat[8], lat[9], lat[10], lat[11], cx[8], cx[9], cx[10], cx[11],
                             lb, hg_g, need_ctx)

    y_conv, y_four, g_att, g_hg = mix_stream(lat, conv_w)
    y = jnp.concatenate([y_conv, att_l * g_att, hg_l * g_hg, y_four], axis=-1) @ w_out
    h_new = h + gate * y
    hc_new = None
    if need_ctx:
        yc_conv, yc_four, gc_att, gc_hg = mix_stream(cx, conv_w)
        yc = jnp.concatenate([yc_conv, att_c * gc_att, hg_c * gc_hg, yc_four], axis=-1) @ w_out
        hc_new = hc + gate_c * yc
    return h_new, hc_new

def second_inputs(seed: int = 0) -> dict:
    key = jax.random.key(seed)
    ks = jax.random.split(key, 16)
    f32 = jnp.float32
    nrm = lambda k, shape: jax.random.normal(k, shape, f32)
    return {
        "x": nrm(ks[0], (BATCH, SEQ, D_MODEL)),
        "c": nrm(ks[1], (BATCH, D_MODEL)),
        "ctx": nrm(ks[2], (BATCH, CTX_LEN, D_MODEL)),
        "c_ctx": nrm(ks[3], (D_MODEL,)),
        "norm_g": 1.0 + 0.1 * nrm(ks[4], (DEPTH_2, D_MODEL)),
        "w_mod": nrm(ks[5], (DEPTH_2, D_MODEL, 3 * D_MODEL)) * (0.5 * D_MODEL ** -0.5),
        "b_mod": 0.02 * nrm(ks[6], (DEPTH_2, 3 * D_MODEL)),
        "w_in": nrm(ks[7], (DEPTH_2, D_MODEL, IN_COLS)) * (D_MODEL ** -0.5),
        "conv_w": nrm(ks[8], (DEPTH_2, CONV_K, BRANCH)) * (CONV_K ** -0.5),
        "q_norm_g": 1.0 + 0.1 * nrm(ks[9], (DEPTH_2, HEAD_DIM)),
        "k_norm_g": 1.0 + 0.1 * nrm(ks[10], (DEPTH_2, HEAD_DIM)),
        "hgrn_lb": nrm(ks[11], (2, DEPTH_2, BRANCH)),
        "hgrn_norm_g": 1.0 + 0.1 * nrm(ks[12], (DEPTH_2, BRANCH)),
        "w_out": nrm(ks[13], (DEPTH_2, MIX_WIDTH, D_MODEL)) * (MIX_WIDTH ** -0.5),
        "final_g": 1.0 + 0.1 * nrm(ks[14], (D_MODEL,)),
    }

def second_block(x, c, ctx, c_ctx, norm_g, w_mod, b_mod, w_in, conv_w, q_norm_g, k_norm_g,
              hgrn_lb, hgrn_norm_g, w_out, final_g):
    rows = x.shape[1] // GRID_W
    cos, sin = axial_rope_tables(rows, x.dtype)
    lb_all = hgrn_lower_bounds(hgrn_lb)
    c_act = jax.nn.silu(c)
    cc_act = jax.nn.silu(c_ctx)
    h, hc = x, ctx
    for layer in range(DEPTH_2):
        h, hc = hybrid_layer(h, hc, c_act, cc_act, norm_g[layer], w_mod[layer], b_mod[layer],
                             w_in[layer], conv_w[layer], q_norm_g[layer], k_norm_g[layer],
                             lb_all[:, layer], hgrn_norm_g[layer], w_out[layer], cos, sin,
                             need_ctx=layer < DEPTH_2 - 1)
    return rms_norm_2(h, final_g)


def setup_inputs(seed=0):
    out = dict(first_inputs(seed))
    for name, value in second_inputs(seed + 1).items():
        if name != "x":
            out[name + "_2"] = value
    return out


def reference(
    x, c, positions, w_ada, b_ada, norm_pre, norm_post, w_in, conv_w, conv_b, w_rg_a, b_rg_a,
    w_rg_x, b_rg_x, lru_lambda, norm_rec, norm_att, w_out, c_2, ctx_2, c_ctx_2, norm_g_2,
    w_mod_2, b_mod_2, w_in_2, conv_w_2, q_norm_g_2, k_norm_g_2, hgrn_lb_2, hgrn_norm_g_2,
    w_out_2, final_g_2,
):
    x = first_block(
        x, c, positions, w_ada, b_ada, norm_pre, norm_post, w_in, conv_w, conv_b, w_rg_a,
        b_rg_a, w_rg_x, b_rg_x, lru_lambda, norm_rec, norm_att, w_out,
    )
    return second_block(
        x, c_2, ctx_2, c_ctx_2, norm_g_2, w_mod_2, b_mod_2, w_in_2, conv_w_2, q_norm_g_2,
        k_norm_g_2, hgrn_lb_2, hgrn_norm_g_2, w_out_2, final_g_2,
    )


_drawn_inputs = setup_inputs


def setup_inputs(seed=0):
    import zlib

    import numpy as np

    out = dict(_drawn_inputs(seed))
    spreads = {}
    factors = {'conv_b': 3.954,
     'b_rg_a': 30.417,
     'b_rg_x': 8.0,
     'ctx_2': 8.0,
     'c_ctx_2': 8.0,
     'b_mod_2': 2.754,
     'q_norm_g_2': 8.0,
     'k_norm_g_2': 8.0,
     'hgrn_lb_2': 6.21,
     'hgrn_norm_g_2': 4.027}
    for name, (base, spread) in spreads.items():
        noise = np.random.default_rng([zlib.crc32(name.encode()), seed]).standard_normal(out[name].shape)
        drawn = base * np.exp(spread * noise) if base else spread * noise
        out[name] = __import__('jax').numpy.asarray(drawn.astype(out[name].dtype))
    for name, factor in factors.items():
        out[name] = (out[name] * factor).astype(out[name].dtype)
    return out
```

```python
from contextlib import ExitStack, contextmanager

import numpy as np
import concourse.bass as bass
from concourse import mybir

F32 = mybir.dt.float32
I32 = mybir.dt.int32
ALU = mybir.AluOpType
ACT = mybir.ActivationFunctionType
AXX = mybir.AxisListType.X

P = 128
D = 1024
S = 2048
KT = D // P
NT = S // P
CH = 512
GC = 256
EPS = 1e-6
BIG = 1e30
DREC = 512
CT = DREC // P
H1 = 8
HD = 64
PATTERNS = ((128, 1), (512, 4), (2048, 16))
RW = H1 * HD + 2 * H1


class Sem:

    def __init__(self, handle):
        self.h, self.base = handle, 0

    def at(self, n):
        return self.base + n


class Env:

    def __init__(self, nc, A):
        self.nc, self.A = nc, A
        self.sems = {}
        self.stack = ExitStack()
        self.groups = []
        self.loaded = 0
        self.n_names = 0
        self.free = []
        self.made = 0

    def sem(self, name):
        if name not in self.sems:
            if self.free:
                self.sems[name] = self.free.pop()
            else:
                self.made += 1
                self.sems[name] = Sem(self.stack.enter_context(self.nc.semaphore(f"{name}_{self.made}")))
        return self.sems[name]

    def retire(self, *names):
        self.free += [self.sems.pop(n) for n in names]

    def sb(self, ctx, name, shape, dt=F32):
        self.n_names += 1
        return ctx.enter_context(self.nc.sbuf_tensor(f"{name}_{self.n_names}", shape, dt))

    def banks(self, ctx, name, n):
        self.n_names += 1
        return [ctx.enter_context(self.nc.psum_tensor(f"{name}{i}_{self.n_names}", [P, CH], F32)) for i in range(n)]

    def load_groups(self, eng, upto):
        for g in range(self.loaded, min(upto, len(self.groups))):
            if g >= 2:
                eng.wait_ge(self.sem("w_used").h, g - 1)
            ap, c0 = self.groups[g]
            eng.dma_start(self.wring[:, g % 2, :, :],
                          ap[:, c0:c0 + GC].rearrange("(k p) c -> p k c", p=P)).then_inc(self.sem(f"w_loaded{g % 2}").h, 16)
        self.loaded = max(self.loaded, min(upto, len(self.groups)))

    def group_here(self, eng, g):
        eng.wait_ge(self.sem(f"w_loaded{g % 2}").h, 16 * (g // 2 + 1))
        return self.wring[:, g % 2, :, :]


class Link:

    def __init__(self, eng, sem):
        self.eng, self.sem, self.n = eng, sem, 0

    def __call__(self, ins):
        self.n += 1
        ins.then_inc(self.sem.h, 1)
        self.eng.wait_ge(self.sem.h, self.sem.at(self.n))

    def close(self):
        self.sem.base += self.n


def stage_vectors(env):
    nc, A = env.nc, env.A
    rows = [
        ("c", A["c"], 8), ("c_2", A["c_2"], 8), ("c_ctx_2", A["c_ctx_2"], 8), ("norm_pre", A["norm_pre"], 8),
        ("norm_g_2", A["norm_g_2"], 16), ("conv_b", A["conv_b"], 4), ("b_rg_a", A["b_rg_a"], 4), ("b_rg_x", A["b_rg_x"], 4),
        ("lru_lambda", A["lru_lambda"], 4), ("conv_w", A["conv_w"], 16), ("norm_rec", A["norm_rec"], 4),
        ("norm_att", A["norm_att"], 4), ("b_ada", A["b_ada"], 24),
        ("b_mod_2", A["b_mod_2"], 48), ("conv_w_2", A["conv_w_2"], 12), ("hgrn_lb_2", A["hgrn_lb_2"], 8),
        ("hgrn_norm_g_2", A["hgrn_norm_g_2"], 4),
    ]
    place, tile, at = {}, 0, 0
    for name, _, n in rows:
        if at + n > P:
            tile, at = tile + 1, 0
        place[name] = (tile, at)
        at += n
    used = [max((p[1] + n) for (name, _, n), p in ((r, place[r[0]]) for r in rows) if p[0] == t) for t in range(tile + 1)]
    env.place = place
    nt = tile + 1
    assert nt == 2

    ld, tr, ev = env.sem("vec_loaded"), env.sem("vec_turned"), env.sem("vec_copied")
    with ExitStack() as ctx:
        vr = env.sb(ctx, "vrows", [P, nt, P])
        posi = env.sb(ctx, "pos_int", [NT, P], I32)
        posf = env.sb(ctx, "pos_rows", [NT, P])
        ang = env.sb(ctx, "angle", [P, NT, 32])
        nn = env.sb(ctx, "turns", [P, NT, 32])
        t1 = env.sb(ctx, "rest", [P, NT, 32])
        pc = env.sb(ctx, "pos_cols", [P, NT])
        levm = env.sb(ctx, "level_masks_in", [P, 16, P])
        ps, ps2 = env.banks(ctx, "ps_vec", 2)
        block = ctx.enter_context(nc.Block())
        consts = [(env.ident, A["k_ident"]), (env.mask1, A["k_mask1"]), (env.invf, A["k_invf"].to_broadcast([P, 32])),
                  (levm, A["k_levmask"]), (env.headmean, A["k_headmean"])]

        @block.sync
        def _(sp):
            for name, ap, n in rows:
                t, r = place[name]
                names = "abcd"[:len(ap.shape)]
                flat = ap if len(ap.shape) == 1 else ap.rearrange(f"{' '.join(names)} -> ({' '.join(names)})")
                sp.dma_start(vr[r:r + n, t, :], flat.rearrange("(r c) -> r c", c=P)).then_inc(ld.h, 16)
            sp.dma_start(posi[:, :], A["positions"].rearrange("a (t p) -> (a t) p", p=P)).then_inc(ld.h, 16)
            for dst, src in consts:
                sp.dma_start(dst[(slice(None),) * len(dst.shape)], src).then_inc(ld.h, 16)
            env.load_groups(sp, 2)

        n_ld = 16 * (len(rows) + 1 + len(consts))

        @block.tensor
        def _(pe):
            pe.wait_ge(ld.h, n_ld)
            for t in range(nt):
                mm = pe.transpose(ps[:, t * P:t * P + used[t]], vr[0:used[t], t, :], env.ident[0:used[t], 0:used[t]])
            mm.then_inc(tr.h, 1)
            pe.wait_ge(env.sem("pos_float").h, 1)
            pe.transpose(ps2[:, 0:NT], posf[:, :], env.ident[0:NT, 0:NT]).then_inc(tr.h, 1)

        @block.vector
        def _(dve):
            link = Link(dve, env.sem("dve_chain"))
            dve.memset(env.mhalf[:, :], -0.5)
            dve.memset(env.ones[:, :], 1.0).then_inc(env.sem("ones_set").h, 1)
            dve.wait_ge(ld.h, n_ld)
            dve.tensor_copy(env.levmask[:, :, :], levm[:, :, :])
            dve.tensor_copy(posf[:, :], posi[:, :]).then_inc(env.sem("pos_float").h, 1)
            dve.wait_ge(tr.h, 1)
            for t in range(nt):
                ins = dve.tensor_copy(env.vcols[:, t, 0:used[t]], ps[:, t * P:t * P + used[t]])
            ins.then_inc(ev.h, 1)
            dve.memset(env.eps[:, :], EPS)
            dve.wait_ge(ev.h, 1)
            lbc = env.cols("hgrn_lb_2", 8).rearrange("p (d l m) -> p d l m", d=2, l=2)
            dve.tensor_tensor(env.lb[:, 2, :, :], lbc[:, :, 1, :], lbc[:, :, 0, :], ALU.subtract).then_inc(env.sem("lb_diff").h, 1)
            dve.wait_ge(tr.h, 2)
            link(dve.tensor_copy(pc[:, :], ps2[:, 0:NT]))
            link(dve.tensor_tensor(ang[:, :, :], pc[:, :, None].to_broadcast([P, NT, 32]),
                                   env.invf[:, None, :].to_broadcast([P, NT, 32]), ALU.mult))
            link(dve.tensor_scalar(nn[:, :, :], ang[:, :, :], 1.0 / (2 * np.pi), MAGIC, ALU.mult, ALU.add))
            link(dve.tensor_scalar(nn[:, :, :], nn[:, :, :], -MAGIC, None, ALU.add))
            for part in TWO_PI_PARTS:
                link(dve.scalar_tensor_tensor(out=ang[:, :, :], in0=nn[:, :, :], scalar=-part, in1=ang[:, :, :],
                                              op0=ALU.mult, op1=ALU.add))
            link(dve.tensor_scalar(ang[:, :, :], ang[:, :, :], PI_F, -PI_F, ALU.min, ALU.max))
            link(dve.tensor_scalar(t1[:, :, :], ang[:, :, :], -1.0, None, ALU.mult))
            link(dve.tensor_tensor(t1[:, :, :], t1[:, :, :], ang[:, :, :], ALU.max))
            dve.tensor_scalar(t1[:, :, :], t1[:, :, :], -1.0, PI_F / 2, ALU.mult, ALU.add).then_inc(env.sem("angle_ready").h, 1)
            dve.wait_ge(env.sem("sines").h, 2)
            for half in range(2):
                dve.tensor_copy(env.cosF[:, :, half, :], t1[:, :, :])
            link(dve.tensor_scalar(env.sinF[:, :, 0, :], ang[:, :, :], -1.0, None, ALU.mult))
            link(dve.tensor_copy(env.sinF[:, :, 1, :], ang[:, :, :]))
            dve.wait_ge(env.sem("lam_exp").h, 1)
            e, z, z2, acc = env.sp[:, 0, :], env.sp[:, 1, :], env.sp[:, 2, :], env.sp[:, 3, :]
            lam = env.cols("lru_lambda", 4)
            link(dve.tensor_scalar(z, e, 2.0, None, ALU.add))
            link(dve.reciprocal(z, z))
            link(dve.tensor_tensor(z, z, e, ALU.mult))
            link(dve.tensor_tensor(z2, z, z, ALU.mult))
            link(dve.memset(acc, 1.0 / 21))
            for n in range(19, 0, -2):
                link(dve.tensor_tensor(acc, acc, z2, ALU.mult))
                link(dve.tensor_scalar(acc, acc, 1.0 / n, None, ALU.add))
            link(dve.tensor_tensor(acc, acc, z, ALU.mult))
            link(dve.tensor_scalar(z, lam, -1.0, 0.0, ALU.mult, ALU.max))
            link(dve.scalar_tensor_tensor(out=acc, in0=acc, scalar=2.0, in1=z, op0=ALU.mult, op1=ALU.add))
            link(dve.tensor_scalar(env.nsp[:, :], acc, -8.0, None, ALU.mult))
            link.close()

        @block.scalar
        def _(act):
            act.wait_ge(ev.h, 1)
            act.activation(env.csilu[:, :], env.vcols[:, place["c"][0], 0:24], ACT.Silu).then_inc(env.sem("csilu").h, 1)
            lam = env.cols("lru_lambda", 4)
            act.activation(env.sp[:, 4, :], lam, ACT.Abs).then_inc(env.sem("act_chain").h, 1)
            act.wait_ge(env.sem("act_chain").h, 1)
            act.activation(env.sp[:, 0, :], env.sp[:, 4, :], ACT.Exp, scale=-1.0).then_inc(env.sem("lam_exp").h, 1)
            act.wait_ge(env.sem("lb_diff").h, 1)
            act.activation(env.lb[:, 0, :, :], env.lb[:, 2, :, :], ACT.Sigmoid).then_inc(env.sem("lb_done").h, 1)
            act.activation(env.lb[:, 1, :, :], env.lb[:, 2, :, :], ACT.Sigmoid, scale=-1.0).then_inc(env.sem("lb_done").h, 1)
            act.wait_ge(env.sem("angle_ready").h, 1)
            act.activation(t1[:, :, :], t1[:, :, :], ACT.Sin).then_inc(env.sem("sines").h, 1)
            act.activation(ang[:, :, :], ang[:, :, :], ACT.Sin).then_inc(env.sem("sines").h, 1)
        env.sem("act_chain").base += 1


MAGIC = 12582912.0
PI_F = 3.1415925
TWO_PI_PARTS = (6.28125, float(np.float32(0.0019350051879882812)), float(2 * np.pi - 6.28125 - 0.0019350051879882812))


def stage_mod(env, tag, w_ap, bias, gkey, goff, vecs, gates, gate_mul):
    nc = env.nc
    g0 = env.next_group
    ng = 3 * D // GC
    nv = len(vecs)
    pd, ct = env.sem("mod_ready"), env.sem("mod_done")
    bt, boff = env.place[bias[0]][0], env.place[bias[0]][1] + bias[1]
    with ExitStack() as ctx:
        pcol = env.banks(ctx, "ps_mod", 1)[0]
        pg = env.banks(ctx, "ps_gate", 2 * nv)
        brow = env.sb(ctx, "gate_bias", [P, 2, D])
        tmp = env.sb(ctx, "mod_tmp", [P, 16, nv])
        block = ctx.enter_context(nc.Block())

        @block.sync
        def _(sp):
            env.load_groups(sp, g0 + ng + 2)

        @block.scalar
        def _(act):
            act.dma_start(brow[:, 0, :], bias[2].to_broadcast([P, D])).then_inc(env.sem("gate_row").h, 16)
            src = gate_mul if gate_mul is not None else bias[2]
            act.dma_start(brow[:, 1, :], src.to_broadcast([P, D])).then_inc(env.sem("gate_row").h, 16)

        @block.tensor
        def _(pe):
            pe.wait_ge(env.sem("csilu").h, 1)
            for g in range(ng):
                w = env.group_here(pe, g0 + g)
                if g < 8:
                    for m in range(2):
                        for k in range(KT):
                            mm = pe.matmul(pcol[:, (2 * g + m) * nv:(2 * g + m + 1) * nv], w[:, k, m * P:(m + 1) * P],
                                           env.csilu[:, vecs[0] * 8 + k:vecs[-1] * 8 + k + 1:8], start=(k == 0), stop=(k == KT - 1))
                else:
                    for v in range(nv):
                        for k in range(KT):
                            col = vecs[v] * 8 + k
                            mm = pe.matmul(pg[2 * v + (g - 8) // 2][:, (g % 2) * GC:(g % 2 + 1) * GC],
                                           env.csilu[:, col:col + 1].to_broadcast([P, P]), w[:, k, :],
                                           start=(k == 0), stop=(k == KT - 1))
                mm.then_inc(env.sem("w_used").h, 1)

        @block.vector
        def _(dve):
            link = Link(dve, env.sem("dve_chain"))
            dve.wait_ge(env.sem("vec_copied").h, 1)
            dve.wait_ge(env.sem("w_used").h, g0 + ng)
            dve.wait_ge(env.sem("gate_row").h, env.sem("gate_row").at(32))
            link(dve.tensor_tensor(tmp[:, :, :], pcol[:, 0:16 * nv].rearrange("p (a b) -> p a b", b=nv),
                                   env.vcols[:, bt, boff:boff + 16, None].to_broadcast([P, 16, nv]), ALU.add))
            gt, go = env.place[gkey]
            gain = env.vcols[:, gt, go + goff:go + goff + 8]
            for v in range(nv):
                link(dve.tensor_copy(env.mods[tag][:, v, 1, :], tmp[:, 0:8, v]))
                link(dve.scalar_tensor_tensor(out=env.mods[tag][:, v, 0, :], in0=tmp[:, 8:16, v], scalar=1.0,
                                              in1=gain, op0=ALU.add, op1=ALU.mult))
                for h in range(2):
                    sl = slice(h * CH, (h + 1) * CH)
                    link(dve.tensor_tensor(gates[v][:, sl], pg[2 * v + h][:, :], brow[:, 0, sl], ALU.add))
                    if gate_mul is not None:
                        link(dve.tensor_tensor(gates[v][:, sl], gates[v][:, sl], brow[:, 1, sl], ALU.mult))
            link.close()
    env.sem("gate_row").base += 32
    env.next_group += ng


def stage_norm(env, hT, pieces):
    nc = env.nc
    tiles, groups = [], []
    for src, n, col0, mod in pieces:
        for q in range(0, n, 4):
            m = min(4, n - q)
            groups.append((len(tiles), m, col0 + q * P, mod))
            tiles += [(src, q + j) for j in range(m)]
    RX = 8
    xl = [env.sem(f"x_loaded{i}") for i in range(RX)]
    sq, ms, rs, xn, tb = env.sem("x_squared"), env.sem("x_mean"), env.sem("x_rstd"), env.sem("x_normed"), env.sem("x_turned")
    ev = [env.sem("turn_copied_act"), env.sem("turn_copied_dve")]
    last_of = {g0 + m - 1: gi for gi, (g0, m, _, _) in enumerate(groups)}
    group_of = [gi for gi, (_, m, _, _) in enumerate(groups) for _ in range(m)]
    with ExitStack() as ctx:
        x = env.sb(ctx, "x_rows", [P, RX, D])
        junk = env.sb(ctx, "x_junk", [P, 2, D])
        st = env.sb(ctx, "x_stat", [P, 3, len(tiles)])
        ps = [env.banks(ctx, "ps_turn_a", 2), env.banks(ctx, "ps_turn_d", 2)]
        block = ctx.enter_context(nc.Block())

        @block.sync
        def _(sp):
            for i, (src, t) in enumerate(tiles):
                if i >= RX:
                    sp.wait_ge(tb.h, tb.at(8 * group_of[i - RX] + 8))
                sp.dma_start(x[:, i % RX, :], src[t * P:(t + 1) * P, :]).then_inc(xl[i % RX].h, 16)

        @block.scalar
        def _(act):
            def evac(gi):
                g0, m, col, mod = groups[gi]
                for j in range(4):
                    k = 2 * j
                    act.wait_ge(tb.h, tb.at(8 * gi + k + 1))
                    act.activation(hT[:, k, col:col + m * P], ps[0][j % 2][:, 0:m * P], ACT.Identity,
                                   bias=mod[1][:, k:k + 1], scale=mod[0][:, k:k + 1]).then_inc(ev[0].h, 1)
            for i in range(len(tiles)):
                act.wait_ge(xl[i % RX].h, xl[i % RX].at(16 * (i // RX + 1)))
                if i >= 2:
                    act.wait_ge(sq.h, sq.at(i - 1))
                act.activation(junk[:, i % 2, :], x[:, i % RX, :], ACT.Square, accum_out=st[:, 0, i:i + 1]).then_inc(sq.h, 1)
                if i in last_of and last_of[i] >= 1:
                    evac(last_of[i] - 1)
            evac(len(groups) - 1)

        @block.gpsimd
        def _(pool):
            for i in range(len(tiles)):
                pool.wait_ge(ms.h, ms.at(i + 1))
                pool.tensor_tensor(st[:, 2, i:i + 1], st[:, 1, i:i + 1], env.mhalf[:, :], ALU.pow).then_inc(rs.h, 1)

        @block.vector
        def _(dve):
            def evac(gi):
                g0, m, col, mod = groups[gi]
                for j in range(4):
                    k = 2 * j + 1
                    dve.wait_ge(tb.h, tb.at(8 * gi + k + 1))
                    dve.tensor_scalar(hT[:, k, col:col + m * P], ps[1][j % 2][:, 0:m * P], mod[0][:, k:k + 1],
                                      mod[1][:, k:k + 1], ALU.mult, ALU.add).then_inc(ev[1].h, 1)
            def mean(i):
                dve.wait_ge(sq.h, sq.at(i + 1))
                dve.tensor_scalar(st[:, 1, i:i + 1], st[:, 0, i:i + 1], 1.0 / D, EPS, ALU.mult, ALU.add).then_inc(ms.h, 1)

            mean(0)
            for i in range(len(tiles)):
                if i not in last_of:
                    mean(i + 1)
                dve.wait_ge(rs.h, rs.at(i + 1))
                dve.tensor_scalar(x[:, i % RX, :], x[:, i % RX, :], st[:, 2, i:i + 1], None, ALU.mult).then_inc(xn.h, 1)
                if i in last_of:
                    if last_of[i] >= 1:
                        evac(last_of[i] - 1)
                    if i + 1 < len(tiles):
                        mean(i + 1)
            evac(len(groups) - 1)

        @block.tensor
        def _(pe):
            for gi, (g0, m, col, mod) in enumerate(groups):
                pe.wait_ge(xn.h, xn.at(g0 + m))
                for k in range(KT):
                    n = 4 * gi + k // 2
                    if n >= 2:
                        pe.wait_ge(ev[k % 2].h, ev[k % 2].at(n - 1))
                    for j in range(m):
                        mm = pe.transpose(ps[k % 2][n % 2][:, j * P:(j + 1) * P],
                                          x[:, (g0 + j) % RX, k * P:(k + 1) * P], env.ident[:, :])
                    mm.then_inc(tb.h, 1)
    n, g = len(tiles), len(groups)
    for i in range(RX):
        xl[i].base += 16 * len(range(i, n, RX))
    for s_, c_ in ((sq, n), (ms, n), (rs, n), (xn, n), (tb, 8 * g), (ev[0], 4 * g), (ev[1], 4 * g)):
        s_.base += c_


def stage_recurrent(env, hT, yaT, sumsq):
    nc, A = env.nc, env.A
    g0 = env.next_group
    NCH = S // CH
    xe, ge, cv, gm, sg = env.sem("xa_out"), env.sem("ga_out"), env.sem("conv_done"), env.sem("gate_mm"), env.sem("gate_act")
    pm_x, pm_g = env.sem("xa_mm"), env.sem("ga_mm")
    ab, sd, rt, ix, yd, y2, ss = (env.sem(n) for n in ("decay_done", "decay_sq", "root_done", "gated_in", "ya_done",
                                                       "ya_squared", "ya_summed"))
    with ExitStack() as ctx:
        xp = env.sb(ctx, "xa_padded", [P, 3 + S])
        xc = env.sb(ctx, "xa_conv", [P, S])
        gs = env.sb(ctx, "ga_silu", [P, 2, S])
        rr = env.sb(ctx, "gate_r", [P, S])
        ii = env.sb(ctx, "gate_i", [P, S])
        aa = env.sb(ctx, "decay", [P, S])
        tt = env.sb(ctx, "decay_tanh", [P, S])
        mm_ = env.sb(ctx, "multiplier", [P, S])
        wg = env.sb(ctx, "w_gates", [P, 2, CT, P])
        psx = env.banks(ctx, "ps_xa", 2)
        psg = env.banks(ctx, "ps_ga", 2)
        psr = env.banks(ctx, "ps_gates", 2)
        pss = env.banks(ctx, "ps_ss", 1)[0]
        block = ctx.enter_context(nc.Block())

        @block.sync
        def _(sp):
            sp.wait_ge(env.sem("wg_zero").h, 1)
            for g, name in enumerate(("w_rg_a", "w_rg_x")):
                for b in range(8):
                    r = HD * (b % 2)
                    sp.dma_start(wg[r:r + HD, g, b // 2, r:r + HD], A[name][0, b, :, :]).then_inc(env.sem("wg_loaded").h, 16)
            env.load_groups(sp, g0 + 6)

        @block.tensor
        def _(pe):
            def project(g, m, ps, n0, done, copied):
                w = env.group_here(pe, g)
                for q in range(NCH):
                    n = n0 + q
                    if n >= 2:
                        pe.wait_ge(copied.h, copied.at(n - 1))
                    for k in range(KT):
                        mm = pe.matmul(ps[n % 2][:, :], w[:, k, m * P:(m + 1) * P], hT[:, k, q * CH:(q + 1) * CH],
                                       start=(k == 0), stop=(k == KT - 1))
                    mm.then_inc(done.h, 1)

            def gates(c):
                pe.wait_ge(cv.h, cv.at(c + 1))
                for g in range(2):
                    for q in range(NCH):
                        n = (2 * c + g) * NCH + q
                        if n >= 2:
                            pe.wait_ge(sg.h, sg.at(n - 1))
                        pe.matmul(psr[n % 2][:, :], wg[:, g, c, :], xc[:, q * CH:(q + 1) * CH],
                                  start=True, stop=True).then_inc(gm.h, 1)

            def squares(c):
                pe.wait_ge(y2.h, y2.at(c + 1))
                for t in range(NT):
                    mm = pe.matmul(pss[:, c * NT + t:c * NT + t + 1], rr[:, t * P:(t + 1) * P], env.ones[:, 0:1],
                                   start=True, stop=True)
                mm.then_inc(ss.h, 1)

            pe.wait_ge(env.sem("wg_loaded").h, 16 * 16)
            for c in range(CT):
                project(g0 + 2 * (c // 2), c % 2, psx, c * NCH, pm_x, xe)
                project(g0 + 2 * (c // 2) + 1, c % 2, psg, c * NCH, pm_g, ge)
                if c % 2:
                    pe.wait_ge(pm_g.h, pm_g.at((c + 1) * NCH))
                    pe.sem_inc(env.sem("w_used").h, 2)
                if c >= 1:
                    squares(c - 1)
                gates(c)
            squares(CT - 1)

        @block.scalar
        def _(act):
            chain = Link(act, env.sem("act_chain"))
            for c in range(CT):
                if c >= 1:
                    act.wait_ge(cv.h, cv.at(c))
                for q in range(NCH):
                    n = c * NCH + q
                    act.wait_ge(pm_x.h, pm_x.at(n + 1))
                    act.activation(xp[:, 3 + q * CH:3 + (q + 1) * CH], psx[n % 2][:, :], ACT.Copy).then_inc(xe.h, 1)
                for q in range(NCH):
                    n = c * NCH + q
                    act.wait_ge(pm_g.h, pm_g.at(n + 1))
                    act.activation(gs[:, c % 2, q * CH:(q + 1) * CH], psg[n % 2][:, :], ACT.Silu).then_inc(ge.h, 1)
                if c >= 1:
                    act.wait_ge(ss.h, ss.at(c))
                for g, (dst, key) in enumerate(((rr, "b_rg_a"), (ii, "b_rg_x"))):
                    for q in range(NCH):
                        n = (2 * c + g) * NCH + q
                        act.wait_ge(gm.h, gm.at(n + 1))
                        act.activation(dst[:, q * CH:(q + 1) * CH], psr[n % 2][:, :], ACT.Sigmoid,
                                       bias=env.cols(key, 4)[:, c:c + 1]).then_inc(sg.h, 1)
                act.wait_ge(sg.h, sg.at((2 * c + 2) * NCH))
                act.activation(aa[:, :], rr[:, :], ACT.Exp, scale=env.nsp[:, c:c + 1]).then_inc(ab.h, 1)
                act.activation(tt[:, :], rr[:, :], ACT.Tanh, scale=env.nsp[:, c:c + 1]).then_inc(ab.h, 1)
                act.wait_ge(sd.h, sd.at(c + 1))
                act.activation(tt[:, :], mm_[:, :], ACT.Sqrt, scale=-1.0).then_inc(rt.h, 1)
                act.wait_ge(yd.h, yd.at(c + 1))
                act.activation(rr[:, :], yaT[:, c, :], ACT.Square).then_inc(y2.h, 1)
            chain.close()

        @block.gpsimd
        def _(pool):
            pool.memset(wg[:, :, :, :], 0.0).then_inc(env.sem("wg_zero").h, 1)
            for c in range(CT):
                pool.wait_ge(sg.h, sg.at((2 * c + 2) * NCH))
                pool.wait_ge(cv.h, cv.at(c + 1))
                pool.tensor_tensor(ii[:, :], ii[:, :], xc[:, :], ALU.mult).then_inc(ix.h, 1)

        @block.vector
        def _(dve):
            link = Link(dve, env.sem("dve_chain"))
            link(dve.memset(xp[:, 0:3], 0.0))
            cw, cb = env.cols("conv_w", 16), env.cols("conv_b", 4)
            for c in range(CT):
                dve.wait_ge(xe.h, xe.at((c + 1) * NCH))
                o = xc[:, :]
                link(dve.tensor_scalar(o, xp[:, 0:S], cw[:, c:c + 1], cb[:, c:c + 1], ALU.mult, ALU.add))
                for j in range(1, 4):
                    ins = dve.scalar_tensor_tensor(out=o, in0=xp[:, j:j + S], scalar=cw[:, 4 * j + c:4 * j + c + 1], in1=o,
                                                   op0=ALU.mult, op1=ALU.add)
                    if j < 3:
                        link(ins)
                ins.then_inc(cv.h, 1)
                dve.wait_ge(ab.h, ab.at(2 * c + 2))
                link(dve.tensor_tensor(mm_[:, :], aa[:, :], aa[:, :], ALU.mult))
                dve.scalar_tensor_tensor(out=mm_[:, :], in0=mm_[:, :], scalar=1.0, in1=tt[:, :],
                                         op0=ALU.add, op1=ALU.mult).then_inc(sd.h, 1)
                dve.wait_ge(rt.h, rt.at(c + 1))
                dve.wait_ge(ix.h, ix.at(c + 1))
                link(dve.tensor_tensor(ii[:, :], ii[:, :], tt[:, :], ALU.mult))
                link(dve.tensor_tensor_scan(mm_[:, :], aa[:, :], ii[:, :], 0.0, ALU.mult, ALU.add))
                dve.wait_ge(ge.h, ge.at((c + 1) * NCH))
                dve.tensor_tensor(yaT[:, c, :], mm_[:, :], gs[:, c % 2, :], ALU.mult).then_inc(yd.h, 1)
            dve.wait_ge(ss.h, ss.at(CT))
            dve.tensor_reduce(sumsq[:, :], pss[:, 0:CT * NT].rearrange("p (c t) -> p t c", c=CT), AXX, ALU.add)
            link.close()
    for s_, c_ in ((xe, CT * NCH), (ge, CT * NCH), (pm_x, CT * NCH), (pm_g, CT * NCH), (cv, CT), (gm, 2 * CT * NCH),
                   (sg, 2 * CT * NCH), (ab, 2 * CT), (sd, CT), (rt, CT), (ix, CT), (yd, CT), (y2, CT), (ss, CT)):
        s_.base += c_
    env.next_group += 4


def stage_qkvg(env, hT, QT, KTt, v_d, gb_d):
    nc = env.nc
    g0 = env.next_group
    UN = 8 * NT
    mmd = env.sem("proj_mm")
    av, rd, st = env.sem("plain_out"), env.sem("rope_read"), env.sem("rope_sum")
    tq, tc = env.sem("qk_turned"), env.sem("qk_copied")
    NRO, NRN = 4, 4
    dv = [env.sem(f"plain_stored{i}") for i in range(NRO)]
    with ExitStack() as ctx:
        vb = env.sb(ctx, "plain_rows", [P, NRO, GC])
        ta = env.sb(ctx, "rope_a", [P, 2, GC])
        tb = env.sb(ctx, "rope_b", [P, 2, GC])
        nat = env.sb(ctx, "rope_rows", [P, NRN, GC])
        ps = env.banks(ctx, "ps_proj", 4)
        pt = env.banks(ctx, "ps_qk", 2)
        block = ctx.enter_context(nc.Block())

        @block.sync
        def _(sp):
            env.load_groups(sp, g0 + 8)
            for i in range(NRO):
                sp.wait_ge(dv[i].h, dv[i].at(16 * (4 * NT // NRO)))

        @block.tensor
        def _(pe):
            def turn(b):
                st_n = 4 * (b + 1)
                pe.wait_ge(st.h, st.at(st_n))
                for pr in range(2):
                    n = 2 * b + pr
                    if n >= 2:
                        pe.wait_ge(tc.h, tc.at(n - 1))
                    for j in range(4):
                        mm = pe.transpose(pt[n % 2][:, j * P:(j + 1) * P], nat[:, (4 * b + j) % NRN, pr * P:(pr + 1) * P],
                                          env.ident[:, :])
                    mm.then_inc(tq.h, 1)

            for u in range(UN):
                g, t = divmod(u, NT)
                w = env.group_here(pe, g0 + g)
                if u >= 4:
                    v = u - 4
                    if v < 4 * NT:
                        pe.wait_ge(av.h, av.at(v + 1))
                    else:
                        pe.wait_ge(rd.h, rd.at(v - 4 * NT + 1))
                for k in range(KT):
                    mm = pe.matmul(ps[u % 4][:, 0:GC], hT[:, k, t * P:(t + 1) * P], w[:, k, :],
                                   start=(k == 0), stop=(k == KT - 1))
                mm.then_inc(mmd.h, 1)
                if t == NT - 1:
                    pe.wait_ge(mmd.h, mmd.at(u + 1))
                    pe.sem_inc(env.sem("w_used").h, 1)
                r = u - 4 * NT
                if r >= 5 and r % 4 == 1:
                    turn(r // 4 - 1)
            turn(4 * NT // 4 - 1)

        @block.scalar
        def _(act):
            def copy_turned(b):
                for pr in range(2):
                    n = 2 * b + pr
                    g, q = divmod(b, NT // 4)
                    dst = (QT if g < 2 else KTt)[:, 2 * (g % 2) + pr, q * CH:(q + 1) * CH]
                    act.wait_ge(tq.h, tq.at(n + 1))
                    act.activation(dst, pt[n % 2][:, :], ACT.Copy, scale=-(HD ** -0.5) if g < 2 else 1.0).then_inc(tc.h, 1)

            def store(u):
                g, t = divmod(u, NT)
                dst = (v_d if g < 2 else gb_d)[t * P:(t + 1) * P, (g % 2) * GC:(g % 2 + 1) * GC]
                act.wait_ge(av.h, av.at(u + 1))
                act.dma_start(dst, vb[:, u % NRO, :]).then_inc(dv[u % NRO].h, 16)

            for u in range(4 * NT):
                act.wait_ge(mmd.h, mmd.at(u + 1))
                if u >= NRO:
                    act.wait_ge(dv[u % NRO].h, dv[u % NRO].at(16 * (u // NRO)))
                act.activation(vb[:, u % NRO, :], ps[u % 4][:, 0:GC], ACT.Copy if u < 2 * NT else ACT.Silu).then_inc(av.h, 1)
                if u >= 1:
                    store(u - 1)
            store(4 * NT - 1)
            for b in range(NT):
                copy_turned(b)

        @block.vector
        def _(dve):
            for r in range(4 * NT):
                t = r % NT
                src = ps[r % 4][:, 0:GC].rearrange("p (h a e) -> p h a e", a=2, e=HD // 2)
                a = ta[:, r % 2, :].rearrange("p (h a e) -> p h a e", a=2, e=HD // 2)
                b = tb[:, r % 2, :].rearrange("p (h a e) -> p h a e", a=2, e=HD // 2)
                shp = [P, 4, HD // 2]
                dve.wait_ge(mmd.h, mmd.at(4 * NT + r + 1))
                if r >= 2:
                    dve.wait_ge(st.h, st.at(r - 1))
                for h in range(2):
                    dve.tensor_tensor(a[:, :, h, :], src[:, :, h, :], env.cosF[:, t, h, None, :].to_broadcast(shp), ALU.mult)
                for h in range(2):
                    ins = dve.tensor_tensor(b[:, :, h, :], src[:, :, 1 - h, :],
                                            env.sinF[:, t, h, None, :].to_broadcast(shp), ALU.mult)
                ins.then_inc(rd.h, 1)

        @block.gpsimd
        def _(pool):
            for r in range(4 * NT):
                pool.wait_ge(rd.h, rd.at(r + 1))
                if r >= NRN:
                    pool.wait_ge(tq.h, tq.at(2 * ((r - NRN) // 4) + 2))
                pool.tensor_tensor(nat[:, r % NRN, :], ta[:, r % 2, :], tb[:, r % 2, :], ALU.add).then_inc(st.h, 1)
    for s_, c_ in ((mmd, UN), (av, 4 * NT), (rd, 4 * NT), (st, 4 * NT), (tq, 2 * NT), (tc, 2 * NT)):
        s_.base += c_
    for i in range(NRO):
        dv[i].base += 16 * (4 * NT // NRO)
    env.next_group += 8


def stage_dilated(env, vspace, QT, KTt, v_d, res_d):
    nc = env.nc
    plan = []
    for p, (window, dil) in enumerate(PATTERNS):
        nblk = S // dil // P
        for t in range(NT):
            n, r = (t, 0) if dil == 1 else ((t // dil, t % dil) if nblk > 1 else (0, t))
            q = (P * dil * n + r, dil)
            w = 1 if n == 0 else 2
            kc0 = P * dil * (n - w + 1) + r
            vt = [t] if w == 1 else [t - dil if dil > 1 else t - 1, t]
            for hh in range(2):
                plan.append((p, t, hh, q, (kc0, dil), w, vt))
    U = len(plan)
    smm, sm_, ex, tm, tc0, tc1, pvm, pvc = (env.sem(n) for n in (
        "score_mm", "score_min", "prob_exp", "prob_turned", "prob_copied_act", "prob_copied_dve", "pv_mm", "pv_copied"))
    vl = [env.sem("v_loaded0"), env.sem("v_loaded1")]
    rs = [env.sem("res_stored0"), env.sem("res_stored1")]
    with ExitStack() as ctx:
        V = vspace[:, :, :].rearrange("p (b x) s -> p b (x s)", b=2).rearrange("p b (t c) -> p b t c", c=H1 * HD)
        sc = env.sb(ctx, "scores", [P, 2, 4, 2 * P])
        pr = sc
        pT = env.wring[:, 0, :, :].rearrange("p (a x) c -> p a (x c)", a=2).rearrange("p a (j k) -> p a j k", k=P)
        res = env.sb(ctx, "result", [P, 2, RW])
        ps = env.banks(ctx, "ps_score", 4)
        pt = env.banks(ctx, "ps_pt", 2)
        pv = env.banks(ctx, "ps_pv", 2)
        block = ctx.enter_context(nc.Block())

        @block.sync
        def _(sp):
            views = [v_d.rearrange("(t p) c -> p t c", p=P),
                     v_d.rearrange("(n i r) c -> i n (r c)", i=P, r=4),
                     v_d.rearrange("(i r) c -> i (r c)", r=16)]
            def load_v(p):
                if p == 2:
                    sp.wait_ge(pvm.h, pvm.at(2 * NT))
                dst = V[:, p % 2, :, :]
                if p == 1:
                    dst = dst.rearrange("i (n r) c -> i n (r c)", r=4)
                if p == 2:
                    dst = dst.rearrange("i r c -> i (r c)")
                sp.dma_start(dst, views[p]).then_inc(vl[p % 2].h, 16)

            load_v(0)
            load_v(1)
            for u in range(1, U, 2):
                p, t, hh, (q0, dil), *_ = plan[u]
                tile = u // 2
                sp.wait_ge(pvc.h, pvc.at(u + 1))
                sp.wait_ge(ex.h, ex.at(4 * (u + 1)))
                rows = res_d[p][q0:q0 + dil * (P - 1) + 1:dil, :]
                sp.dma_start(rows, res[:, tile % 2, :]).then_inc(rs[tile % 2].h, 16)
                if u == 2 * NT + 3:
                    load_v(2)
            for i in range(2):
                sp.wait_ge(rs[i].h, rs[i].at(16 * (U // 4)))

        @block.tensor
        def _(pe):
            def scores(u):
                p, t, hh, (q0, dil), (k0, _), w, vt = plan[u]
                if u >= 2:
                    pe.wait_ge(sm_.h, sm_.at(4 * (u - 1)))
                for odd in range(2):
                    for j in range(2):
                        pair, lo = 2 * hh + j, HD * odd
                        mm = pe.matmul(ps[2 * (u % 2) + odd][:, j * 2 * P:j * 2 * P + w * P],
                                       QT[lo:lo + HD, pair, q0:q0 + dil * (P - 1) + 1:dil],
                                       KTt[lo:lo + HD, pair, k0:k0 + dil * (w * P - 1) + 1:dil], start=True, stop=True)
                mm.then_inc(smm.h, 1)

            def turn(u):
                w = plan[u][5]
                pe.wait_ge(ex.h, ex.at(4 * (u + 1)))
                for b in range(2):
                    if u >= 1:
                        c = (tc0, tc1)[b]
                        pe.wait_ge(c.h, c.at(u))
                    for j in range(2):
                        for x in range(w):
                            mm = pe.transpose(pt[b][:, (j * w + x) * P:(j * w + x + 1) * P],
                                              pr[:, u % 2, 2 * b + j, x * P:(x + 1) * P], env.ident[:, :])
                    mm.then_inc(tm.h, 1)

            def values(u):
                p, t, hh, _, _, w, vt = plan[u]
                if u % (2 * NT) == 0:
                    pe.wait_ge(vl[p % 2].h, vl[p % 2].at(16 * (p // 2 + 1)))
                if u >= 2:
                    pe.wait_ge(pvc.h, pvc.at(u - 1))
                for b in range(2):
                    c = (tc0, tc1)[b]
                    pe.wait_ge(c.h, c.at(u + 1))
                    for j in range(2):
                        head = 2 * (2 * hh + j) + b
                        for x in range(w):
                            mm = pe.matmul(pv[u % 2][:, (head % 4) * HD:(head % 4 + 1) * HD],
                                           pT[:, u % 2, 4 * b + j * w + x, :], V[:, p % 2, vt[x], head * HD:(head + 1) * HD],
                                           start=(x == 0), stop=(x == w - 1))
                mm.then_inc(pvm.h, 1)

            scores(0)
            scores(1)
            for u in range(U):
                turn(u)
                if u + 2 < U:
                    scores(u + 2)
                values(u)

        def slot_head(hh, b, j):
            return 2 * (2 * hh + j) + b

        @block.vector
        def _(dve):
            def minima(u):
                p, t, hh, _, _, w, _ = plan[u]
                dve.wait_ge(smm.h, smm.at(u + 1))
                if u >= 2:
                    dve.wait_ge(tm.h, tm.at(2 * (u - 1)))
                if hh == 0 and u >= 4:
                    i = (u // 2) % 2
                    dve.wait_ge(rs[i].h, rs[i].at(16 * (u // 4)))
                for b in range(2):
                    for j in range(2):
                        h = slot_head(hh, b, j)
                        dve.tensor_tensor_reduce(sc[:, u % 2, 2 * b + j, 0:w * P],
                                                 ps[2 * (u % 2) + b][:, j * 2 * P:j * 2 * P + w * P],
                                                 env.mask1[:, (2 - w) * P:2 * P], 1.0, 3e38, ALU.add, ALU.min,
                                                 res[:, (u // 2) % 2, H1 * HD + h:H1 * HD + h + 1]).then_inc(sm_.h, 1)

            def copies(u):
                p, t, hh, _, _, w, _ = plan[u]
                dve.wait_ge(tm.h, tm.at(2 * u + 2))
                if u >= 2:
                    dve.wait_ge(pvm.h, pvm.at(u - 1))
                dve.tensor_copy(pT[:, u % 2, 4:4 + 2 * w, :], pt[1][:, 0:2 * w * P].rearrange("p (a b) -> p a b", b=P))\
                   .then_inc(tc1.h, 1)
                dve.wait_ge(pvm.h, pvm.at(u + 1))
                dve.tensor_copy(res[:, (u // 2) % 2, hh * 4 * HD:(hh + 1) * 4 * HD], pv[u % 2][:, 0:4 * HD]).then_inc(pvc.h, 1)

            minima(0)
            for u in range(U):
                if u + 1 < U:
                    minima(u + 1)
                copies(u)

        @block.scalar
        def _(act):
            for u in range(U + 1):
                if u < U:
                    p, t, hh, _, _, w, _ = plan[u]
                    for b in range(2):
                        for j in range(2):
                            h = slot_head(hh, b, j)
                            act.wait_ge(sm_.h, sm_.at(4 * u + 2 * b + j + 1))
                            act.activation(pr[:, u % 2, 2 * b + j, 0:w * P], sc[:, u % 2, 2 * b + j, 0:w * P], ACT.Exp,
                                           bias=res[:, (u // 2) % 2, H1 * HD + h:H1 * HD + h + 1], scale=-1.0,
                                           accum_out=res[:, (u // 2) % 2, H1 * HD + H1 + h:H1 * HD + H1 + h + 1])\
                               .then_inc(ex.h, 1)
                if u >= 1:
                    v = u - 1
                    w = plan[v][5]
                    act.wait_ge(tm.h, tm.at(2 * v + 1))
                    if v >= 2:
                        act.wait_ge(pvm.h, pvm.at(v - 1))
                    act.activation(pT[:, v % 2, 0:2 * w, :], pt[0][:, 0:2 * w * P].rearrange("p (a b) -> p a b", b=P),
                                   ACT.Copy).then_inc(tc0.h, 1)
    for s_, c_ in ((smm, U), (sm_, 4 * U), (ex, 4 * U), (tm, 2 * U), (tc0, U), (tc1, U), (pvm, U), (pvc, U),
                   (vl[0], 32), (vl[1], 16), (rs[0], 16 * (U // 4)), (rs[1], 16 * (U // 4))):
        s_.base += c_


def stage_output1(env, yaT, sumsq, res_d, gb_d, gate, h_d):
    nc, A = env.nc, env.A
    ld = [env.sem("o_rows0"), env.sem("o_rows1")]
    xld = [env.sem("o_x0"), env.sem("o_x1")]
    yb, tm, tc, mmd, st = (env.sem(n) for n in ("yb_done", "yb_turned", "yb_copied", "out_mm", "out_sum"))
    ra, pa, pb = env.sem("ra_ready"), env.sem("out_a_scaled"), env.sem("out_b_added")
    hs = [env.sem("h_stored0"), env.sem("h_stored1")]
    mn, wx = env.sem("min_ready"), env.sem("weight_exp")
    sqs, pw_in, pw = env.sem("sq_ready"), env.sem("pow_in"), env.sem("pow_out")
    with ExitStack() as ctx:
        wo = env.sb(ctx, "w_out", [P, KT, D])
        r = env.sb(ctx, "res_rows", [P, 2, 3, RW])
        gb = env.sb(ctx, "gb_rows", [P, 2, H1 * HD])
        xr = env.sb(ctx, "x_res", [P, 2, D])
        sm = env.sb(ctx, "smalls", [P, 2, 12, H1])
        ybn = env.sb(ctx, "yb_rows", [P, 2, H1 * HD])
        tmp = env.sb(ctx, "yb_tmp", [P, 2, H1 * HD])
        junk = env.sb(ctx, "junk", [P, 2, D])
        ybT = env.sb(ctx, "yb_t", [P, 2, 4, P])
        mix = env.sb(ctx, "mix", [P, 2, D])
        stt = env.sb(ctx, "stats", [P, NT, 8])
        rst = env.sb(ctx, "ya_rstd", [P, 2, NT])
        pA = env.banks(ctx, "ps_oa", 2)
        pB = env.banks(ctx, "ps_ob", 2)
        pT = env.banks(ctx, "ps_ybt", 1)
        block = ctx.enter_context(nc.Block())

        @block.sync
        def _(sp):
            sp.dma_start(wo[:, :, :], A["w_out"][0].rearrange("(k p) c -> p k c", p=P)).then_inc(env.sem("wo_loaded").h, 16)
            for t in range(NT + 2):
                if t < NT:
                    if t >= 2:
                        sp.wait_ge(yb.h, yb.at(t - 1))
                        sp.wait_ge(st.h, st.at(t - 1))
                    rows = slice(t * P, (t + 1) * P)
                    for p in range(3):
                        sp.dma_start(r[:, t % 2, p, :], res_d[p][rows, :]).then_inc(ld[t % 2].h, 16)
                    sp.dma_start(gb[:, t % 2, :], gb_d[rows, :]).then_inc(ld[t % 2].h, 16)
                    sp.dma_start(xr[:, t % 2, :], A["x"][0, rows, :]).then_inc(xld[t % 2].h, 16)
                if t >= 2:
                    v = t - 2
                    sp.wait_ge(st.h, st.at(v + 1))
                    sp.dma_start(h_d[v * P:(v + 1) * P, :], mix[:, v % 2, :]).then_inc(hs[v % 2].h, 16)
            for i in range(2):
                sp.wait_ge(hs[i].h, hs[i].at(16 * (NT // 2)))

        @block.gpsimd
        def _(pool):
            pool.wait_ge(pw_in.h, pw_in.at(1))
            pool.tensor_tensor(rst[:, 1, :], rst[:, 0, :], env.mhalf[:, :].to_broadcast([P, NT]), ALU.pow).then_inc(ra.h, 1)
            n = 1
            for t in range(NT + 1):
                if t < NT:
                    n += 1
                    pool.wait_ge(pw_in.h, pw_in.at(n))
                    pool.tensor_tensor(stt[:, t, 2:3], stt[:, t, 1:2], env.mhalf[:, :], ALU.pow).then_inc(pw.h, 1)
                if t >= 1:
                    n += 1
                    pool.wait_ge(pw_in.h, pw_in.at(n))
                    pool.tensor_tensor(stt[:, t - 1, 5:6], stt[:, t - 1, 4:5], env.mhalf[:, :], ALU.pow).then_inc(pw.h, 1)

        @block.tensor
        def _(pe):
            for t in range(NT + 1):
                if t < NT:
                    pe.wait_ge(yb.h, yb.at(t + 1))
                    if t >= 1:
                        pe.wait_ge(tc.h, tc.at(t))
                    for j in range(4):
                        mm = pe.transpose(pT[0][:, j * P:(j + 1) * P], ybn[:, t % 2, j * P:(j + 1) * P], env.ident[:, :])
                    mm.then_inc(tm.h, 1)
                if t == 0:
                    pe.wait_ge(env.sem("wo_scaled").h, 1)
                    continue
                v = t - 1
                for part, (bank, freed) in enumerate(((pA, pa), (pB, pb))):
                    if v >= 1:
                        pe.wait_ge(freed.h, freed.at(2 * v))
                    if part:
                        pe.wait_ge(tc.h, tc.at(v + 1))
                    for half in range(2):
                        for k in range(4):
                            lhs = yaT[:, k, v * P:(v + 1) * P] if part == 0 else ybT[:, v % 2, k, :]
                            mm = pe.matmul(bank[half][:, :], lhs, wo[:, 4 * part + k, half * CH:(half + 1) * CH],
                                           start=(k == 0), stop=(k == 3))
                    mm.then_inc(mmd.h, 1)

        @block.scalar
        def _(act):
            n_exp = 0
            for t in range(NT + 1):
                if t < NT:
                    act.wait_ge(mn.h, mn.at(t + 1))
                    act.activation(sm[:, t % 2, 4:7, :], sm[:, t % 2, 1:4, :], ACT.Exp).then_inc(wx.h, 1)
                    act.wait_ge(yb.h, yb.at(t + 1))
                    if t >= 1:
                        act.wait_ge(sqs.h, sqs.at(max(1, 2 * t - 2)))
                    act.activation(junk[:, 0, 0:H1 * HD], ybn[:, t % 2, :], ACT.Square,
                                   accum_out=stt[:, t, 0:1]).then_inc(sqs.h, 1)
                    act.wait_ge(tm.h, tm.at(t + 1))
                    if t >= 2:
                        act.wait_ge(mmd.h, mmd.at(2 * (t - 1)))
                    act.activation(ybT[:, t % 2, :, :], pT[0][:, :].rearrange("p (a b) -> p a b", b=P), ACT.Copy)\
                       .then_inc(tc.h, 1)
                if t >= 1:
                    v = t - 1
                    if v == 0:
                        act.wait_ge(ra.h, ra.at(1))
                    act.wait_ge(mmd.h, mmd.at(2 * v + 1))
                    if v >= 2:
                        act.wait_ge(hs[v % 2].h, hs[v % 2].at(16 * (v // 2)))
                    for half in range(2):
                        act.activation(mix[:, v % 2, half * CH:(half + 1) * CH], pA[half][:, :], ACT.Copy,
                                       scale=rst[:, 1, v:v + 1]).then_inc(pa.h, 1)
                    act.wait_ge(pb.h, pb.at(2 * v + 2))
                    if v >= 1:
                        act.wait_ge(sqs.h, sqs.at(2 * v + 1))
                    act.activation(junk[:, 1, :], mix[:, v % 2, :], ACT.Square, accum_out=stt[:, v, 3:4]).then_inc(sqs.h, 1)

        @block.vector
        def _(dve):
            link = Link(dve, env.sem("dve_chain"))
            dve.tensor_scalar(rst[:, 0, :], sumsq[:, :], 1.0 / DREC, EPS, ALU.mult, ALU.add).then_inc(pw_in.h, 1)
            dve.wait_ge(env.sem("wo_loaded").h, 16)
            for k in range(KT):
                g = env.cols("norm_rec", 4) if k < 4 else env.cols("norm_att", 4)
                ins = dve.tensor_scalar(wo[:, k, :], wo[:, k, :], g[:, k % 4:k % 4 + 1], None, ALU.mult)
            ins.then_inc(env.sem("wo_scaled").h, 1)
            nsq = 0
            for t in range(NT + 1):
                if t < NT:
                    b = t % 2
                    R, s = r[:, b, :, :], sm[:, b, :, :]
                    o = H1 * HD
                    dve.wait_ge(ld[b].h, ld[b].at(64 * (t // 2 + 1)))
                    link(dve.tensor_tensor(s[:, 0, :], R[:, 0, o:o + H1], R[:, 1, o:o + H1], ALU.min))
                    link(dve.tensor_tensor(s[:, 0, :], s[:, 0, :], R[:, 2, o:o + H1], ALU.min))
                    dve.tensor_tensor(s[:, 1:4, :], s[:, 0:1, :].to_broadcast([P, 3, H1]), R[:, :, o:o + H1],
                                      ALU.subtract).then_inc(mn.h, 1)
                    dve.wait_ge(wx.h, wx.at(t + 1))
                    link(dve.tensor_tensor(s[:, 7:10, :], s[:, 4:7, :], R[:, :, o + H1:o + 2 * H1], ALU.mult))
                    link(dve.tensor_tensor(s[:, 10, :], s[:, 7, :], s[:, 8, :], ALU.add))
                    link(dve.tensor_tensor(s[:, 10, :], s[:, 10, :], s[:, 9, :], ALU.add))
                    link(dve.reciprocal(s[:, 10, :], s[:, 10, :]))
                    link(dve.tensor_tensor(s[:, 7:10, :], s[:, 4:7, :], s[:, 10:11, :].to_broadcast([P, 3, H1]), ALU.mult))
                    for p in range(3):
                        ins = dve.tensor_tensor(R[:, p, 0:o].rearrange("p (h e) -> p h e", e=HD),
                                                R[:, p, 0:o].rearrange("p (h e) -> p h e", e=HD),
                                                s[:, 7 + p, :, None].to_broadcast([P, H1, HD]), ALU.mult)
                    link(ins)
                    link(dve.tensor_tensor(tmp[:, b, :], R[:, 0, 0:o], R[:, 1, 0:o], ALU.add))
                    link(dve.tensor_tensor(tmp[:, b, :], tmp[:, b, :], R[:, 2, 0:o], ALU.add))
                    if t >= 2:
                        dve.wait_ge(tm.h, tm.at(t - 1))
                    dve.tensor_tensor(ybn[:, b, :], tmp[:, b, :], gb[:, b, :], ALU.mult).then_inc(yb.h, 1)
                    nsq += 1
                    dve.wait_ge(sqs.h, sqs.at(nsq))
                    dve.tensor_scalar(stt[:, t, 1:2], stt[:, t, 0:1], 1.0 / (H1 * HD), EPS, ALU.mult, ALU.add)\
                       .then_inc(pw_in.h, 1)
                if t >= 1:
                    v = t - 1
                    dve.wait_ge(pw.h, pw.at(1 if v == 0 else 2 * v))
                    dve.wait_ge(mmd.h, mmd.at(2 * v + 2))
                    dve.wait_ge(pa.h, pa.at(2 * v + 2))
                    for half in range(2):
                        sl = slice(half * CH, (half + 1) * CH)
                        dve.scalar_tensor_tensor(out=mix[:, v % 2, sl], in0=pB[half][:, :], scalar=stt[:, v, 2:3],
                                                 in1=mix[:, v % 2, sl], op0=ALU.mult, op1=ALU.add).then_inc(pb.h, 1)
                    nsq += 1
                    dve.wait_ge(sqs.h, sqs.at(nsq))
                    dve.tensor_scalar(stt[:, v, 4:5], stt[:, v, 3:4], 1.0 / D, EPS, ALU.mult, ALU.add).then_inc(pw_in.h, 1)
                    dve.wait_ge(pw.h, pw.at(2 * v + 3 if v < NT - 1 else 2 * v + 2))
                    dve.wait_ge(xld[v % 2].h, xld[v % 2].at(16 * (v // 2 + 1)))
                    link(dve.scalar_tensor_tensor(out=mix[:, v % 2, :], in0=mix[:, v % 2, :], scalar=stt[:, v, 5:6],
                                                  in1=gate[:, :], op0=ALU.mult, op1=ALU.mult))
                    dve.tensor_tensor(mix[:, v % 2, :], mix[:, v % 2, :], xr[:, v % 2, :], ALU.add).then_inc(st.h, 1)
            link.close()
    for s_, c_ in ((yb, NT), (tm, NT), (tc, NT), (mmd, 2 * NT), (st, NT), (ra, 1), (pa, 2 * NT), (pb, 2 * NT), (mn, NT),
                   (wx, NT), (sqs, 2 * NT), (pw_in, 2 * NT + 1), (pw, 2 * NT), (hs[0], 16 * (NT // 2)), (hs[1], 16 * (NT // 2)),
                   (ld[0], 64 * (NT // 2)), (ld[1], 64 * (NT // 2)), (xld[0], 16 * (NT // 2)), (xld[1], 16 * (NT // 2))):
        s_.base += c_


CTX = 256
W = S + CTX
WT = W // P
CHUNKS = [(q * CH, CH) for q in range(S // CH)] + [(S, CTX)]


def stage_hgrn_in(env, hT, qT, vN, zT, zchunks):
    nc = env.nc
    g0 = env.next_group
    units = [("t", 0, m, c, qT) for m in range(2) for c in CHUNKS]
    units += [("n", 1, t, None, vN) for t in range(WT)]
    units += [("t", 2, m, c, zT) for m in range(2) for c in zchunks]
    mmd, ev = env.sem("proj_mm"), env.sem("proj_out")
    with ExitStack() as ctx:
        ps = env.banks(ctx, "ps_in", 4)
        block = ctx.enter_context(nc.Block())

        @block.sync
        def _(sp):
            env.load_groups(sp, g0 + 3 + 1)

        @block.tensor
        def _(pe):
            for u, (kind, g, m, c, dst) in enumerate(units):
                w = env.group_here(pe, g0 + g)
                if u >= 4:
                    pe.wait_ge(ev.h, ev.at(u - 3))
                for k in range(KT):
                    if kind == "t":
                        mm = pe.matmul(ps[u % 4][:, 0:c[1]], w[:, k, m * P:(m + 1) * P], hT[:, k, c[0]:c[0] + c[1]],
                                       start=(k == 0), stop=(k == KT - 1))
                    else:
                        mm = pe.matmul(ps[u % 4][:, 0:GC], hT[:, k, m * P:(m + 1) * P], w[:, k, :],
                                       start=(k == 0), stop=(k == KT - 1))
                mm.then_inc(mmd.h, 1)
                if u + 1 == len(units) or units[u + 1][1] != g:
                    pe.wait_ge(mmd.h, mmd.at(u + 1))
                    pe.sem_inc(env.sem("w_used").h, 1)

        @block.scalar
        def _(act):
            for u, (kind, g, m, c, dst) in enumerate(units):
                act.wait_ge(mmd.h, mmd.at(u + 1))
                if kind == "t":
                    act.activation(dst[:, m, c[0]:c[0] + c[1]], ps[u % 4][:, 0:c[1]], ACT.Silu).then_inc(ev.h, 1)
                else:
                    act.activation(dst[:, m, :], ps[u % 4][:, 0:GC], ACT.Copy).then_inc(ev.h, 1)
    mmd.base += len(units)
    ev.base += len(units)
    env.next_group += 3


def stage_hgrn_scan(env, layer, d, hT, qT, vN, oT, out_ctx):
    nc, A = env.nc, env.A
    g = env.next_group
    lat = [(S // CH - 1 - q if d else q) for q in range(S // CH)]
    steps = [(S, 2)] + [(q * CH, 4) for q in lat]
    NSTEP = len(steps)
    LV = 8
    pj, fk, fl = env.sem("f_mm"), env.sem("f_done"), env.sem("f_bounded")
    qi, up, sc, cp = env.sem("qf_start"), env.sem("level_up"), env.sem("score_lv"), env.sem("score_kept")
    tm, tc, um, su, om, oc = (env.sem(n) for n in ("kb_turned", "kb_copied", "state_mm", "state_up", "o_mm", "o_out"))
    qh, kh = (0, 1) if d else (1, 0)
    NU = 2 * LV
    with ExitStack() as ctx:
        f = env.sb(ctx, "f", [P, 2, CH])
        kb = env.sb(ctx, "kb", [P, 2, CH])
        qf = env.sb(ctx, "qf", [P, 2, CH])
        fn = env.sb(ctx, "f_next", [P, 2, CH])
        kn = env.sb(ctx, "k_next", [P, 2, CH])
        pp = env.sb(ctx, "products", [P, 2, CH])
        sT = env.sb(ctx, "scores_t", [P, 2, 2, CH])
        kbn = env.sb(ctx, "kb_rows", [P, 2, CH])
        st = env.sb(ctx, "state", [P, 2, 2, P])
        poff = [0] * 8
        for l in range(1, 8):
            poff[l] = poff[l - 1] + (CH >> (l - 1) if l > 1 else 0)
        pf = env.banks(ctx, "ps_f", 2)
        pS = [env.banks(ctx, f"ps_s{i}", 2) for i in range(2)]
        pO = env.banks(ctx, "ps_o", 2)
        block = ctx.enter_context(nc.Block())

        def prod(pr, l, n):
            return f[:, pr, 0:n * P] if l == 0 else pp[:, pr, poff[l]:poff[l] + (n * P >> l)]

        @block.sync
        def _(sp):
            env.load_groups(sp, g + 1 + 1)

        @block.tensor
        def _(pe):
            w = env.group_here(pe, g)

            def project(s, pr, k):
                col, n = steps[s]
                if k == 0 and s >= 1:
                    pe.wait_ge(fk.h, fk.at(4 * (s - 1) + 2 * pr + 2))
                mm = pe.matmul(pf[pr][:, 0:n * P], w[:, k, pr * P:(pr + 1) * P], hT[:, k, col:col + n * P],
                               start=(k == 0), stop=(k == KT - 1))
                if k == KT - 1:
                    mm.then_inc(pj.h, 1)

            for pr in range(2):
                for k in range(KT):
                    project(0, pr, k)
            for s, (col, n) in enumerate(steps):
                for lv in range(LV):
                    for pr in range(2):
                        if lv < 2:
                            pe.wait_ge(qi.h, qi.at(4 * s + 2 * pr + 2))
                        else:
                            pe.wait_ge(up.h, up.at(14 * s + 2 * (lv - 2) + pr + 1))
                        if lv >= 1:
                            pe.wait_ge(cp.h, cp.at(2 * (NU * s + 2 * (lv - 1) + pr) + 2))
                        elif s >= 1:
                            pe.wait_ge(su.h, su.at(sum(2 * m for _, m in steps[:s])))
                            pe.wait_ge(tc.h, tc.at(2 * s))
                        for h in range(2):
                            lo = HD * h
                            for i in range(n):
                                cs = slice(i * P, (i + 1) * P)
                                rhs = qT[lo:lo + HD, pr, col + i * P:col + (i + 1) * P] if lv == 0 else qf[lo:lo + HD, pr, cs]
                                mm = pe.matmul(pS[pr][h][:, cs], kb[lo:lo + HD, pr, cs], rhs, start=True, stop=True)
                        mm.then_inc(sc.h, 1)
                        if s + 1 < NSTEP:
                            project(s + 1, pr, lv)
                for pr in range(2):
                    pe.wait_ge(up.h, up.at(14 * s + 12 + pr + 1))
                    pe.wait_ge(cp.h, cp.at(2 * (NU * s + 2 * (LV - 1) + pr) + 2))
                    for i in range(n):
                        mm = pe.transpose(pS[pr][0][:, i * P:(i + 1) * P], kb[:, pr, i * P:(i + 1) * P], env.ident[:, :])
                    mm.then_inc(tm.h, 1)
                for pr in range(2):
                    pe.wait_ge(tc.h, tc.at(2 * s + pr + 1))
                    for i in range(n):
                        mm = pe.matmul(pS[pr][1][:, i * P:(i + 1) * P], kbn[:, pr, i * P:(i + 1) * P],
                                       vN[:, col // P + i, pr * P:(pr + 1) * P], start=True, stop=True)
                    mm.then_inc(um.h, 1)
                order = range(n - 1, -1, -1) if d else range(n)
                for x, i in enumerate(order):
                    n_done = sum(m for _, m in steps[:s]) + x
                    for pr in range(2):
                        cs = slice(i * P, (i + 1) * P)
                        if x == 0 and s >= 1:
                            pe.wait_ge(oc.h, oc.at(2 * (s - 1) + pr + 1))
                        for h in range(2):
                            pe.matmul(pO[pr][HD * h:HD * (h + 1), cs],
                                      vN[:, col // P + i, pr * P + h * HD:pr * P + (h + 1) * HD],
                                      sT[:, pr, h, cs], start=True, stop=False)
                        if n_done >= 1:
                            pe.wait_ge(su.h, su.at(2 * (n_done - 1) + pr + 1))
                        for h in range(2):
                            lo = slice(HD * h, HD * (h + 1))
                            mm = pe.matmul(pO[pr][lo, cs], st[lo, pr, n_done % 2, lo], qf[lo, pr, cs],
                                           start=False, stop=True)
                        mm.then_inc(om.h, 1)
            pe.wait_ge(om.h, om.at(2 * WT))
            pe.sem_inc(env.sem("w_used").h, 1)

        @block.scalar
        def _(act):
            def sigmoids(s):
                n = steps[s][1]
                for pr in range(2):
                    act.wait_ge(pj.h, pj.at(2 * s + pr + 1))
                    if s >= 1:
                        act.wait_ge(qi.h, qi.at(4 * (s - 1) + 4))
                    act.activation(fn[:, pr, 0:n * P], pf[pr][:, 0:n * P], ACT.Sigmoid).then_inc(fk.h, 1)
                    act.activation(kn[:, pr, 0:n * P], pf[pr][:, 0:n * P], ACT.Sigmoid, scale=-1.0).then_inc(fk.h, 1)

            sigmoids(0)
            for s, (col, n) in enumerate(steps):
                if s + 1 < NSTEP:
                    sigmoids(s + 1)
                for pr in range(2):
                    act.wait_ge(tm.h, tm.at(2 * s + pr + 1))
                    if s >= 1:
                        act.wait_ge(um.h, um.at(2 * (s - 1) + pr + 1))
                    act.activation(kbn[:, pr, 0:n * P], pS[pr][0][:, 0:n * P], ACT.Copy).then_inc(tc.h, 1)
                if d == 0:
                    for pr in range(2):
                        act.wait_ge(om.h, om.at(2 * sum(m for _, m in steps[:s + 1])))
                        act.activation(oT[:, pr, col:col + n * P], pO[pr][:, 0:n * P], ACT.Copy).then_inc(oc.h, 1)

        if layer == 1:
            @block.gpsimd
            def _(pool):
                for s, (col, n) in enumerate(steps):
                    for pr in range(2):
                        pool.wait_ge(fk.h, fk.at(4 * s + 2 * pr + 2))
                        lo, hi = env.lb[:, 0, d, pr:pr + 1], env.lb[:, 1, d, pr:pr + 1]
                        pool.tensor_scalar(fn[:, pr, 0:n * P], fn[:, pr, 0:n * P], hi, lo, ALU.mult, ALU.add).then_inc(fl.h, 1)
                        pool.tensor_scalar(kn[:, pr, 0:n * P], kn[:, pr, 0:n * P], hi, None, ALU.mult).then_inc(fl.h, 1)

        @block.vector
        def _(dve):
            link = Link(dve, env.sem("dve_chain"))
            link(dve.memset(st[:, :, :, :], 0.0))

            def halves(ap, h):
                return ap.rearrange("p (b a x) -> p b a x", a=2, x=h)

            for s, (col, n) in enumerate(steps):
                w = n * P
                ready, done = (fl, 4) if layer == 1 else (fk, 4)
                for pr in range(2):
                    dve.wait_ge(ready.h, ready.at(4 * s + 2 * pr + 2))
                    if s >= 1:
                        dve.wait_ge(tm.h, tm.at(2 * (s - 1) + pr + 1))
                        dve.wait_ge(om.h, om.at(2 * sum(m for _, m in steps[:s])))
                    dve.tensor_copy(f[:, pr, 0:w], fn[:, pr, 0:w])
                    dve.tensor_copy(kb[:, pr, 0:w], kn[:, pr, 0:w]).then_inc(qi.h, 1)
                    dve.tensor_tensor(qf[:, pr, 0:w], qT[:, pr, col:col + w], fn[:, pr, 0:w], ALU.mult).then_inc(qi.h, 1)
                dve.wait_ge(qi.h, qi.at(4 * s + 4))
                for lv in range(LV):
                    l = lv - 1
                    for pr in range(2):
                        dve.wait_ge(sc.h, sc.at(NU * s + 2 * lv + pr + 1))
                        if lv >= 1:
                            h = 1 << l
                            q2, k2 = halves(qf[:, pr, 0:w], h), halves(kb[:, pr, 0:w], h)
                            if lv >= 2:
                                dve.wait_ge(up.h, up.at(14 * s + 2 * (l - 1) + pr + 1))
                            p2 = prod(pr, l, n).rearrange("p (b a) -> p b a", a=2)
                            nb = w // (2 * h)
                            dve.tensor_tensor(q2[:, :, qh, :], q2[:, :, qh, :],
                                              p2[:, :, kh, None].to_broadcast([P, nb, h]), ALU.mult)
                            dve.tensor_tensor(k2[:, :, kh, :], k2[:, :, kh, :],
                                              p2[:, :, qh, None].to_broadcast([P, nb, h]), ALU.mult)
                            dve.tensor_tensor(prod(pr, l + 1, n), p2[:, :, 0], p2[:, :, 1], ALU.mult).then_inc(up.h, 1)
                        for h in range(2):
                            src = pS[pr][h][:, 0:w].rearrange("p (i x) -> p i x", x=P)
                            dst = sT[:, pr, h, 0:w].rearrange("p (i x) -> p i x", x=P)
                            if lv == 0:
                                dve.tensor_tensor(dst, src, env.ident[:, None, :].to_broadcast([P, n, P]), ALU.mult)\
                                   .then_inc(cp.h, 1)
                            else:
                                dve.wait_ge(cp.h, cp.at(2 * (NU * s + 2 * (lv - 1) + pr) + h + 1))
                                dve.copy_predicated(dst, env.levmask[:, 8 * d + l, None, :].to_broadcast([P, n, P]), src)\
                                   .then_inc(cp.h, 1)
                order = range(n - 1, -1, -1) if d else range(n)
                for x, i in enumerate(order):
                    n_done = sum(m for _, m in steps[:s]) + x
                    for pr in range(2):
                        if x == 0:
                            dve.wait_ge(um.h, um.at(2 * s + pr + 1))
                            dve.wait_ge(up.h, up.at(14 * s + 12 + pr + 1))
                        if n_done >= 1:
                            dve.wait_ge(om.h, om.at(2 * (n_done - 1) + pr + 1))
                            dve.wait_ge(su.h, su.at(2 * (n_done - 1) + pr + 1))
                        for h in range(2):
                            lo = slice(HD * h, HD * (h + 1))
                            ins = dve.scalar_tensor_tensor(
                                out=st[lo, pr, (n_done + 1) % 2, HD * h:HD * (h + 1)],
                                in0=st[lo, pr, n_done % 2, HD * h:HD * (h + 1)],
                                scalar=pp[lo, pr, poff[7] + i:poff[7] + i + 1],
                                in1=pS[pr][1][lo, i * P + HD * h:i * P + HD * (h + 1)], op0=ALU.mult, op1=ALU.add)
                        ins.then_inc(su.h, 1)
                if d == 1:
                    for pr in range(2):
                        dve.wait_ge(om.h, om.at(2 * sum(m for _, m in steps[:s + 1])))
                        dve.tensor_tensor(oT[:, pr, col:col + w], oT[:, pr, col:col + w], pO[pr][:, 0:w], ALU.add)\
                           .then_inc(oc.h, 1)
            link.close()
    for s_, c_ in ((pj, 2 * NSTEP), (fk, 4 * NSTEP), (fl, 4 * NSTEP if layer == 1 else 0), (qi, 4 * NSTEP), (up, 14 * NSTEP),
                   (sc, NU * NSTEP), (cp, 2 * NU * NSTEP), (tm, 2 * NSTEP), (tc, 2 * NSTEP), (um, 2 * NSTEP),
                   (su, 2 * WT), (om, 2 * WT), (oc, 2 * NSTEP)):
        s_.base += c_
    env.next_group += 1


def stage_hgrn_norm(env, layer, oT, zT, chunks):
    nc = env.nc
    units = [(pr, c) for pr in range(2) for c in chunks]
    sq, mm_, rt, rc, sd, yo = (env.sem(n) for n in ("o_squared", "o_mean", "o_root", "o_recip", "o_scaled", "o_gated"))
    with ExitStack() as ctx:
        o2 = env.sb(ctx, "o_sq", [P, 2, CH])
        rr = env.sb(ctx, "o_rms", [P, 2, CH])
        ps = env.banks(ctx, "ps_on", 2)
        block = ctx.enter_context(nc.Block())
        gains = env.cols("hgrn_norm_g_2", 4)

        @block.scalar
        def _(act):
            for u in range(len(units) + 1):
                if u < len(units):
                    pr, (c0, n) = units[u]
                    if u >= 2:
                        act.wait_ge(mm_.h, mm_.at(u - 1))
                    act.activation(o2[:, u % 2, 0:n], oT[:, pr, c0:c0 + n], ACT.Square).then_inc(sq.h, 1)
                if u >= 1:
                    v = u - 1
                    n = units[v][1][1]
                    act.wait_ge(mm_.h, mm_.at(v + 1))
                    if v >= 2:
                        act.wait_ge(sd.h, sd.at(v - 1))
                    act.activation(rr[:, v % 2, 0:n], ps[v % 2][:, 0:n], ACT.Sqrt, bias=env.eps[:, :]).then_inc(rt.h, 1)

        @block.tensor
        def _(pe):
            for u, (pr, (c0, n)) in enumerate(units):
                pe.wait_ge(sq.h, sq.at(u + 1))
                if u >= 2:
                    pe.wait_ge(rt.h, rt.at(u - 1))
                pe.matmul(ps[u % 2][:, 0:n], env.headmean[:, :], o2[:, u % 2, 0:n], start=True, stop=True).then_inc(mm_.h, 1)

        @block.vector
        def _(dve):
            for u, (pr, (c0, n)) in enumerate(units):
                o = oT[:, pr, c0:c0 + n]
                dve.wait_ge(rt.h, rt.at(u + 1))
                dve.reciprocal(rr[:, u % 2, 0:n], rr[:, u % 2, 0:n]).then_inc(rc.h, 1)
                dve.wait_ge(rc.h, rc.at(u + 1))
                dve.scalar_tensor_tensor(out=o, in0=o, scalar=gains[:, 2 * layer + pr:2 * layer + pr + 1],
                                         in1=rr[:, u % 2, 0:n], op0=ALU.mult, op1=ALU.mult).then_inc(sd.h, 1)

        @block.gpsimd
        def _(pool):
            for u, (pr, (c0, n)) in enumerate(units):
                o = oT[:, pr, c0:c0 + n]
                pool.wait_ge(sd.h, sd.at(u + 1))
                pool.tensor_tensor(o, o, zT[:, pr, c0:c0 + n], ALU.mult).then_inc(yo.h, 1)
    for s_ in (sq, mm_, rt, rc, sd, yo):
        s_.base += len(units)


def stage_qkv2(env, layer, hT, QT, KTt, VN, aT, qtiles, zchunks):
    nc, A = env.nc, env.A
    g0 = env.next_group
    units = [(0, t, 4) for t in range(qtiles)] + [(1, t, 2) for t in range(WT)]
    zun = [(m, c) for m in range(2) for c in zchunks]
    NU = len(units)
    mmd, nrm, rp, st = env.sem("proj_mm"), env.sem("qk_normed"), env.sem("rope_read"), env.sem("rope_sum")
    sq, mn, pw, vv = env.sem("qk_sq"), env.sem("qk_mean"), env.sem("qk_rstd"), env.sem("v_kept")
    tq, tc = env.sem("qk_turned"), env.sem("qk_copied")
    zm, ze = env.sem("az_mm"), env.sem("az_out")
    NV = sum(1 for u in units if u[0] == 1)
    with ExitStack() as ctx:
        s2 = env.sb(ctx, "qk_square", [P, 2, GC])
        ss = env.sb(ctx, "qk_stats", [P, 3, NU, 4])
        nn = env.sb(ctx, "qk_rows", [P, 2, GC])
        ta = env.sb(ctx, "rope_a", [P, 2, GC])
        tb = env.sb(ctx, "rope_b", [P, 2, GC])
        nat = env.sb(ctx, "rope_rows", [P, 2, GC])
        cs = env.sb(ctx, "axial", [P, 2, NT, 32])
        gn = env.sb(ctx, "qk_gain", [P, 2, HD])
        ps = env.banks(ctx, "ps_proj", 4)
        pt = env.banks(ctx, "ps_qk", 2)
        pz = env.banks(ctx, "ps_az", 2)
        block = ctx.enter_context(nc.Block())
        ld = env.sem("axial_loaded")

        @block.sync
        def _(sp):
            sp.dma_start(cs[:, :, :, :], A["k_axial"]).then_inc(ld.h, 16)
            sp.dma_start(gn[:, 0, :], A["q_norm_g_2"][layer:layer + 1, :].to_broadcast([P, HD])).then_inc(ld.h, 16)
            sp.dma_start(gn[:, 1, :], A["k_norm_g_2"][layer:layer + 1, :].to_broadcast([P, HD])).then_inc(ld.h, 16)
            env.load_groups(sp, g0 + 3 + 1)

        def turned(u):
            return sum(2 if g == 0 else 1 for g, _, _ in units[:u + 1])

        @block.tensor
        def _(pe):
            def turn(u):
                g, t, nh = units[u]
                pe.wait_ge(st.h, st.at(u + 1))
                for x in range(nh // 2):
                    n = turned(u - 1) + x
                    if n >= 2:
                        pe.wait_ge(tc.h, tc.at(n - 1))
                    pe.transpose(pt[n % 2][:, 0:P], nat[:, u % 2, x * P:(x + 1) * P], env.ident[:, :]).then_inc(tq.h, 1)

            for u, (g, t, nh) in enumerate(units):
                w = env.group_here(pe, g0 + g)
                if u >= 4:
                    pe.wait_ge(nrm.h, nrm.at(u - 3))
                    pe.wait_ge(sq.h, sq.at(u - 3))
                    if units[u - 4][0] == 1:
                        pe.wait_ge(vv.h, vv.at(units[u - 4][1] + 1))
                for k in range(KT):
                    mm = pe.matmul(ps[u % 4][:, 0:GC], hT[:, k, t * P:(t + 1) * P], w[:, k, :],
                                   start=(k == 0), stop=(k == KT - 1))
                mm.then_inc(mmd.h, 1)
                if u + 1 == NU or units[u + 1][0] != g:
                    pe.wait_ge(mmd.h, mmd.at(u + 1))
                    pe.sem_inc(env.sem("w_used").h, 1)
                if u >= 3:
                    turn(u - 3)
            w = env.group_here(pe, g0 + 2)
            for z, (m, (c0, n)) in enumerate(zun):
                if z >= 2:
                    pe.wait_ge(ze.h, ze.at(z - 1))
                for k in range(KT):
                    mm = pe.matmul(pz[z % 2][:, 0:n], w[:, k, m * P:(m + 1) * P], hT[:, k, c0:c0 + n],
                                   start=(k == 0), stop=(k == KT - 1))
                mm.then_inc(zm.h, 1)
                if z < 3:
                    turn(NU - 3 + z)
            pe.wait_ge(zm.h, zm.at(len(zun)))
            pe.sem_inc(env.sem("w_used").h, 1)

        @block.scalar
        def _(act):
            def copy_turned(u):
                g, t, nh = units[u]
                for x in range(nh // 2):
                    n = turned(u - 1) + x
                    act.wait_ge(tq.h, tq.at(n + 1))
                    dst = QT[:, x, t * P:(t + 1) * P] if g == 0 else KTt[:, t * P:(t + 1) * P]
                    act.activation(dst, pt[n % 2][:, 0:P], ACT.Copy).then_inc(tc.h, 1)

            for u, (g, t, nh) in enumerate(units):
                act.wait_ge(mmd.h, mmd.at(u + 1))
                if u >= 2:
                    act.wait_ge(mn.h, mn.at(u - 1))
                act.activation(s2[:, u % 2, 0:nh * HD], ps[u % 4][:, 0:nh * HD], ACT.Square).then_inc(sq.h, 1)
                if g == 1:
                    act.activation(VN[:, t, :], ps[u % 4][:, P:2 * P], ACT.Copy).then_inc(vv.h, 1)
                if u >= 4:
                    copy_turned(u - 4)
            for z, (m, (c0, n)) in enumerate(zun):
                if z < 4:
                    copy_turned(NU - 4 + z)
                act.wait_ge(zm.h, zm.at(z + 1))
                act.activation(aT[:, m, c0:c0 + n], pz[z % 2][:, 0:n], ACT.Silu).then_inc(ze.h, 1)

        @block.vector
        def _(dve):
            link = Link(dve, env.sem("dve_chain"))
            dve.wait_ge(ld.h, ld.at(48))

            def mean(u):
                nh = units[u][2]
                dve.wait_ge(sq.h, sq.at(u + 1))
                link(dve.tensor_reduce(ss[:, 0, u, 0:nh], s2[:, u % 2, 0:nh * HD].rearrange("p (h e) -> p h e", e=HD),
                                       AXX, ALU.add))
                dve.tensor_scalar(ss[:, 1, u, 0:nh], ss[:, 0, u, 0:nh], 1.0 / HD, EPS, ALU.mult, ALU.add).then_inc(mn.h, 1)

            mean(0)
            for u, (g, t, nh) in enumerate(units):
                if u + 1 < NU:
                    mean(u + 1)
                w = nh * HD
                v3 = lambda a: a[:, u % 2, 0:w].rearrange("p (h e) -> p h e", e=HD)
                v4 = lambda a: a[:, u % 2, 0:w].rearrange("p (h j x) -> p h j x", j=32, x=2)
                dve.wait_ge(pw.h, pw.at(u + 1))
                if u >= 2:
                    dve.wait_ge(st.h, st.at(u - 1))
                if g == 1:
                    dve.wait_ge(vv.h, vv.at(t + 1))
                dve.tensor_tensor(v3(nn), ps[u % 4][:, 0:w].rearrange("p (h e) -> p h e", e=HD),
                                  ss[:, 2, u, 0:nh, None].to_broadcast([P, nh, HD]), ALU.mult).then_inc(nrm.h, 1)
                dve.wait_ge(nrm.h, nrm.at(u + 1))
                if t >= NT:
                    dve.tensor_tensor(v3(ta), v3(nn), gn[:, g, None, :].to_broadcast([P, nh, HD]), ALU.mult)
                    dve.memset(tb[:, u % 2, 0:w], 0.0).then_inc(rp.h, 1)
                    continue
                link(dve.tensor_tensor(v3(nn), v3(nn), gn[:, g, None, :].to_broadcast([P, nh, HD]), ALU.mult))
                cosv, sinv = (cs[:, i, t, None, :].to_broadcast([P, nh, 32]) for i in range(2))
                for x in range(2):
                    dve.tensor_tensor(v4(ta)[:, :, :, x], v4(nn)[:, :, :, x], cosv, ALU.mult)
                dve.scalar_tensor_tensor(out=v4(tb)[:, :, :, 0], in0=v4(nn)[:, :, :, 1], scalar=-1.0, in1=sinv,
                                         op0=ALU.mult, op1=ALU.mult)
                dve.tensor_tensor(v4(tb)[:, :, :, 1], v4(nn)[:, :, :, 0], sinv, ALU.mult).then_inc(rp.h, 1)
            link.close()

        @block.gpsimd
        def _(pool):
            def add(u):
                g, t, nh = units[u]
                w = nh * HD
                pool.wait_ge(rp.h, rp.at(u + 1))
                if u >= 2:
                    pool.wait_ge(tq.h, tq.at(turned(u - 2)))
                if g == 0:
                    dst = nat[:, u % 2, 0:w].rearrange("p (i v e) -> p v i e", v=2, e=HD)
                    a, b = (x[:, u % 2, 0:w].rearrange("p (v i e) -> p v i e", v=2, e=HD) for x in (ta, tb))
                else:
                    dst, a, b = (x[:, u % 2, 0:w] for x in (nat, ta, tb))
                pool.tensor_tensor(dst, a, b, ALU.add).then_inc(st.h, 1)

            for u, (g, t, nh) in enumerate(units):
                pool.wait_ge(mn.h, mn.at(u + 1))
                pool.tensor_tensor(ss[:, 2, u, 0:nh], ss[:, 1, u, 0:nh], env.mhalf[:, :].to_broadcast([P, nh]), ALU.pow)\
                    .then_inc(pw.h, 1)
                if u >= 1:
                    add(u - 1)
            add(NU - 1)
    T = turned(NU - 1)
    for s_, c_ in ((mmd, NU), (nrm, NU), (rp, NU), (st, NU), (sq, NU), (mn, NU), (pw, NU), (vv, NV), (tq, T), (tc, T),
                   (zm, len(zun)), (ze, len(zun)), (ld, 48)):
        s_.base += c_
    env.next_group += 3


def stage_attend(env, QT, KTt, VN, aT, qtiles):
    nc = env.nc
    units = []
    for t in range(qtiles):
        k0, nk = (0, WT) if t < NT else (NT, WT - NT)
        for h in range(4):
            units.append((t, h, k0, nk))
    U = len(units)
    nch = [-(-nk // 4) for _, _, _, nk in units]
    na = [-(-n // 2) for n in nch]
    nd = [n // 2 for n in nch]
    smm, mx, nb, ex = env.sem("score_mm"), env.sem("max_part"), env.sem("max_ready"), env.sem("prob_exp")
    tA, tD, cA, cD = (env.sem(n) for n in ("turn_a", "turn_d", "prob_copied_act", "prob_copied_dve"))
    pvm, nr, at, ac = (env.sem(n) for n in ("pv_mm", "att_normed", "att_turned", "att_gated"))
    with ExitStack() as ctx:
        pr = env.sb(ctx, "probs", [P, 2, W])
        pT = env.sb(ctx, "probs_t", [P, 4, CH])
        st = env.sb(ctx, "soft", [P, 2, 12])
        an = env.sb(ctx, "att_rows", [P, 2, GC])
        env.n_names += 1
        ps = ctx.enter_context(nc.psum_tensor(f"ps_scores_{env.n_names}", [P, 5 * CH], F32))
        pt = env.banks(ctx, "ps_pt", 2)
        pv = env.banks(ctx, "ps_pv", 1)[0]
        block = ctx.enter_context(nc.Block())

        def parts(u):
            nk = units[u][3]
            return [(b, min(4, nk - b)) for b in range(0, nk, 4)]

        def spans(u):
            nk = units[u][3]
            return [(0, min(8, nk))] + ([(8, nk - 8)] if nk > 8 else [])

        nsp = [len(spans(u)) for u in range(U)]

        @block.tensor
        def _(pe):
            def scores(u):
                t, h, k0, nk = units[u]
                kv, i = divmod(h, 2)
                lo = HD * kv
                done = 0
                for b, n in parts(u):
                    if u >= 1:
                        need = sum(nsp[:u - 1]) + (1 if b < 8 else nsp[u - 1])
                        pe.wait_ge(ex.h, ex.at(min(need, sum(nsp[:u]))))
                    mm = pe.matmul(ps[:, b * P:(b + n) * P], QT[lo:lo + HD, i, t * P:(t + 1) * P],
                                   KTt[lo:lo + HD, (k0 + b) * P:(k0 + b + n) * P], start=True, stop=True)
                    if b + n in (8, nk):
                        mm.then_inc(smm.h, 1)

            def turn(u, c):
                nk = units[u][3]
                n = min(4, nk - 4 * c)
                if c % 2 == 0:
                    i = sum(na[:u]) + c // 2
                    if i >= 1:
                        pe.wait_ge(cA.h, cA.at(i))
                else:
                    i = sum(nd[:u]) + c // 2
                    if i >= 1:
                        pe.wait_ge(cD.h, cD.at(i))
                for j in range(n):
                    k = 4 * c + j
                    mm = pe.transpose(pt[c % 2][:, j * P:(j + 1) * P], pr[:, u % 2, k * P:(k + 1) * P], env.ident[:, :])
                mm.then_inc((tA, tD)[c % 2].h, 1)

            def values(u, c):
                t, h, k0, nk = units[u]
                kv = h // 2
                n = min(4, nk - 4 * c)
                if c % 2 == 0:
                    pe.wait_ge(cA.h, cA.at(sum(na[:u]) + c // 2 + 1))
                else:
                    pe.wait_ge(cD.h, cD.at(sum(nd[:u]) + c // 2 + 1))
                if c == 0 and u >= 1:
                    pe.wait_ge(nr.h, nr.at(u))
                    if h == 0:
                        pe.wait_ge(ac.h, ac.at(u // 4))
                for j in range(n):
                    k = 4 * c + j
                    mm = pe.matmul(pv[:, 0:HD], pT[:, (sum(nch[:u]) + c) % 4, j * P:(j + 1) * P],
                                   VN[:, k0 + k, kv * HD:(kv + 1) * HD], start=(k == 0), stop=(k == nk - 1))
                mm.then_inc(pvm.h, 1)

            for u in range(U + 1):
                if u < U:
                    scores(u)
                if u >= 1:
                    v = u - 1
                    pe.wait_ge(ex.h, ex.at(sum(nsp[:v + 1])))
                    for c in range(nch[v] + 1):
                        if c < nch[v]:
                            turn(v, c)
                        if c >= 1:
                            values(v, c - 1)
                    if v % 4 == 3:
                        pe.wait_ge(nr.h, nr.at(v + 1))
                        for x in range(2):
                            mm = pe.transpose(pv[:, P + x * P:2 * P + x * P], an[:, (v // 4) % 2, x * P:(x + 1) * P],
                                              env.ident[:, :])
                        mm.then_inc(at.h, 1)

        @block.scalar
        def _(act):
            def copy(v, c):
                if c < nch[v]:
                    n = min(4, units[v][3] - 4 * c)
                    i = sum(nch[:v]) + c
                    act.wait_ge(tA.h, tA.at(sum(na[:v]) + c // 2 + 1))
                    if i >= 4:
                        act.wait_ge(pvm.h, pvm.at(i - 3))
                    act.activation(pT[:, i % 4, 0:n * P], pt[0][:, 0:n * P], ACT.Copy).then_inc(cA.h, 1)

            for u in range(U + 1):
                for x in range(2):
                    if u >= 1:
                        copy(u - 1, 2 * x)
                    if u < U and x < nsp[u]:
                        b, (k, n) = u % 2, spans(u)[x]
                        act.wait_ge(nb.h, nb.at(u + 1))
                        if u >= 2:
                            act.wait_ge(nr.h, nr.at(u - 1))
                        act.activation(pr[:, b, k * P:(k + n) * P], ps[:, k * P:(k + n) * P], ACT.Exp, bias=st[:, b, 4:5],
                                       scale=HD ** -0.5, accum_out=st[:, b, 5 + x:6 + x]).then_inc(ex.h, 1)
                if u >= 1:
                    copy(u - 1, 4)

        @block.vector
        def _(dve):
            link = Link(dve, env.sem("dve_chain"))

            def maxima(u):
                b = u % 2
                if u >= 2:
                    dve.wait_ge(nr.h, nr.at(u - 1))
                for x, (k, n) in enumerate(spans(u)):
                    dve.wait_ge(smm.h, smm.at(sum(nsp[:u]) + x + 1))
                    link(dve.tensor_reduce(st[:, b, x:x + 1], ps[:, k * P:(k + n) * P], AXX, ALU.max))
                if nsp[u] == 2:
                    link(dve.tensor_tensor(st[:, b, 0:1], st[:, b, 0:1], st[:, b, 1:2], ALU.max))
                dve.tensor_scalar(st[:, b, 4:5], st[:, b, 0:1], -(HD ** -0.5), None, ALU.mult).then_inc(nb.h, 1)

            def finish(v):
                t, h, k0, nk = units[v]
                b = v % 2
                for c in range(1, nch[v], 2):
                    n = min(4, nk - 4 * c)
                    i = sum(nch[:v]) + c
                    dve.wait_ge(tD.h, tD.at(sum(nd[:v]) + c // 2 + 1))
                    if i >= 4:
                        dve.wait_ge(pvm.h, pvm.at(i - 3))
                    dve.tensor_copy(pT[:, i % 4, 0:n * P], pt[1][:, 0:n * P]).then_inc(cD.h, 1)
                dve.wait_ge(ex.h, ex.at(sum(nsp[:v + 1])))
                if nsp[v] == 2:
                    link(dve.tensor_tensor(st[:, b, 8:9], st[:, b, 5:6], st[:, b, 6:7], ALU.add))
                    link(dve.reciprocal(st[:, b, 9:10], st[:, b, 8:9]))
                else:
                    link(dve.reciprocal(st[:, b, 9:10], st[:, b, 5:6]))
                dve.wait_ge(pvm.h, pvm.at(sum(nch[:v + 1])))
                if h == 0 and v >= 8:
                    dve.wait_ge(at.h, at.at(v // 4 - 1))
                dve.tensor_scalar(an[:, (v // 4) % 2, h * HD:(h + 1) * HD], pv[:, 0:HD], st[:, b, 9:10], None, ALU.mult)\
                   .then_inc(nr.h, 1)
                if h == 3:
                    dve.wait_ge(at.h, at.at(v // 4 + 1))
                    y = aT[:, :, t * P:(t + 1) * P]
                    dve.tensor_tensor(y, y, pv[:, P:3 * P].rearrange("p (m x) -> p m x", x=P), ALU.mult).then_inc(ac.h, 1)

            for u in range(U + 1):
                if u < U:
                    maxima(u)
                if u >= 1:
                    finish(u - 1)
            link.close()
    for s_, c_ in ((smm, sum(nsp)), (nb, U), (ex, sum(nsp)), (tA, sum(na)), (tD, sum(nd)), (cA, sum(na)), (cD, sum(nd)),
                   (pvm, sum(nch)), (nr, U), (at, U // 4), (ac, U // 4)):
        s_.base += c_


def stage_fourier(env, hT, uT, yT, with_ctx, zt_d):
    nc, A = env.nc, env.A
    g0 = env.next_group
    chunks = CHUNKS if with_ctx else CHUNKS[:-1]
    units = [(0, m, c, uT) for m in range(2) for c in chunks] + [(1, m, c, yT) for m in range(2) for c in chunks]
    mmd, ev = env.sem("proj_mm"), env.sem("proj_out")
    a_mm, a_ev, b_mm, b_ev = env.sem("ch_mm"), env.sem("ch_out"), env.sem("t1_mm"), env.sem("t1_out")
    c_mm, c_ev = env.sem("t2_mm"), env.sem("t2_out")
    a_ed = env.sem("ch_out_dve")
    ml = [env.sem(f"dft_loaded{i}") for i in range(3)]
    zs = [env.sem(f"z_stored{i}") for i in range(2)]
    zl = [env.sem(f"z_loaded{i}") for i in range(4)]
    cl = env.sem("dft_const")
    NB = 16
    NA = NB + (2 if with_ctx else 0)
    with ExitStack() as ctx:
        ch = env.sb(ctx, "dft_ch", [P, 3 * P])
        a = env.sb(ctx, "ch_rows", [P, 2, 3 * GC])
        m16 = env.sb(ctx, "dft_t1", [P, 3, 2, P])
        z = env.sb(ctx, "t1_rows", [P, 2, 2 * GC])
        zt = env.sb(ctx, "t2_rows", [P, 4, 2 * GC])
        m128 = env.sb(ctx, "dft_t2", [P, 2, P])
        mctx = env.sb(ctx, "dft_ctx", [P, 2, 2, CTX])
        ps = env.banks(ctx, "ps_in", 2)
        pa = env.banks(ctx, "ps_ch", 2)
        pb = env.banks(ctx, "ps_t1", 2)
        pc = env.banks(ctx, "ps_t2", 2)
        block = ctx.enter_context(nc.Block())

        @block.sync
        def _(sp):
            env.load_groups(sp, g0 + 2)
            sp.dma_start(ch[:, :], A["k_dft_ch"]).then_inc(cl.h, 16)
            sp.dma_start(m128[:, :, :], A["k_dft_128"]).then_inc(cl.h, 16)
            sp.dma_start(mctx[:, :, :, :], A["k_dft_ctx"]).then_inc(cl.h, 16)
            for b in range(NB):
                if b >= 3:
                    sp.wait_ge(b_mm.h, b_mm.at(b - 2))
                sp.dma_start(m16[:, b % 3, :, :], A["k_dft_16"][b]).then_inc(ml[b % 3].h, 16)
                if b >= 1:
                    sp.wait_ge(b_ev.h, b_ev.at(b))
                    sp.dma_start(zt_d[8 * (b - 1):8 * b].rearrange("a k c -> (a k) c"), z[:, (b - 1) % 2, :])\
                        .then_inc(zs[(b - 1) % 2].h, 16)
            sp.wait_ge(b_ev.h, b_ev.at(NB))
            sp.dma_start(zt_d[8 * (NB - 1):8 * NB].rearrange("a k c -> (a k) c"), z[:, (NB - 1) % 2, :])\
                .then_inc(zs[(NB - 1) % 2].h, 16)
            for i in range(2):
                sp.wait_ge(zs[i].h, zs[i].at(16 * NB // 2))
            for k in range(NB):
                if k >= 4:
                    sp.wait_ge(c_mm.h, c_mm.at(k - 3))
                sp.dma_start(zt[:, k % 4, :], zt_d[:, k, :]).then_inc(zl[k % 4].h, 16)
            env.load_groups(sp, g0 + 3)

        @block.tensor
        def _(pe):
            def project(u):
                g, m, (c0, n), dst = units[u]
                w = env.group_here(pe, g0 + g)
                if u >= 2:
                    pe.wait_ge(ev.h, ev.at(u - 1))
                for k in range(KT):
                    mm = pe.matmul(ps[u % 2][:, 0:n], w[:, k, m * P:(m + 1) * P], hT[:, k, c0:c0 + n],
                                   start=(k == 0), stop=(k == KT - 1))
                mm.then_inc(mmd.h, 1)
                if u + 1 == len(units) or units[u + 1][0] != g:
                    pe.wait_ge(mmd.h, mmd.at(u + 1))
                    pe.sem_inc(env.sem("w_used").h, 1)

            def channels(b):
                if b >= 1:
                    pe.wait_ge(a_ev.h, a_ev.at(b))
                    pe.wait_ge(a_ed.h, a_ed.at(b))
                for m in range(2):
                    if b < NB:
                        lhs = uT[:, m, b * P:(b + 1) * P]
                    else:
                        lhs = uT[:, m, S + (b - NB) * P:S + (b - NB + 1) * P]
                    mm = pe.matmul(pa[m][:, 0:3 * P], lhs, ch[:, :], start=True, stop=True)
                mm.then_inc(a_mm.h, 1)

            def first_points(b):
                pe.wait_ge(a_ev.h, a_ev.at(b + 1))
                pe.wait_ge(a_ed.h, a_ed.at(b + 1))
                pe.wait_ge(ml[b % 3].h, ml[b % 3].at(16 * (b // 3 + 1)))
                if b >= 2:
                    pe.wait_ge(b_ev.h, b_ev.at(b - 1))
                pe.matmul(pb[b % 2][:, :], m16[:, b % 3, 0, :], a[:, b % 2, GC:3 * GC], start=True, stop=False)
                pe.matmul(pb[b % 2][:, :], m16[:, b % 3, 1, :], a[:, b % 2, 0:2 * GC], start=False, stop=True).then_inc(b_mm.h, 1)

            half = len(units) // 2
            for u in range(half):
                project(u)
            pe.wait_ge(ev.h, ev.at(half))
            pe.wait_ge(cl.h, cl.at(48))
            channels(0)
            nxt = half
            for b in range(NB):
                if nxt < len(units) and b % 2:
                    project(nxt)
                    nxt += 1
                if b + 1 < NB:
                    channels(b + 1)
                first_points(b)
            for u in range(nxt, len(units)):
                project(u)
            for k in range(NB):
                pe.wait_ge(zl[k % 4].h, zl[k % 4].at(16 * (k // 4 + 1)))
                if k % 4 == 0 and k >= 4:
                    pe.wait_ge(c_ev.h, c_ev.at(2 * (k // 4)))
                for m in range(2):
                    for part in range(2):
                        mm = pe.matmul(pc[m][:, (k % 4) * P:(k % 4 + 1) * P], zt[:, k % 4, part * GC + m * P:part * GC + (m + 1) * P],
                                       m128[:, part, :], start=(part == 0), stop=(part == 1))
                mm.then_inc(c_mm.h, 1)
            if with_ctx:
                pe.wait_ge(c_ev.h, c_ev.at(8))
                for j in range(2):
                    channels(NB + j)
                pe.wait_ge(a_ev.h, a_ev.at(NB + 2))
                pe.wait_ge(a_ed.h, a_ed.at(NB + 2))
                for m in range(2):
                    for j in range(2):
                        for part in range(2):
                            mm = pe.matmul(pc[m][:, 0:CTX], a[:, j, (1 + part) * GC + m * P:(1 + part) * GC + (m + 1) * P],
                                           mctx[:, j, part, :], start=(j == 0 and part == 0), stop=(j == 1 and part == 1))
                mm.then_inc(c_mm.h, 1)

        def ch_view(b, m):
            return a[:, b % 2, :].rearrange("p (s c) -> p s c", s=3)[:, :, m * P:(m + 1) * P]

        @block.scalar
        def _(act):
            def project_out(u):
                g, m, (c0, n), dst = units[u]
                act.wait_ge(mmd.h, mmd.at(u + 1))
                out, src = dst[:, m, c0:c0 + n], ps[u % 2][:, 0:n]
                if g == 0 and c0 < S:
                    out = dst[:, m, 0:S].rearrange("p (b t a) -> p t b a", b=NB, a=8)[:, c0 // P:(c0 + n) // P]
                    src = src.rearrange("p (t b a) -> p t b a", b=NB, a=8)
                act.activation(out, src, ACT.Copy if g == 0 else ACT.Silu).then_inc(ev.h, 1)

            def channels_out(b):
                act.wait_ge(a_mm.h, a_mm.at(b + 1))
                if 2 <= b < NB:
                    act.wait_ge(b_mm.h, b_mm.at(b - 1))
                act.activation(ch_view(b, 0), pa[0][:, 0:3 * P].rearrange("p (s c) -> p s c", s=3), ACT.Copy).then_inc(a_ev.h, 1)

            half = len(units) // 2
            for u in range(half):
                project_out(u)
            nxt = half
            channels_out(0)
            for b in range(NB):
                if nxt < len(units) and b % 2:
                    project_out(nxt)
                    nxt += 1
                if b + 1 < NB:
                    channels_out(b + 1)
                act.wait_ge(b_mm.h, b_mm.at(b + 1))
                if b >= 2:
                    act.wait_ge(zs[b % 2].h, zs[b % 2].at(16 * (b // 2)))
                act.activation(z[:, b % 2, :], pb[b % 2][:, :], ACT.Copy).then_inc(b_ev.h, 1)
            for u in range(nxt, len(units)):
                project_out(u)
            if with_ctx:
                for j in range(2):
                    channels_out(NB + j)

        @block.vector
        def _(dve):
            for b in range(NB):
                dve.wait_ge(a_mm.h, a_mm.at(b + 1))
                if b >= 2:
                    dve.wait_ge(b_mm.h, b_mm.at(b - 1))
                dve.tensor_copy(ch_view(b, 1), pa[1][:, 0:3 * P].rearrange("p (s c) -> p s c", s=3)).then_inc(a_ed.h, 1)
            dve.wait_ge(ev.h, ev.at(len(units)))
            for q in range(NB // 4):
                dve.wait_ge(c_mm.h, c_mm.at(4 * (q + 1)))
                for m in range(2):
                    y = yT[:, m, 0:S].rearrange("p (b a) -> p a b", a=NB)[:, 4 * q:4 * q + 4, :]
                    dve.tensor_tensor(y, y, pc[m][:, :].rearrange("p (a b) -> p a b", b=P), ALU.mult).then_inc(c_ev.h, 1)
            if with_ctx:
                for j in range(2):
                    dve.wait_ge(a_mm.h, a_mm.at(NB + j + 1))
                    dve.tensor_copy(ch_view(NB + j, 1), pa[1][:, 0:3 * P].rearrange("p (s c) -> p s c", s=3)).then_inc(a_ed.h, 1)
                dve.wait_ge(c_mm.h, c_mm.at(NB + 1))
                for m in range(2):
                    dve.tensor_tensor(yT[:, m, S:W], yT[:, m, S:W], pc[m][:, 0:CTX], ALU.mult).then_inc(c_ev.h, 1)
    x = 1 if with_ctx else 0
    for s_, c_ in ((mmd, len(units)), (ev, len(units)), (a_mm, NA), (a_ev, NA), (a_ed, NA), (b_mm, NB), (b_ev, NB),
                   (c_mm, NB + x), (c_ev, 8 + 2 * x), (cl, 48)):
        s_.base += c_
    for i in range(3):
        ml[i].base += 16 * len(range(i, NB, 3))
    for i in range(2):
        zs[i].base += 16 * NB // 2
    for i in range(4):
        zl[i].base += 16 * NB // 4
    env.next_group += 2


def stage_conv(env, layer, hT, yT, with_ctx):
    nc = env.nc
    g0 = env.next_group
    chunks = CHUNKS if with_ctx else CHUNKS[:-1]
    order = ("cc", "cv", "cb", "cz")
    units = [(g, m, c) for g in range(4) for m in range(2) for c in chunks]
    N = 2 * len(chunks)
    mmd, ea, ed, gt, cv = env.sem("proj_mm"), env.sem("conv_out_act"), env.sem("conv_out_dve"), env.sem("conv_gated"), env.sem("conv_done")
    UW = W + 4
    pos = lambda c: c + 1 if c < S else c + 3
    w3 = env.cols("conv_w_2", 12)
    with ExitStack() as ctx:
        u_ = env.sb(ctx, "cc_cv", [P, 2, UW])
        zb = env.sb(ctx, "cz_silu", [P, 2, CH])
        ps = env.banks(ctx, "ps_in", 4)
        block = ctx.enter_context(nc.Block())

        @block.sync
        def _(sp):
            env.load_groups(sp, g0 + 4)

        @block.tensor
        def _(pe):
            for u, (g, m, (c0, n)) in enumerate(units):
                w = env.group_here(pe, g0 + g)
                if u >= 4:
                    v = u - 4
                    e = ea if v // N in (0, 3) else ed
                    pe.wait_ge(e.h, e.at(v % N + 1 + (N if v // N >= 2 else 0)))
                for k in range(KT):
                    mm = pe.matmul(ps[u % 4][:, 0:n], w[:, k, m * P:(m + 1) * P], hT[:, k, c0:c0 + n],
                                   start=(k == 0), stop=(k == KT - 1))
                mm.then_inc(mmd.h, 1)
                if u + 1 == len(units) or units[u + 1][0] != g:
                    pe.wait_ge(mmd.h, mmd.at(u + 1))
                    pe.sem_inc(env.sem("w_used").h, 1)

        @block.scalar
        def _(act):
            for i in range(N):
                g, m, (c0, n) = units[i]
                act.wait_ge(mmd.h, mmd.at(i + 1))
                act.activation(u_[:, m, pos(c0):pos(c0) + n], ps[i % 4][:, 0:n], ACT.Copy).then_inc(ea.h, 1)
            for i in range(N):
                u = 3 * N + i
                g, m, (c0, n) = units[u]
                act.wait_ge(mmd.h, mmd.at(u + 1))
                if i >= 2:
                    act.wait_ge(gt.h, gt.at(i - 1))
                act.activation(zb[:, i % 2, 0:n], ps[u % 4][:, 0:n], ACT.Silu).then_inc(ea.h, 1)

        @block.gpsimd
        def _(pool):
            for i in range(N):
                g, m, (c0, n) = units[i]
                pool.wait_ge(ea.h, ea.at(N + i + 1))
                pool.wait_ge(ed.h, ed.at(N + i + 1))
                y = yT[:, m, c0:c0 + n]
                pool.tensor_tensor(y, y, zb[:, i % 2, 0:n], ALU.mult).then_inc(gt.h, 1)

        @block.vector
        def _(dve):
            link = Link(dve, env.sem("dve_chain"))
            for m in range(2):
                for edge in (0, S + 1, S + 2, UW - 1):
                    ins = dve.memset(u_[:, m, edge:edge + 1], 0.0)
            link(ins)
            for i in range(N):
                g, m, (c0, n) = units[i]
                dve.wait_ge(ea.h, ea.at(i + 1))
                dve.wait_ge(mmd.h, mmd.at(N + i + 1))
                uu = u_[:, m, pos(c0):pos(c0) + n]
                dve.tensor_tensor(uu, uu, ps[(N + i) % 4][:, 0:n], ALU.mult).then_inc(ed.h, 1)
            dve.wait_ge(ed.h, ed.at(N))
            for m in range(2):
                for c0, n in ([(0, S), (S, CTX)] if with_ctx else [(0, S)]):
                    y = yT[:, m, c0:c0 + n]
                    p0 = pos(c0) - 1
                    wc = lambda k: w3[:, (layer * 3 + k) * 2 + m:(layer * 3 + k) * 2 + m + 1]
                    link(dve.tensor_scalar(y, u_[:, m, p0:p0 + n], wc(0), None, ALU.mult))
                    for k in (1, 2):
                        link(dve.scalar_tensor_tensor(out=y, in0=u_[:, m, p0 + k:p0 + k + n], scalar=wc(k), in1=y,
                                                      op0=ALU.mult, op1=ALU.add))
            for i in range(N):
                g, m, (c0, n) = units[i]
                dve.wait_ge(mmd.h, mmd.at(2 * N + i + 1))
                y = yT[:, m, c0:c0 + n]
                dve.tensor_tensor(y, y, ps[(2 * N + i) % 4][:, 0:n], ALU.mult).then_inc(ed.h, 1)
            link.close()
    for s_, c_ in ((mmd, 4 * N), (ea, 2 * N), (ed, 2 * N), (gt, N)):
        s_.base += c_
    env.next_group += 4


def stage_output2(env, wo, yT, w_ap, pieces, final):
    nc, A = env.nc, env.A
    tiles = [(src, dst, t, col0 + t * P, gi) for gi, (src, dst, n, col0, _) in enumerate(pieces) for t in range(n)]
    NTI = len(tiles)
    wl, gl = env.sem("wo_loaded2"), env.sem("gate_loaded")
    xl = [env.sem(f"o2_x{i}") for i in range(2)]
    hs = [env.sem(f"o2_stored{i}") for i in range(2)]
    mmd, gd, ad, sq, ms, pw, fn = (env.sem(n) for n in ("out_mm", "out_gated", "out_added", "fin_sq", "fin_mean", "fin_rstd", "fin_done"))
    last = fn if final else ad
    with ExitStack() as ctx:
        g_ = env.sb(ctx, "gates", [P, len(pieces), D])
        x = env.sb(ctx, "x_res", [P, 2, D])
        t_ = env.sb(ctx, "gated", [P, D])
        junk = env.sb(ctx, "junk", [P, D]) if final else None
        fg = env.sb(ctx, "final_gain", [P, D]) if final else None
        st = env.sb(ctx, "fin_stat", [P, 3, NTI])
        ps = [env.banks(ctx, f"ps_o{i}", 2) for i in range(2)]
        block = ctx.enter_context(nc.Block())

        @block.sync
        def _(sp):
            sp.dma_start(wo[:, :, :], w_ap.rearrange("(k p) c -> p k c", p=P)).then_inc(wl.h, 16)
            for i, (_, _, _, _, gd_) in enumerate(pieces):
                sp.dma_start(g_[:, i, :], gd_.to_broadcast([P, D])).then_inc(gl.h, 16)
            if final:
                sp.dma_start(fg[:, :], A["final_g_2"].rearrange("(a d) -> a d", a=1).to_broadcast([P, D])).then_inc(gl.h, 16)
            env.load_groups(sp, env.next_group + 2)
            for i in range(NTI + 1):
                if i < NTI:
                    src, dst, t, col, gi = tiles[i]
                    if i >= 2:
                        sp.wait_ge(hs[i % 2].h, hs[i % 2].at(16 * (i // 2)))
                    sp.dma_start(x[:, i % 2, :], src[t * P:(t + 1) * P, :]).then_inc(xl[i % 2].h, 16)
                if i >= 1:
                    v = i - 1
                    src, dst, t, col, gi = tiles[v]
                    sp.wait_ge(last.h, last.at(v + 1))
                    sp.dma_start(dst[t * P:(t + 1) * P, :], x[:, v % 2, :]).then_inc(hs[v % 2].h, 16)
            for i in range(2):
                sp.wait_ge(hs[i].h, hs[i].at(16 * len(range(i, NTI, 2))))

        @block.tensor
        def _(pe):
            pe.wait_ge(wl.h, wl.at(16))
            for i, (src, dst, t, col, gi) in enumerate(tiles):
                if i >= 2:
                    pe.wait_ge(gd.h, gd.at(i - 1))
                for half in range(2):
                    for k in range(KT):
                        mm = pe.matmul(ps[i % 2][half][:, :], yT[:, k, col:col + P], wo[:, k, half * CH:(half + 1) * CH],
                                       start=(k == 0), stop=(k == KT - 1))
                mm.then_inc(mmd.h, 1)

        @block.vector
        def _(dve):
            link = Link(dve, env.sem("dve_chain"))
            dve.wait_ge(gl.h, gl.at(16 * (len(pieces) + (1 if final else 0))))
            for i, (src, dst, t, col, gi) in enumerate(tiles):
                dve.wait_ge(mmd.h, mmd.at(i + 1))
                if i >= 1:
                    dve.wait_ge(ad.h, ad.at(i))
                for half in range(2):
                    sl = slice(half * CH, (half + 1) * CH)
                    ins = dve.tensor_tensor(t_[:, sl], ps[i % 2][half][:, :], g_[:, gi, sl], ALU.mult)
                ins.then_inc(gd.h, 1)
                dve.wait_ge(gd.h, gd.at(i + 1))
                dve.wait_ge(xl[i % 2].h, xl[i % 2].at(16 * (i // 2 + 1)))
                dve.tensor_tensor(x[:, i % 2, :], x[:, i % 2, :], t_[:, :], ALU.add).then_inc(ad.h, 1)
                if final:
                    dve.wait_ge(sq.h, sq.at(i + 1))
                    dve.tensor_scalar(st[:, 1, i:i + 1], st[:, 0, i:i + 1], 1.0 / D, EPS, ALU.mult, ALU.add).then_inc(ms.h, 1)
                    dve.wait_ge(pw.h, pw.at(i + 1))
                    dve.scalar_tensor_tensor(out=x[:, i % 2, :], in0=x[:, i % 2, :], scalar=st[:, 2, i:i + 1], in1=fg[:, :],
                                             op0=ALU.mult, op1=ALU.mult).then_inc(fn.h, 1)
            link.close()

        if final:
            @block.scalar
            def _(act):
                for i in range(NTI):
                    act.wait_ge(ad.h, ad.at(i + 1))
                    if i >= 1:
                        act.wait_ge(sq.h, sq.at(i))
                    act.activation(junk[:, :], x[:, i % 2, :], ACT.Square, accum_out=st[:, 0, i:i + 1]).then_inc(sq.h, 1)

            @block.gpsimd
            def _(pool):
                for i in range(NTI):
                    pool.wait_ge(ms.h, ms.at(i + 1))
                    pool.tensor_tensor(st[:, 2, i:i + 1], st[:, 1, i:i + 1], env.mhalf[:, :], ALU.pow).then_inc(pw.h, 1)
    f = NTI if final else 0
    for s_, c_ in ((wl, 16), (gl, 16 * (len(pieces) + (1 if final else 0))), (mmd, NTI), (gd, NTI), (ad, NTI), (sq, f), (ms, f),
                   (pw, f), (fn, f)):
        s_.base += c_
    for i in range(2):
        n = 16 * len(range(i, NTI, 2))
        xl[i].base += n
        hs[i].base += n


def stage_store_gates(env, gates, rows):
    done = env.sem("gate_stored")
    with ExitStack() as ctx:
        block = ctx.enter_context(env.nc.Block())

        @block.sync
        def _(sp):
            for g, r in zip(gates, rows):
                sp.dma_start(r, g[0:1, :]).then_inc(done.h, 16)
            sp.wait_ge(done.h, done.at(16 * len(gates)))
    done.base += 16 * len(gates)


def stage_gqa(env, layer, hT, QT, KTt, VN, aT, qtiles, zchunks):
    stage_qkv2(env, layer, hT, QT, KTt, VN, aT, qtiles, zchunks)
    stage_attend(env, QT, KTt, VN, aT, qtiles)


def program(nc, A, upto=99, layers=(0, 1), skip1=False):
    env = Env(nc, A)
    env.next_group = 0
    with env.stack:
        top = env.stack
        env.cols = lambda key, n: env.vcols[:, env.place[key][0], env.place[key][1]:env.place[key][1] + n]
        env.ident = env.sb(top, "ident", [P, P])
        env.vcols = env.sb(top, "vcols", [P, 2, P])
        env.ones = env.sb(top, "ones", [P, P])
        env.mhalf = env.sb(top, "minus_half", [P, 1])
        env.mask1 = env.sb(top, "mask1", [P, 2 * P])
        env.levmask = env.sb(top, "level_masks", [P, 16, P], mybir.dt.uint8)
        env.headmean = env.sb(top, "head_mean", [P, P])
        env.eps = env.sb(top, "eps", [P, 1])
        env.lb = env.sb(top, "lower_bounds", [P, 3, 2, 2])
        env.invf = env.sb(top, "inv_freq", [P, 32])
        env.sp = env.sb(top, "softplus", [P, 5, 4])
        env.nsp = env.sb(top, "decay_scale", [P, 4])
        env.csilu = env.sb(top, "c_silu", [P, 24])
        env.wring = env.sb(top, "weight_ring", [P, 2, KT, GC])
        env.mods = {t: env.sb(top, f"mod_{t}", [P, 2, 2, KT]) for t in ("one", "l0", "l1")}
        v_d = nc.dram_tensor("v_rows", [S, H1 * HD], F32, kind="Internal").ap()
        gb_d = nc.dram_tensor("gb_rows", [S, H1 * HD], F32, kind="Internal").ap()
        res_d = [nc.dram_tensor(f"res{p}", [S, RW], F32, kind="Internal").ap() for p in range(3)]
        h_d = A["out"] if upto == 1 else nc.dram_tensor("h_rows", [S, D], F32, kind="Internal").ap()
        env.groups += [(A["w_ada"][0], g * GC) for g in range(12)]
        env.groups += [(A["w_in"][0], c) for c in (0, 512, 256, 768, 2048, 2304, 2560, 2816, 1024, 1280, 1536, 1792)]
        for l in layers:
            env.groups += [(A["w_mod_2"][l], g * GC) for g in range(12)]
            env.groups += [(A["w_in_2"][l], c) for c in (1792, 2560, 2816, 2048, 2304, 1024, 1280, 1536, 3072, 3328, 256, 512, 0, 768)]
        with ExitStack() as one:
            gate = env.sb(one, "gate1", [P, D])
            yaT = env.sb(one, "ya_t", [P, CT, S])
            sumsq = env.sb(one, "ya_sumsq", [P, NT])
            with ExitStack() as pr:
                hT = env.sb(pr, "h_t", [P, KT, S])
                with ExitStack() as tables:
                    env.cosF = env.sb(tables, "cos", [P, NT, 2, 32])
                    env.sinF = env.sb(tables, "sin", [P, NT, 2, 32])
                    stage_vectors(env)
                    stage_mod(env, "one", A["w_ada"][0], ("b_ada", 0, A["b_ada"][:, 2 * D:]), "norm_pre", 0, [0], [gate],
                              A["norm_post"])
                    m = env.mods["one"]
                    stage_norm(env, hT, [(A["x"][0], NT, 0, (m[:, 0, 0, :], m[:, 0, 1, :]))])
                    stage_recurrent(env, hT, yaT, sumsq)
                    with ExitStack() as qk:
                        QT = env.sb(qk, "q_t", [P, 4, S])
                        KTt = env.sb(qk, "k_t", [P, 4, S])
                        stage_qkvg(env, hT, QT, KTt, v_d, gb_d)
                        stage_dilated(env, hT, QT, KTt, v_d, res_d)
            stage_output1(env, yaT, sumsq, res_d, gb_d, gate, h_d)
        if upto == 1:
            return
        env.retire("xa_out", "ga_out", "conv_done", "gate_mm", "gate_act", "xa_mm", "ga_mm", "decay_done", "decay_sq",
                   "root_done", "gated_in", "score_mm", "score_min", "prob_exp", "prob_turned",
                   "prob_copied_act", "prob_copied_dve", "pv_mm", "pv_copied")
        gate_d = [[nc.dram_tensor(f"gate{l}{v}", [1, D], F32, kind="Internal").ap() for v in range(2)] for l in range(2)]
        zt_d = nc.dram_tensor("t2_rows", [P, 16, 2 * GC], F32, kind="Internal").ap()
        h1_d = nc.dram_tensor("h1_rows", [S, D], F32, kind="Internal").ap()
        c1_d = nc.dram_tensor("c1_rows", [CTX, D], F32, kind="Internal").ap()
        rows = [(h_d, A["ctx_2"][0]), (h1_d, c1_d)]
        for l in layers:
            tag = f"l{l}"
            h_in, c_in = rows[l]
            with ExitStack() as lay:
                hT = env.sb(lay, "h_t", [P, KT, W])
                with ExitStack() as md:
                    gates = [env.sb(md, f"gate_rows{v}", [P, D]) for v in range(2)]
                    stage_mod(env, tag, A["w_mod_2"][l], ("b_mod_2", 24 * l, A["b_mod_2"][l:l + 1, 2 * D:]), "norm_g_2", 8 * l,
                              [1, 2], gates, None)
                    stage_store_gates(env, gates, gate_d[l])
                m = env.mods[tag]
                stage_norm(env, hT, [(h_in, NT, 0, (m[:, 0, 0, :], m[:, 0, 1, :])),
                                     (c_in, CTX // P, S, (m[:, 1, 0, :], m[:, 1, 1, :]))])
                yT = env.sb(lay, "y_t", [P, KT, W])
                with_ctx = l == 0
                chunks = CHUNKS if with_ctx else CHUNKS[:-1]
                qtiles = WT if with_ctx else NT
                vN = yT[:, 2:4, :].rearrange("p a (t c) -> p (a t) c", c=GC)
                stage_hgrn_in(env, hT, yT[:, 0:2, :], vN, yT[:, 6:8, :], chunks)
                for d in range(2):
                    stage_hgrn_scan(env, l, d, hT, yT[:, 0:2, :], vN, yT[:, 4:6, :], with_ctx)
                stage_hgrn_norm(env, l, yT[:, 4:6, :], yT[:, 6:8, :], chunks)
                stage_gqa(env, l, hT, yT[:, 0:2, :], yT[:, 6, :], yT[:, 7, :].rearrange("p (t c) -> p t c", c=P),
                          yT[:, 2:4, :], qtiles, chunks)
                stage_fourier(env, hT, yT[:, 0:2, :], yT[:, 6:8, :], with_ctx, zt_d)
                stage_conv(env, l, hT, yT[:, 0:2, :], with_ctx)
                wo = hT[:, :, 0:D]
                pieces = [(h_in, A["out"] if l == 1 else h1_d, NT, 0, gate_d[l][0])]
                if with_ctx:
                    pieces.append((c_in, c1_d, CTX // P, S, gate_d[l][1]))
                stage_output2(env, wo, yT, A["w_out_2"][l], pieces, final=l == 1)


def constants():
    i = np.arange(P)
    ident = np.eye(P, dtype=np.float32)
    mask1 = np.zeros((P, 2 * P), np.float32)
    mask1[:, :P][i[None, :] < i[:, None]] = BIG
    mask1[:, P:][i[None, :] > i[:, None]] = BIG
    invf = (np.float32(10000.0) ** (-np.arange(32, dtype=np.float32) / np.float32(32))).astype(np.float32)[None]
    lev = np.zeros((P, 16, P), np.float32)
    for l in range(7):
        same = (i[:, None] >> (l + 1)) == (i[None, :] >> (l + 1))
        kb, qb = (i[:, None] >> l) & 1, (i[None, :] >> l) & 1
        lev[:, l, :] = same & (kb == 0) & (qb == 1)
        lev[:, 8 + l, :] = same & (kb == 1) & (qb == 0)
    lev[:, 7, :] = lev[:, 15, :] = np.eye(P)
    headmean = np.kron(np.eye(2), np.full((HD, HD), 1.0 / HD)).astype(np.float32)
    tok = np.arange(S)
    fr = (np.float32(10000.0) ** (-np.arange(16, dtype=np.float32) / np.float32(16))).astype(np.float32)
    ang = np.concatenate([(tok // 64).astype(np.float32)[:, None] * fr, (tok % 64).astype(np.float32)[:, None] * fr], -1)
    axial = np.stack([np.cos(ang.astype(np.float64)), np.sin(ang.astype(np.float64))], 0).astype(np.float32)
    axial = np.ascontiguousarray(axial.reshape(2, NT, P, 32).transpose(2, 0, 1, 3))
    c64 = 2 * np.pi * np.outer(np.arange(HD), np.arange(HD)) / HD
    two = lambda m: np.kron(np.eye(2), m)
    dft_ch = np.concatenate([two(np.sin(c64)), two(np.cos(c64)), two(-np.sin(c64))], 1).astype(np.float32)
    dft_16 = np.zeros((16, P, 2, P))
    t1, a, k1 = np.arange(16)[:, None], np.arange(8), np.arange(16)[None, :]
    for b in range(16):
        for aa in a:
            th = 2 * np.pi * (t1 * k1 / 16 + (8 * b + aa) * k1 / S)
            dft_16[b][np.ix_(t1[:, 0] * 8 + aa, [0], aa * 16 + k1[0])] = np.cos(th)[:, None, :]
            dft_16[b][np.ix_(t1[:, 0] * 8 + aa, [1], aa * 16 + k1[0])] = -np.sin(th)[:, None, :]
    scale = 1 / np.sqrt(S * HD)
    ph = 2 * np.pi * np.outer(i, i) / P
    dft_128 = np.stack([np.cos(ph), np.sin(ph)], 1) * scale
    tc = np.arange(CTX)
    pc = 2 * np.pi * np.outer(tc, tc) / CTX
    dft_ctx = (np.stack([np.cos(pc), np.sin(pc)], 1) / np.sqrt(CTX * HD)).reshape(2, P, 2, CTX).transpose(1, 0, 2, 3)
    f = lambda x: np.ascontiguousarray(x, dtype=np.float32)
    return {"k_ident": ident, "k_mask1": mask1, "k_invf": invf, "k_levmask": lev, "k_headmean": headmean, "k_axial": axial,
            "k_dft_ch": f(dft_ch), "k_dft_16": f(dft_16), "k_dft_128": f(dft_128), "k_dft_ctx": f(dft_ctx)}


INPUTS = ["x", "c", "positions", "w_ada", "b_ada", "norm_pre", "norm_post", "w_in", "conv_w", "conv_b", "w_rg_a", "b_rg_a",
          "w_rg_x", "b_rg_x", "lru_lambda", "norm_rec", "norm_att", "w_out", "c_2", "ctx_2", "c_ctx_2", "norm_g_2",
          "w_mod_2", "b_mod_2", "w_in_2", "conv_w_2", "q_norm_g_2", "k_norm_g_2", "hgrn_lb_2", "hgrn_norm_g_2",
          "w_out_2", "final_g_2"]


def kernel(**inputs):
    import concourse.bacc as bacc
    from concourse.bass_utils import run_bass_kernel_spmd as _run

    nc = bacc.Bacc("TRN2", target_bir_lowering=False, num_devices=1)
    given = {name: inputs[name] for name in INPUTS}
    given.update(constants())
    arrays, A = {}, {}
    for name, value in given.items():
        a = np.ascontiguousarray(value)
        arrays[f"in_{name}_dram"] = a
        A[name] = nc.dram_tensor(f"in_{name}_dram", a.shape, mybir.dt.from_np(a.dtype), kind="ExternalInput").ap()
    A["out"] = nc.dram_tensor("out_dram", (S, D), F32, kind="ExternalOutput").ap()
    program(nc, A)
    r = _run(nc, [arrays], core_ids=[0])
    return r.results[0]["out_dram"].reshape(1, S, D)
```

```python
from contextlib import ExitStack, contextmanager

import numpy as np
import concourse.bass as bass
from concourse import mybir

F32 = mybir.dt.float32
F32R = mybir.dt.float32r
I32 = mybir.dt.int32
ALU = mybir.AluOpType
ACT = mybir.ActivationFunctionType
AXX = mybir.AxisListType.X

P = 128
D = 1024
S = 2048
KT = D // P
NT = S // P
CH = 512
GC = 256
EPS = 1e-6
BIG = 1e30
DREC = 512
CT = DREC // P
H1 = 8
HD = 64
PATTERNS = ((128, 1), (512, 4), (2048, 16))
RW = H1 * HD + 2 * H1


class Sem:

    def __init__(self, handle):
        self.h, self.base = handle, 0

    def at(self, n):
        return self.base + n


class Env:

    def __init__(self, nc, A):
        self.nc, self.A = nc, A
        self.sems = {}
        self.stack = ExitStack()
        self.groups = []
        self.loaded = 0
        self.n_names = 0
        self.free = []
        self.made = 0

    def sem(self, name):
        if name not in self.sems:
            if self.free:
                self.sems[name] = self.free.pop()
            else:
                self.made += 1
                self.sems[name] = Sem(self.stack.enter_context(self.nc.semaphore(f"{name}_{self.made}")))
        return self.sems[name]

    def retire(self, *names):
        self.free += [self.sems.pop(n) for n in names]

    def sb(self, ctx, name, shape, dt=F32):
        self.n_names += 1
        return ctx.enter_context(self.nc.sbuf_tensor(f"{name}_{self.n_names}", shape, dt))

    def banks(self, ctx, name, n):
        self.n_names += 1
        return [ctx.enter_context(self.nc.psum_tensor(f"{name}{i}_{self.n_names}", [P, CH], F32)) for i in range(n)]

    def load_groups(self, eng, upto):
        for g in range(self.loaded, min(upto, len(self.groups))):
            if g >= 2:
                eng.wait_ge(self.sem("w_used").h, g - 1)
            ap, c0 = self.groups[g]
            eng.dma_start(self.wring[:, g % 2, :, :],
                          ap[:, c0:c0 + GC].rearrange("(k p) c -> p k c", p=P)).then_inc(self.sem(f"w_loaded{g % 2}").h, 16)
        self.loaded = max(self.loaded, min(upto, len(self.groups)))

    def group_here(self, eng, g):
        eng.wait_ge(self.sem(f"w_loaded{g % 2}").h, 16 * (g // 2 + 1))
        return self.wring[:, g % 2, :, :]


class Link:

    def __init__(self, eng, sem):
        self.eng, self.sem, self.n = eng, sem, 0

    def __call__(self, ins):
        self.n += 1
        ins.then_inc(self.sem.h, 1)
        self.eng.wait_ge(self.sem.h, self.sem.at(self.n))

    def close(self):
        self.sem.base += self.n


def stage_vectors(env, slots):
    nc, A = env.nc, env.A
    rows = [
        ("c", A["c"], 8), ("c_2", A["c_2"], 8), ("c_ctx_2", A["c_ctx_2"], 8), ("norm_pre", A["norm_pre"], 8),
        ("norm_g_2", A["norm_g_2"], 16), ("conv_b", A["conv_b"], 4), ("b_rg_a", A["b_rg_a"], 4), ("b_rg_x", A["b_rg_x"], 4),
        ("lru_lambda", A["lru_lambda"], 4), ("conv_w", A["conv_w"], 16), ("norm_rec", A["norm_rec"], 4),
        ("norm_att", A["norm_att"], 4), ("b_ada", A["b_ada"], 24),
        ("b_mod_2", A["b_mod_2"], 48), ("conv_w_2", A["conv_w_2"], 12), ("hgrn_lb_2", A["hgrn_lb_2"], 8),
        ("hgrn_norm_g_2", A["hgrn_norm_g_2"], 4),
    ]
    place, tile, at = {}, 0, 0
    for name, _, n in rows:
        if at + n > P:
            tile, at = tile + 1, 0
        place[name] = (tile, at)
        at += n
    used = [max((p[1] + n) for (name, _, n), p in ((r, place[r[0]]) for r in rows) if p[0] == t) for t in range(tile + 1)]
    env.place = place
    nt = tile + 1
    assert nt == 2

    ld, tr, ev = env.sem("vec_loaded"), env.sem("vec_turned"), env.sem("vec_copied")
    with ExitStack() as ctx:
        vr = env.sb(ctx, "vrows", [P, nt, P])
        posi = env.sb(ctx, "pos_int", [NT, P], I32)
        posf = env.sb(ctx, "pos_rows", [NT, P])
        ang = env.sb(ctx, "angle", [P, NT, 32])
        nn = env.sb(ctx, "turns", [P, NT, 32])
        t1 = env.sb(ctx, "rest", [P, NT, 32])
        pc = env.sb(ctx, "pos_cols", [P, NT])
        levm = env.sb(ctx, "level_masks_in", [P, 16, P])
        ps, ps2 = env.banks(ctx, "ps_vec", 2)
        block = ctx.enter_context(nc.Block())
        consts = [(env.ident, A["k_ident"]), (env.mask1, A["k_mask1"]), (env.invf, A["k_invf"].to_broadcast([P, 32])),
                  (levm, A["k_levmask"]), (env.headmean, A["k_headmean"])]

        @block.sync
        def _(sp):
            for name, ap, n in rows:
                t, r = place[name]
                names = "abcd"[:len(ap.shape)]
                flat = ap if len(ap.shape) == 1 else ap.rearrange(f"{' '.join(names)} -> ({' '.join(names)})")
                sp.dma_start(vr[r:r + n, t, :], flat.rearrange("(r c) -> r c", c=P)).then_inc(ld.h, 16)
            sp.dma_start(posi[:, :], A["positions"].rearrange("a (t p) -> (a t) p", p=P)).then_inc(ld.h, 16)
            for dst, src in consts:
                sp.dma_start(dst[(slice(None),) * len(dst.shape)], src).then_inc(ld.h, 16)
            load_mod_groups(env, sp, 0, slots)

        n_ld = 16 * (len(rows) + 1 + len(consts))

        @block.tensor
        def _(pe):
            pe.wait_ge(ld.h, n_ld)
            for t in range(nt):
                mm = pe.transpose(ps[:, t * P:t * P + used[t]], vr[0:used[t], t, :], env.ident[0:used[t], 0:used[t]])
            mm.then_inc(tr.h, 1)
            pe.wait_ge(env.sem("pos_float").h, 1)
            pe.transpose(ps2[:, 0:NT], posf[:, :], env.ident[0:NT, 0:NT]).then_inc(tr.h, 1)

        @block.vector
        def _(dve):
            link = Link(dve, env.sem("dve_chain"))
            dve.memset(env.mhalf[:, :], -0.5)
            dve.memset(env.ones[:, :], 1.0).then_inc(env.sem("ones_set").h, 1)
            dve.wait_ge(ld.h, n_ld)
            dve.tensor_copy(env.levmask[:, :, :], levm[:, :, :])
            dve.tensor_copy(posf[:, :], posi[:, :]).then_inc(env.sem("pos_float").h, 1)
            dve.wait_ge(tr.h, 1)
            for t in range(nt):
                ins = dve.tensor_copy(env.vcols[:, t, 0:used[t]], ps[:, t * P:t * P + used[t]])
            ins.then_inc(ev.h, 1)
            dve.memset(env.eps[:, :], EPS)
            dve.wait_ge(ev.h, 1)
            lbc = env.cols("hgrn_lb_2", 8).rearrange("p (d l m) -> p d l m", d=2, l=2)
            dve.tensor_tensor(env.lb[:, 2, :, :], lbc[:, :, 1, :], lbc[:, :, 0, :], ALU.subtract).then_inc(env.sem("lb_diff").h, 1)
            dve.wait_ge(tr.h, 2)
            link(dve.tensor_copy(pc[:, :], ps2[:, 0:NT]))
            link(dve.tensor_tensor(ang[:, :, :], pc[:, :, None].to_broadcast([P, NT, 32]),
                                   env.invf[:, None, :].to_broadcast([P, NT, 32]), ALU.mult))
            link(dve.tensor_scalar(nn[:, :, :], ang[:, :, :], 1.0 / (2 * np.pi), MAGIC, ALU.mult, ALU.add))
            link(dve.tensor_scalar(nn[:, :, :], nn[:, :, :], -MAGIC, None, ALU.add))
            for part in TWO_PI_PARTS:
                link(dve.scalar_tensor_tensor(out=ang[:, :, :], in0=nn[:, :, :], scalar=-part, in1=ang[:, :, :],
                                              op0=ALU.mult, op1=ALU.add))
            link(dve.tensor_scalar(ang[:, :, :], ang[:, :, :], PI_F, -PI_F, ALU.min, ALU.max))
            link(dve.tensor_scalar(t1[:, :, :], ang[:, :, :], -1.0, None, ALU.mult))
            link(dve.tensor_tensor(t1[:, :, :], t1[:, :, :], ang[:, :, :], ALU.max))
            dve.tensor_scalar(t1[:, :, :], t1[:, :, :], -1.0, PI_F / 2, ALU.mult, ALU.add).then_inc(env.sem("angle_ready").h, 1)
            dve.wait_ge(env.sem("sines").h, 2)
            for half in range(2):
                dve.tensor_copy(env.cosF[:, :, half, :], t1[:, :, :])
            link(dve.tensor_scalar(env.sinF[:, :, 0, :], ang[:, :, :], -1.0, None, ALU.mult))
            link(dve.tensor_copy(env.sinF[:, :, 1, :], ang[:, :, :]))
            dve.wait_ge(env.sem("lam_exp").h, 1)
            e, z, z2, acc = env.sp[:, 0, :], env.sp[:, 1, :], env.sp[:, 2, :], env.sp[:, 3, :]
            lam = env.cols("lru_lambda", 4)
            link(dve.tensor_scalar(z, e, 2.0, None, ALU.add))
            link(dve.reciprocal(z, z))
            link(dve.tensor_tensor(z, z, e, ALU.mult))
            link(dve.tensor_tensor(z2, z, z, ALU.mult))
            link(dve.memset(acc, 1.0 / 21))
            for n in range(19, 0, -2):
                link(dve.tensor_tensor(acc, acc, z2, ALU.mult))
                link(dve.tensor_scalar(acc, acc, 1.0 / n, None, ALU.add))
            link(dve.tensor_tensor(acc, acc, z, ALU.mult))
            link(dve.tensor_scalar(z, lam, -1.0, 0.0, ALU.mult, ALU.max))
            link(dve.scalar_tensor_tensor(out=acc, in0=acc, scalar=2.0, in1=z, op0=ALU.mult, op1=ALU.add))
            link(dve.tensor_scalar(env.nsp[:, :], acc, -8.0, None, ALU.mult))
            link.close()

        @block.scalar
        def _(act):
            load_mod_groups(env, act, 1, slots)
            act.wait_ge(ev.h, 1)
            act.activation(env.csilu[:, :], env.vcols[:, place["c"][0], 0:24], ACT.Silu).then_inc(env.sem("csilu").h, 1)
            lam = env.cols("lru_lambda", 4)
            act.activation(env.sp[:, 4, :], lam, ACT.Abs).then_inc(env.sem("act_chain").h, 1)
            act.wait_ge(env.sem("act_chain").h, 1)
            act.activation(env.sp[:, 0, :], env.sp[:, 4, :], ACT.Exp, scale=-1.0).then_inc(env.sem("lam_exp").h, 1)
            act.wait_ge(env.sem("lb_diff").h, 1)
            act.activation(env.lb[:, 0, :, :], env.lb[:, 2, :, :], ACT.Sigmoid).then_inc(env.sem("lb_done").h, 1)
            act.activation(env.lb[:, 1, :, :], env.lb[:, 2, :, :], ACT.Sigmoid, scale=-1.0).then_inc(env.sem("lb_done").h, 1)
            act.wait_ge(env.sem("angle_ready").h, 1)
            act.activation(t1[:, :, :], t1[:, :, :], ACT.Sin).then_inc(env.sem("sines").h, 1)
            act.activation(ang[:, :, :], ang[:, :, :], ACT.Sin).then_inc(env.sem("sines").h, 1)
        env.sem("act_chain").base += 1


MAGIC = 12582912.0
PI_F = 3.1415925
TWO_PI_PARTS = (6.28125, float(np.float32(0.0019350051879882812)), float(2 * np.pi - 6.28125 - 0.0019350051879882812))


MC = 512
MG = 3 * D // MC


def load_mod_groups(env, eng, half, slots):
    ks = slice(half * KT // 2, (half + 1) * KT // 2)
    for g in range(MG):
        eng.dma_start(slots[g][:, ks, :], env.A["w_ada"][0][:, g * MC:(g + 1) * MC].rearrange("(k p) c -> p k c", p=P)[:, ks, :])\
           .then_inc(env.sem(f"mod_w{g}").h, 16)


def stage_mod(env, slots, gate):
    nc, A = env.nc, env.A
    used, rc, bd, tn = env.sem("mod_w_used"), env.sem("mod_row"), env.sem("gate_row"), env.sem("mod_turned")
    with ExitStack() as ctx:
        row = env.sb(ctx, "mod_rows", [1, 4, MC])
        brow = env.sb(ctx, "gate_bias", [P, D])
        mul = env.sb(ctx, "gate_gain", [P, D])
        tmp = env.sb(ctx, "mod_tmp", [P, 16])
        ps = env.banks(ctx, "ps_mod", MG)
        pt = env.banks(ctx, "ps_cols", 1)[0]
        block = ctx.enter_context(nc.Block())

        @block.sync
        def _(sp):
            sp.dma_start(brow[:, :], A["b_ada"][:, 2 * D:].to_broadcast([P, D])).then_inc(bd.h, 16)
            sp.dma_start(mul[:, :], A["norm_post"].to_broadcast([P, D])).then_inc(bd.h, 16)
            env.load_groups(sp, env.next_group + 2)

        @block.tensor
        def _(pe):
            def turn(g):
                pe.wait_ge(rc.h, g + 1)
                for m in range(4):
                    mm = pe.transpose(pt[:, 4 * g + m:4 * g + m + 1], row[:, g, m * P:(m + 1) * P], env.ident[0:1, 0:1])
                mm.then_inc(tn.h, 1)

            pe.wait_ge(env.sem("csilu").h, 1)
            for g in range(MG):
                pe.wait_ge(env.sem(f"mod_w{g}").h, 32)
                for k in range(KT):
                    mm = pe.matmul(ps[g][:, :], env.csilu[:, k:k + 1].to_broadcast([P, P]), slots[g][:, k, :],
                                   start=(k == 0), stop=(k == KT - 1))
                mm.then_inc(used.h, 1)
                if 1 <= g <= 4:
                    turn(g - 1)

        @block.scalar
        def _(act):
            for g in range(4):
                act.wait_ge(used.h, g + 1)
                act.activation(row[:, g, :], ps[g][0:1, :], ACT.Copy).then_inc(rc.h, 1)

        @block.vector
        def _(dve):
            link = Link(dve, env.sem("dve_chain"))
            dve.wait_ge(env.sem("vec_copied").h, 1)
            dve.wait_ge(bd.h, 32)
            dve.wait_ge(tn.h, 4)
            link(dve.tensor_tensor(tmp[:, :], pt[:, 0:16], env.cols("b_ada", 24)[:, 0:16], ALU.add))
            link(dve.tensor_copy(env.mods["one"][:, 0, 1, :], tmp[:, 0:8]))
            link(dve.scalar_tensor_tensor(out=env.mods["one"][:, 0, 0, :], in0=tmp[:, 8:16], scalar=1.0,
                                          in1=env.cols("norm_pre", 8), op0=ALU.add, op1=ALU.mult))
            for h in range(2):
                sl = slice(h * MC, (h + 1) * MC)
                dve.wait_ge(used.h, 5 + h)
                link(dve.tensor_tensor(gate[:, sl], ps[4 + h][:, :], brow[:, sl], ALU.add))
                link(dve.tensor_tensor(gate[:, sl], gate[:, sl], mul[:, sl], ALU.mult))
            link.close()
    used.base, rc.base, bd.base, tn.base = MG, 4, 32, 4
    for g in range(MG):
        env.sem(f"mod_w{g}").base = 32


def stage_norm(env, hT, pieces):
    nc = env.nc
    tiles, groups = [], []
    for src, n, col0, mod in pieces:
        for q in range(0, n, 4):
            m = min(4, n - q)
            groups.append((len(tiles), m, col0 + q * P, mod))
            tiles += [(src, q + j) for j in range(m)]
    RX = 8
    xl = [env.sem(f"x_loaded{i}") for i in range(RX)]
    sq, ms, rs, xn, tb = env.sem("x_squared"), env.sem("x_mean"), env.sem("x_rstd"), env.sem("x_normed"), env.sem("x_turned")
    ev = [env.sem("turn_copied_act"), env.sem("turn_copied_dve")]
    last_of = {g0 + m - 1: gi for gi, (g0, m, _, _) in enumerate(groups)}
    group_of = [gi for gi, (_, m, _, _) in enumerate(groups) for _ in range(m)]
    with ExitStack() as ctx:
        x = env.sb(ctx, "x_rows", [P, RX, D])
        junk = env.sb(ctx, "x_junk", [P, 2, D])
        st = env.sb(ctx, "x_stat", [P, 3, len(tiles)])
        ps = [env.banks(ctx, "ps_turn_a", 2), env.banks(ctx, "ps_turn_d", 2)]
        block = ctx.enter_context(nc.Block())

        @block.sync
        def _(sp):
            for i, (src, t) in enumerate(tiles):
                if i >= RX:
                    sp.wait_ge(tb.h, tb.at(8 * group_of[i - RX] + 8))
                sp.dma_start(x[:, i % RX, :], src[t * P:(t + 1) * P, :]).then_inc(xl[i % RX].h, 16)
            env.load_groups(sp, env.next_group + 2)

        @block.scalar
        def _(act):
            def evac(gi):
                g0, m, col, mod = groups[gi]
                for j in range(4):
                    k = 2 * j
                    act.wait_ge(tb.h, tb.at(8 * gi + k + 1))
                    act.activation(hT[:, k, col:col + m * P], ps[0][j % 2][:, 0:m * P], ACT.Identity,
                                   bias=mod[1][:, k:k + 1], scale=mod[0][:, k:k + 1]).then_inc(ev[0].h, 1)
            for i in range(len(tiles)):
                act.wait_ge(xl[i % RX].h, xl[i % RX].at(16 * (i // RX + 1)))
                if i >= 2:
                    act.wait_ge(sq.h, sq.at(i - 1))
                act.activation(junk[:, i % 2, :], x[:, i % RX, :], ACT.Square, accum_out=st[:, 0, i:i + 1]).then_inc(sq.h, 1)
                if i in last_of and last_of[i] >= 1:
                    evac(last_of[i] - 1)
            evac(len(groups) - 1)

        @block.gpsimd
        def _(pool):
            for i in range(len(tiles)):
                pool.wait_ge(ms.h, ms.at(i + 1))
                pool.tensor_tensor(st[:, 2, i:i + 1], st[:, 1, i:i + 1], env.mhalf[:, :], ALU.pow).then_inc(rs.h, 1)

        @block.vector
        def _(dve):
            def evac(gi):
                g0, m, col, mod = groups[gi]
                for j in range(4):
                    k = 2 * j + 1
                    dve.wait_ge(tb.h, tb.at(8 * gi + k + 1))
                    dve.tensor_scalar(hT[:, k, col:col + m * P], ps[1][j % 2][:, 0:m * P], mod[0][:, k:k + 1],
                                      mod[1][:, k:k + 1], ALU.mult, ALU.add).then_inc(ev[1].h, 1)
            def mean(i):
                dve.wait_ge(sq.h, sq.at(i + 1))
                dve.tensor_scalar(st[:, 1, i:i + 1], st[:, 0, i:i + 1], 1.0 / D, EPS, ALU.mult, ALU.add).then_inc(ms.h, 1)

            mean(0)
            for i in range(len(tiles)):
                if i not in last_of:
                    mean(i + 1)
                dve.wait_ge(rs.h, rs.at(i + 1))
                dve.tensor_scalar(x[:, i % RX, :], x[:, i % RX, :], st[:, 2, i:i + 1], None, ALU.mult).then_inc(xn.h, 1)
                if i in last_of:
                    if last_of[i] >= 1:
                        evac(last_of[i] - 1)
                    if i + 1 < len(tiles):
                        mean(i + 1)
            evac(len(groups) - 1)

        @block.tensor
        def _(pe):
            for gi, (g0, m, col, mod) in enumerate(groups):
                pe.wait_ge(xn.h, xn.at(g0 + m))
                for k in range(KT):
                    n = 4 * gi + k // 2
                    if n >= 2:
                        pe.wait_ge(ev[k % 2].h, ev[k % 2].at(n - 1))
                    for j in range(m):
                        mm = pe.transpose(ps[k % 2][n % 2][:, j * P:(j + 1) * P],
                                          x[:, (g0 + j) % RX, k * P:(k + 1) * P], env.ident[:, :])
                    mm.then_inc(tb.h, 1)
    n, g = len(tiles), len(groups)
    for i in range(RX):
        xl[i].base += 16 * len(range(i, n, RX))
    for s_, c_ in ((sq, n), (ms, n), (rs, n), (xn, n), (tb, 8 * g), (ev[0], 4 * g), (ev[1], 4 * g)):
        s_.base += c_


def stage_recurrent(env, hT, yaT, sumsq):
    nc, A = env.nc, env.A
    g0 = env.next_group
    NCH = S // CH
    xe, ge, cv, gm, sg = env.sem("xa_out"), env.sem("ga_out"), env.sem("conv_done"), env.sem("gate_mm"), env.sem("gate_act")
    pm_x, pm_g = env.sem("xa_mm"), env.sem("ga_mm")
    ab, sd, rt, ix, yd, y2, ss = (env.sem(n) for n in ("decay_done", "decay_sq", "root_done", "gated_in", "ya_done",
                                                       "ya_squared", "ya_summed"))
    with ExitStack() as ctx:
        xp = env.sb(ctx, "xa_padded", [P, 3 + S])
        xc = env.sb(ctx, "xa_conv", [P, S])
        gs = env.sb(ctx, "ga_silu", [P, 2, S])
        rr = env.sb(ctx, "gate_r", [P, S])
        ii = env.sb(ctx, "gate_i", [P, S])
        aa = env.sb(ctx, "decay", [P, S])
        tt = env.sb(ctx, "decay_tanh", [P, S])
        mm_ = env.sb(ctx, "multiplier", [P, S])
        wg = env.sb(ctx, "w_gates", [P, 2, CT, P])
        psx = env.banks(ctx, "ps_xa", 2)
        psg = env.banks(ctx, "ps_ga", 2)
        psr = env.banks(ctx, "ps_gates", 2)
        pss = env.banks(ctx, "ps_ss", 1)[0]
        block = ctx.enter_context(nc.Block())

        @block.sync
        def _(sp):
            sp.wait_ge(env.sem("wg_zero").h, 1)
            for g, name in enumerate(("w_rg_a", "w_rg_x")):
                for b in range(8):
                    r = HD * (b % 2)
                    sp.dma_start(wg[r:r + HD, g, b // 2, r:r + HD], A[name][0, b, :, :]).then_inc(env.sem("wg_loaded").h, 16)
            env.load_groups(sp, g0 + 6)

        @block.tensor
        def _(pe):
            def project(g, m, ps, n0, done, copied):
                w = env.group_here(pe, g)
                for q in range(NCH):
                    n = n0 + q
                    if n >= 2:
                        pe.wait_ge(copied.h, copied.at(n - 1))
                    for k in range(KT):
                        mm = pe.matmul(ps[n % 2][:, :], w[:, k, m * P:(m + 1) * P], hT[:, k, q * CH:(q + 1) * CH],
                                       start=(k == 0), stop=(k == KT - 1))
                    mm.then_inc(done.h, 1)

            def gates(c):
                pe.wait_ge(cv.h, cv.at(c + 1))
                for g in range(2):
                    for q in range(NCH):
                        n = (2 * c + g) * NCH + q
                        if n >= 2:
                            pe.wait_ge(sg.h, sg.at(n - 1))
                        pe.matmul(psr[n % 2][:, :], wg[:, g, c, :], xc[:, q * CH:(q + 1) * CH],
                                  start=True, stop=True).then_inc(gm.h, 1)

            def squares(c):
                pe.wait_ge(y2.h, y2.at(c + 1))
                for t in range(NT):
                    mm = pe.matmul(pss[:, c * NT + t:c * NT + t + 1], rr[:, t * P:(t + 1) * P], env.ones[:, 0:1],
                                   start=True, stop=True)
                mm.then_inc(ss.h, 1)

            pe.wait_ge(env.sem("wg_loaded").h, 16 * 16)
            for c in range(CT):
                project(g0 + 2 * (c // 2), c % 2, psx, c * NCH, pm_x, xe)
                project(g0 + 2 * (c // 2) + 1, c % 2, psg, c * NCH, pm_g, ge)
                if c % 2:
                    pe.wait_ge(pm_g.h, pm_g.at((c + 1) * NCH))
                    pe.sem_inc(env.sem("w_used").h, 2)
                if c >= 1:
                    squares(c - 1)
                gates(c)
            squares(CT - 1)

        @block.scalar
        def _(act):
            for c in range(CT):
                if c >= 1:
                    act.wait_ge(cv.h, cv.at(c))
                for q in range(NCH):
                    n = c * NCH + q
                    act.wait_ge(pm_x.h, pm_x.at(n + 1))
                    act.activation(xp[:, 3 + q * CH:3 + (q + 1) * CH], psx[n % 2][:, :], ACT.Copy).then_inc(xe.h, 1)
                for q in range(NCH):
                    n = c * NCH + q
                    act.wait_ge(pm_g.h, pm_g.at(n + 1))
                    act.activation(gs[:, c % 2, q * CH:(q + 1) * CH], psg[n % 2][:, :], ACT.Silu).then_inc(ge.h, 1)
                if c >= 1:
                    act.wait_ge(ss.h, ss.at(c))
                for g, (dst, key) in enumerate(((rr, "b_rg_a"), (ii, "b_rg_x"))):
                    for q in range(NCH):
                        n = (2 * c + g) * NCH + q
                        act.wait_ge(gm.h, gm.at(n + 1))
                        act.activation(dst[:, q * CH:(q + 1) * CH], psr[n % 2][:, :], ACT.Sigmoid,
                                       bias=env.cols(key, 4)[:, c:c + 1]).then_inc(sg.h, 1)
                act.wait_ge(sg.h, sg.at((2 * c + 2) * NCH))
                act.activation(aa[:, :], rr[:, :], ACT.Exp, scale=env.nsp[:, c:c + 1]).then_inc(ab.h, 1)
                act.activation(tt[:, :], rr[:, :], ACT.Tanh, scale=env.nsp[:, c:c + 1]).then_inc(ab.h, 1)
                act.wait_ge(sd.h, sd.at(c + 1))
                act.activation(tt[:, :], mm_[:, :], ACT.Sqrt, scale=-1.0).then_inc(rt.h, 1)
                act.wait_ge(yd.h, yd.at(c + 1))
                act.activation(rr[:, :], yaT[:, c, :], ACT.Square).then_inc(y2.h, 1)

        @block.gpsimd
        def _(pool):
            pool.memset(wg[:, :, :, :], 0.0).then_inc(env.sem("wg_zero").h, 1)
            for c in range(CT):
                pool.wait_ge(sg.h, sg.at((2 * c + 2) * NCH))
                pool.wait_ge(cv.h, cv.at(c + 1))
                pool.tensor_tensor(ii[:, :], ii[:, :], xc[:, :], ALU.mult).then_inc(ix.h, 1)

        @block.vector
        def _(dve):
            link = Link(dve, env.sem("dve_chain"))
            link(dve.memset(xp[:, 0:3], 0.0))
            cw, cb = env.cols("conv_w", 16), env.cols("conv_b", 4)
            for c in range(CT):
                dve.wait_ge(xe.h, xe.at((c + 1) * NCH))
                o = xc[:, :]
                link(dve.tensor_scalar(o, xp[:, 0:S], cw[:, c:c + 1], cb[:, c:c + 1], ALU.mult, ALU.add))
                for j in range(1, 4):
                    ins = dve.scalar_tensor_tensor(out=o, in0=xp[:, j:j + S], scalar=cw[:, 4 * j + c:4 * j + c + 1], in1=o,
                                                   op0=ALU.mult, op1=ALU.add)
                    if j < 3:
                        link(ins)
                ins.then_inc(cv.h, 1)
                dve.wait_ge(ab.h, ab.at(2 * c + 2))
                link(dve.tensor_tensor(mm_[:, :], aa[:, :], aa[:, :], ALU.mult))
                dve.scalar_tensor_tensor(out=mm_[:, :], in0=mm_[:, :], scalar=1.0, in1=tt[:, :],
                                         op0=ALU.add, op1=ALU.mult).then_inc(sd.h, 1)
                dve.wait_ge(rt.h, rt.at(c + 1))
                dve.wait_ge(ix.h, ix.at(c + 1))
                link(dve.tensor_tensor(ii[:, :], ii[:, :], tt[:, :], ALU.mult))
                link(dve.tensor_tensor_scan(mm_[:, :], aa[:, :], ii[:, :], 0.0, ALU.mult, ALU.add))
                dve.wait_ge(ge.h, ge.at((c + 1) * NCH))
                dve.tensor_tensor(yaT[:, c, :], mm_[:, :], gs[:, c % 2, :], ALU.mult).then_inc(yd.h, 1)
            dve.wait_ge(ss.h, ss.at(CT))
            dve.tensor_reduce(sumsq[:, :], pss[:, 0:CT * NT].rearrange("p (c t) -> p t c", c=CT), AXX, ALU.add)
            link.close()
    for s_, c_ in ((xe, CT * NCH), (ge, CT * NCH), (pm_x, CT * NCH), (pm_g, CT * NCH), (cv, CT), (gm, 2 * CT * NCH),
                   (sg, 2 * CT * NCH), (ab, 2 * CT), (sd, CT), (rt, CT), (ix, CT), (yd, CT), (y2, CT), (ss, CT)):
        s_.base += c_
    env.next_group += 4


def stage_qkvg(env, hT, QT, KTt, v_d, gb_d):
    nc = env.nc
    g0 = env.next_group
    UN = 8 * NT
    mmd = env.sem("proj_mm")
    av, rd, st = env.sem("plain_out"), env.sem("rope_read"), env.sem("rope_sum")
    tq, tc = env.sem("qk_turned"), env.sem("qk_copied")
    NRO, NRN = 4, 4
    dv = [env.sem(f"plain_stored{i}") for i in range(NRO)]
    with ExitStack() as ctx:
        vb = env.sb(ctx, "plain_rows", [P, NRO, GC])
        ta = env.sb(ctx, "rope_a", [P, 2, GC])
        tb = env.sb(ctx, "rope_b", [P, 2, GC])
        nat = env.sb(ctx, "rope_rows", [P, NRN, GC])
        ps = env.banks(ctx, "ps_proj", 4)
        pt = env.banks(ctx, "ps_qk", 2)
        block = ctx.enter_context(nc.Block())

        @block.sync
        def _(sp):
            env.load_groups(sp, g0 + 8)
            for i in range(NRO):
                sp.wait_ge(dv[i].h, dv[i].at(16 * (4 * NT // NRO)))

        @block.tensor
        def _(pe):
            def turn(b):
                st_n = 4 * (b + 1)
                pe.wait_ge(st.h, st.at(st_n))
                for pr in range(2):
                    n = 2 * b + pr
                    if n >= 2:
                        pe.wait_ge(tc.h, tc.at(n - 1))
                    for j in range(4):
                        mm = pe.transpose(pt[n % 2][:, j * P:(j + 1) * P], nat[:, (4 * b + j) % NRN, pr * P:(pr + 1) * P],
                                          env.ident[:, :])
                    mm.then_inc(tq.h, 1)

            for u in range(UN):
                g, t = divmod(u, NT)
                w = env.group_here(pe, g0 + g)
                if u >= 4:
                    v = u - 4
                    if v < 4 * NT:
                        pe.wait_ge(av.h, av.at(v + 1))
                    else:
                        pe.wait_ge(rd.h, rd.at(v - 4 * NT + 1))
                for k in range(KT):
                    mm = pe.matmul(ps[u % 4][:, 0:GC], hT[:, k, t * P:(t + 1) * P], w[:, k, :],
                                   start=(k == 0), stop=(k == KT - 1))
                mm.then_inc(mmd.h, 1)
                if t == NT - 1:
                    pe.wait_ge(mmd.h, mmd.at(u + 1))
                    pe.sem_inc(env.sem("w_used").h, 1)
                r = u - 4 * NT
                if r >= 5 and r % 4 == 1:
                    turn(r // 4 - 1)
            turn(4 * NT // 4 - 1)

        @block.scalar
        def _(act):
            def copy_turned(b):
                for pr in range(2):
                    n = 2 * b + pr
                    g, q = divmod(b, NT // 4)
                    dst = (QT if g < 2 else KTt)[:, 2 * (g % 2) + pr, q * CH:(q + 1) * CH]
                    act.wait_ge(tq.h, tq.at(n + 1))
                    act.activation(dst, pt[n % 2][:, :], ACT.Copy, scale=-(HD ** -0.5) if g < 2 else 1.0).then_inc(tc.h, 1)

            def store(u):
                g, t = divmod(u, NT)
                dst = (v_d if g < 2 else gb_d)[t * P:(t + 1) * P, (g % 2) * GC:(g % 2 + 1) * GC]
                act.wait_ge(av.h, av.at(u + 1))
                act.dma_start(dst, vb[:, u % NRO, :]).then_inc(dv[u % NRO].h, 16)

            for u in range(4 * NT):
                act.wait_ge(mmd.h, mmd.at(u + 1))
                if u >= NRO:
                    act.wait_ge(dv[u % NRO].h, dv[u % NRO].at(16 * (u // NRO)))
                act.activation(vb[:, u % NRO, :], ps[u % 4][:, 0:GC], ACT.Copy if u < 2 * NT else ACT.Silu).then_inc(av.h, 1)
                if u >= 1:
                    store(u - 1)
            store(4 * NT - 1)
            for b in range(NT):
                copy_turned(b)

        @block.vector
        def _(dve):
            for r in range(4 * NT):
                t = r % NT
                src = ps[r % 4][:, 0:GC].rearrange("p (h a e) -> p h a e", a=2, e=HD // 2)
                a = ta[:, r % 2, :].rearrange("p (h a e) -> p h a e", a=2, e=HD // 2)
                b = tb[:, r % 2, :].rearrange("p (h a e) -> p h a e", a=2, e=HD // 2)
                shp = [P, 4, HD // 2]
                dve.wait_ge(mmd.h, mmd.at(4 * NT + r + 1))
                if r >= 2:
                    dve.wait_ge(st.h, st.at(r - 1))
                for h in range(2):
                    dve.tensor_tensor(a[:, :, h, :], src[:, :, h, :], env.cosF[:, t, h, None, :].to_broadcast(shp), ALU.mult)
                for h in range(2):
                    ins = dve.tensor_tensor(b[:, :, h, :], src[:, :, 1 - h, :],
                                            env.sinF[:, t, h, None, :].to_broadcast(shp), ALU.mult)
                ins.then_inc(rd.h, 1)

        @block.gpsimd
        def _(pool):
            for r in range(4 * NT):
                pool.wait_ge(rd.h, rd.at(r + 1))
                if r >= NRN:
                    pool.wait_ge(tq.h, tq.at(2 * ((r - NRN) // 4) + 2))
                pool.tensor_tensor(nat[:, r % NRN, :], ta[:, r % 2, :], tb[:, r % 2, :], ALU.add).then_inc(st.h, 1)
    for s_, c_ in ((mmd, UN), (av, 4 * NT), (rd, 4 * NT), (st, 4 * NT), (tq, 2 * NT), (tc, 2 * NT)):
        s_.base += c_
    for i in range(NRO):
        dv[i].base += 16 * (4 * NT // NRO)
    env.next_group += 8


def stage_dilated(env, vspace, QT, KTt, v_d, res_d):
    nc = env.nc
    plan = []
    for p, (window, dil) in enumerate(PATTERNS):
        nblk = S // dil // P
        for t in range(NT):
            n, r = (t, 0) if dil == 1 else ((t // dil, t % dil) if nblk > 1 else (0, t))
            q = (P * dil * n + r, dil)
            w = 1 if n == 0 else 2
            kc0 = P * dil * (n - w + 1) + r
            vt = [t] if w == 1 else [t - dil if dil > 1 else t - 1, t]
            for hh in range(2):
                plan.append((p, t, hh, q, (kc0, dil), w, vt))
    U = len(plan)
    smm, sm_, ex, tm, tc0, tc1, pvm, pvc = (env.sem(n) for n in (
        "score_mm", "score_min", "prob_exp", "prob_turned", "prob_copied_act", "prob_copied_dve", "pv_mm", "pv_copied"))
    vl = [env.sem("v_loaded0"), env.sem("v_loaded1")]
    rs = [env.sem("res_stored0"), env.sem("res_stored1")]
    with ExitStack() as ctx:
        V = vspace[:, :, :].rearrange("p (b x) s -> p b (x s)", b=2).rearrange("p b (t c) -> p b t c", c=H1 * HD)
        sc = env.sb(ctx, "scores", [P, 2, 4, 2 * P])
        pr = sc
        pT = env.wring[:, 0, :, :].rearrange("p (a x) c -> p a (x c)", a=2).rearrange("p a (j k) -> p a j k", k=P)
        res = env.sb(ctx, "result", [P, 2, RW])
        ps = env.banks(ctx, "ps_score", 4)
        pt = env.banks(ctx, "ps_pt", 2)
        pv = env.banks(ctx, "ps_pv", 2)
        block = ctx.enter_context(nc.Block())

        @block.sync
        def _(sp):
            views = [v_d.rearrange("(t p) c -> p t c", p=P),
                     v_d.rearrange("(n i r) c -> i n (r c)", i=P, r=4),
                     v_d.rearrange("(i r) c -> i (r c)", r=16)]
            def load_v(p):
                if p == 2:
                    sp.wait_ge(pvm.h, pvm.at(2 * NT))
                dst = V[:, p % 2, :, :]
                if p == 1:
                    dst = dst.rearrange("i (n r) c -> i n (r c)", r=4)
                if p == 2:
                    dst = dst.rearrange("i r c -> i (r c)")
                sp.dma_start(dst, views[p]).then_inc(vl[p % 2].h, 16)

            load_v(0)
            load_v(1)
            for u in range(1, U, 2):
                p, t, hh, (q0, dil), *_ = plan[u]
                tile = u // 2
                sp.wait_ge(pvc.h, pvc.at(u + 1))
                sp.wait_ge(ex.h, ex.at(4 * (u + 1)))
                rows = res_d[p][q0:q0 + dil * (P - 1) + 1:dil, :]
                sp.dma_start(rows, res[:, tile % 2, :]).then_inc(rs[tile % 2].h, 16)
                if u == 2 * NT + 3:
                    load_v(2)
            for i in range(2):
                sp.wait_ge(rs[i].h, rs[i].at(16 * (U // 4)))

        @block.tensor
        def _(pe):
            def scores(u):
                p, t, hh, (q0, dil), (k0, _), w, vt = plan[u]
                if u >= 2:
                    pe.wait_ge(sm_.h, sm_.at(4 * (u - 1)))
                for odd in range(2):
                    for j in range(2):
                        pair, lo = 2 * hh + j, HD * odd
                        mm = pe.matmul(ps[2 * (u % 2) + odd][:, j * 2 * P:j * 2 * P + w * P],
                                       QT[lo:lo + HD, pair, q0:q0 + dil * (P - 1) + 1:dil],
                                       KTt[lo:lo + HD, pair, k0:k0 + dil * (w * P - 1) + 1:dil], start=True, stop=True)
                mm.then_inc(smm.h, 1)

            def turn(u):
                w = plan[u][5]
                pe.wait_ge(ex.h, ex.at(4 * (u + 1)))
                for b in range(2):
                    if u >= 1:
                        c = (tc0, tc1)[b]
                        pe.wait_ge(c.h, c.at(u))
                    for j in range(2):
                        for x in range(w):
                            mm = pe.transpose(pt[b][:, (j * w + x) * P:(j * w + x + 1) * P],
                                              pr[:, u % 2, 2 * b + j, x * P:(x + 1) * P], env.ident[:, :])
                    mm.then_inc(tm.h, 1)

            def values(u):
                p, t, hh, _, _, w, vt = plan[u]
                if u % (2 * NT) == 0:
                    pe.wait_ge(vl[p % 2].h, vl[p % 2].at(16 * (p // 2 + 1)))
                if u >= 2:
                    pe.wait_ge(pvc.h, pvc.at(u - 1))
                for b in range(2):
                    c = (tc0, tc1)[b]
                    pe.wait_ge(c.h, c.at(u + 1))
                    for j in range(2):
                        head = 2 * (2 * hh + j) + b
                        for x in range(w):
                            mm = pe.matmul(pv[u % 2][:, (head % 4) * HD:(head % 4 + 1) * HD],
                                           pT[:, u % 2, 4 * b + j * w + x, :], V[:, p % 2, vt[x], head * HD:(head + 1) * HD],
                                           start=(x == 0), stop=(x == w - 1))
                mm.then_inc(pvm.h, 1)

            scores(0)
            scores(1)
            for u in range(U):
                turn(u)
                if u + 2 < U:
                    scores(u + 2)
                values(u)

        def slot_head(hh, b, j):
            return 2 * (2 * hh + j) + b

        @block.vector
        def _(dve):
            def minima(u):
                p, t, hh, _, _, w, _ = plan[u]
                dve.wait_ge(smm.h, smm.at(u + 1))
                if u >= 2:
                    dve.wait_ge(tm.h, tm.at(2 * (u - 1)))
                if hh == 0 and u >= 4:
                    i = (u // 2) % 2
                    dve.wait_ge(rs[i].h, rs[i].at(16 * (u // 4)))
                for b in range(2):
                    for j in range(2):
                        h = slot_head(hh, b, j)
                        dve.tensor_tensor_reduce(sc[:, u % 2, 2 * b + j, 0:w * P],
                                                 ps[2 * (u % 2) + b][:, j * 2 * P:j * 2 * P + w * P],
                                                 env.mask1[:, (2 - w) * P:2 * P], 1.0, 3e38, ALU.add, ALU.min,
                                                 res[:, (u // 2) % 2, H1 * HD + h:H1 * HD + h + 1]).then_inc(sm_.h, 1)

            def copies(u):
                p, t, hh, _, _, w, _ = plan[u]
                dve.wait_ge(tm.h, tm.at(2 * u + 2))
                if u >= 2:
                    dve.wait_ge(pvm.h, pvm.at(u - 1))
                dve.tensor_copy(pT[:, u % 2, 4:4 + 2 * w, :], pt[1][:, 0:2 * w * P].rearrange("p (a b) -> p a b", b=P))\
                   .then_inc(tc1.h, 1)

            def keep(u):
                _, _, hh, _, _, _, _ = plan[u]
                dve.wait_ge(pvm.h, pvm.at(u + 1))
                dve.tensor_copy(res[:, (u // 2) % 2, hh * 4 * HD:(hh + 1) * 4 * HD], pv[u % 2][:, 0:4 * HD]).then_inc(pvc.h, 1)

            minima(0)
            for u in range(U):
                if u + 1 < U:
                    minima(u + 1)
                copies(u)
                if u >= 1:
                    keep(u - 1)
            keep(U - 1)

        @block.scalar
        def _(act):
            for u in range(U + 1):
                if u < U:
                    p, t, hh, _, _, w, _ = plan[u]
                    for b in range(2):
                        for j in range(2):
                            h = slot_head(hh, b, j)
                            act.wait_ge(sm_.h, sm_.at(4 * u + 2 * b + j + 1))
                            act.activation(pr[:, u % 2, 2 * b + j, 0:w * P], sc[:, u % 2, 2 * b + j, 0:w * P], ACT.Exp,
                                           bias=res[:, (u // 2) % 2, H1 * HD + h:H1 * HD + h + 1], scale=-1.0,
                                           accum_out=res[:, (u // 2) % 2, H1 * HD + H1 + h:H1 * HD + H1 + h + 1])\
                               .then_inc(ex.h, 1)
                if u >= 1:
                    v = u - 1
                    w = plan[v][5]
                    act.wait_ge(tm.h, tm.at(2 * v + 1))
                    if v >= 2:
                        act.wait_ge(pvm.h, pvm.at(v - 1))
                    act.activation(pT[:, v % 2, 0:2 * w, :], pt[0][:, 0:2 * w * P].rearrange("p (a b) -> p a b", b=P),
                                   ACT.Copy).then_inc(tc0.h, 1)
    for s_, c_ in ((smm, U), (sm_, 4 * U), (ex, 4 * U), (tm, 2 * U), (tc0, U), (tc1, U), (pvm, U), (pvc, U),
                   (vl[0], 32), (vl[1], 16), (rs[0], 16 * (U // 4)), (rs[1], 16 * (U // 4))):
        s_.base += c_


def stage_output1(env, yaT, sumsq, res_d, gb_d, gate, h_d, gate_d):
    nc, A = env.nc, env.A
    LG = 3 * D // GC
    MG2 = 2 * LG
    md, mu = [env.sem(f"mod2_w{i}") for i in range(4)], env.sem("mod2_used")
    gcs, gtn, gdn = env.sem("mod2_gate_cols"), env.sem("mod2_gate_turned"), env.sem("gate_stored")
    NB = 3
    ld = [env.sem(f"o_rows{i}") for i in range(NB)]
    xld = [env.sem(f"o_x{i}") for i in range(NB)]
    order = [(kind, t - lag) for t in range(NT + 2) for kind, lag in (("y", 0), ("m", 2)) if 0 <= t - lag < NT]
    nth = {step: n + 1 for n, step in enumerate(order)}
    yb, tm, tc, mmd, st = (env.sem(n) for n in ("yb_done", "yb_turned", "yb_copied", "out_mm", "out_sum"))
    ra, pa, pb = env.sem("ra_ready"), env.sem("out_a_scaled"), env.sem("out_b_added")
    hs = [env.sem("h_stored0"), env.sem("h_stored1")]
    mn, wx = env.sem("min_ready"), env.sem("weight_exp")
    sqs, pw_in, pw = env.sem("sq_ready"), env.sem("pow_in"), env.sem("pow_out")
    with ExitStack() as ctx:
        wo = env.sb(ctx, "w_out", [P, KT, D])
        r = env.sb(ctx, "res_rows", [P, NB, 3, RW])
        gb = env.sb(ctx, "gb_rows", [P, NB, H1 * HD])
        xr = env.sb(ctx, "x_res", [P, NB, D])
        sm = env.sb(ctx, "smalls", [P, 2, 12, H1])
        ybn = env.sb(ctx, "yb_rows", [P, 2, H1 * HD])
        junk = env.sb(ctx, "junk", [P, 2, D])
        ybT = env.sb(ctx, "yb_t", [P, 2, 4, P])
        mix = env.sb(ctx, "mix", [P, 2, D])
        stt = env.sb(ctx, "stats", [P, NT, 8])
        rst = env.sb(ctx, "ya_rstd", [P, 2, NT])
        mw = env.sb(ctx, "mod_weights", [P, 4, KT, GC])
        mc = env.sb(ctx, "mod_cols", [P, 2, 24, 2])
        gcol = env.sb(ctx, "gate_cols", [P, 2, 2, KT])
        grow = env.sb(ctx, "gate_rows", [4 * KT, P])
        pM = env.banks(ctx, "ps_mod2", 1)[0]
        pA = env.banks(ctx, "ps_oa", 2)
        pB = [env.banks(ctx, f"ps_ob{i}", 2) for i in range(2)]
        pT = env.banks(ctx, "ps_ybt", 1)
        block = ctx.enter_context(nc.Block())

        @block.sync
        def _(sp):
            sp.dma_start(wo[:, :, :], A["w_out"][0].rearrange("(k p) c -> p k c", p=P)).then_inc(env.sem("wo_loaded").h, 16)
            for t in range(NT + 3):
                if t < NT:
                    if t >= NB:
                        sp.wait_ge(yb.h, yb.at(t - NB + 1))
                    rows = slice(t * P, (t + 1) * P)
                    for p in range(3):
                        sp.dma_start(r[:, t % NB, p, :], res_d[p][rows, :]).then_inc(ld[t % NB].h, 16)
                    sp.dma_start(gb[:, t % NB, :], gb_d[rows, :]).then_inc(ld[t % NB].h, 16)
                if 0 <= t - 1 < NT:
                    v = t - 1
                    if v >= NB:
                        sp.wait_ge(st.h, st.at(v - NB + 1))
                    sp.dma_start(xr[:, v % NB, :], A["x"][0, v * P:(v + 1) * P, :]).then_inc(xld[v % NB].h, 16)
                if t >= 3:
                    v = t - 3
                    sp.wait_ge(st.h, st.at(v + 1))
                    sp.dma_start(h_d[v * P:(v + 1) * P, :], mix[:, v % 2, :]).then_inc(hs[v % 2].h, 16)
            sp.wait_ge(gcs.h, gcs.at(2))
            for l in range(2):
                for v in range(2):
                    r0 = (2 * l + v) * KT
                    sp.dma_start(gate_d[l][v].rearrange("a (m p) -> (a m) p", p=P), grow[r0:r0 + KT, :]).then_inc(gdn.h, 16)
            for i in range(2):
                sp.wait_ge(hs[i].h, hs[i].at(16 * (NT // 2)))
            sp.wait_ge(gdn.h, gdn.at(64))

        @block.gpsimd
        def _(pool):
            pool.wait_ge(pw_in.h, pw_in.at(1))
            pool.tensor_tensor(rst[:, 1, :], rst[:, 0, :], env.mhalf[:, :].to_broadcast([P, NT]), ALU.pow).then_inc(ra.h, 1)
            for kind, t in order:
                c = 1 if kind == "y" else 4
                pool.wait_ge(pw_in.h, pw_in.at(1 + nth[kind, t]))
                pool.tensor_tensor(stt[:, t, c + 1:c + 2], stt[:, t, c:c + 1], env.mhalf[:, :], ALU.pow).then_inc(pw.h, 1)

        @block.tensor
        def _(pe):
            def modulate(g):
                pe.wait_ge(md[g % 4].h, md[g % 4].at(16 * (g // 4 + 1)))
                for m in range(2):
                    o = 2 * (2 * g + m)
                    for k in range(KT):
                        mm = pe.matmul(pM[:, o:o + 2], mw[:, g % 4, k, m * P:(m + 1) * P], env.csilu[:, 8 + k:24:8],
                                       start=(k == 0), stop=(k == KT - 1))
                mm.then_inc(mu.h, 1)

            for t in range(NT + 1):
                for g in range(3 * t // 2, min(MG2, 3 * (t + 1) // 2)):
                    modulate(g)
                if t < NT:
                    pe.wait_ge(yb.h, yb.at(t + 1))
                    if t >= 1:
                        pe.wait_ge(tc.h, tc.at(t))
                    for j in range(4):
                        mm = pe.transpose(pT[0][:, j * P:(j + 1) * P], ybn[:, t % 2, j * P:(j + 1) * P], env.ident[:, :])
                    mm.then_inc(tm.h, 1)
                if t == 0:
                    pe.wait_ge(env.sem("wo_scaled").h, 1)
                    continue
                v = t - 1
                for part, (bank, freed, ago) in enumerate(((pA, pa, 1), (pB[v % 2], pb, 2))):
                    if v >= ago:
                        pe.wait_ge(freed.h, freed.at(2 * (v - ago + 1)))
                    if part:
                        pe.wait_ge(tc.h, tc.at(v + 1))
                    for half in range(2):
                        for k in range(4):
                            lhs = yaT[:, k, v * P:(v + 1) * P] if part == 0 else ybT[:, v % 2, k, :]
                            mm = pe.matmul(bank[half][:, :], lhs, wo[:, 4 * part + k, half * CH:(half + 1) * CH],
                                           start=(k == 0), stop=(k == 3))
                    mm.then_inc(mmd.h, 1)
            pe.wait_ge(gcs.h, gcs.at(1))
            pe.transpose(pM[0:4 * KT, 2 * P:3 * P], gcol[:, :, :, :].rearrange("p l v m -> p (l v m)"), env.ident[:, :])\
              .then_inc(gtn.h, 1)

        @block.scalar
        def _(act):
            def load_mod(g):
                if g >= 4:
                    act.wait_ge(mu.h, mu.at(g - 3))
                l, c = divmod(g, LG)
                act.dma_start(mw[:, g % 4, :, :], A["w_mod_2"][l][:, c * GC:(c + 1) * GC].rearrange("(k p) c -> p k c", p=P))\
                   .then_inc(md[g % 4].h, 16)

            for g in range(3):
                load_mod(g)
            for t in range(NT + 2):
                for g in range(3 * t // 2, min(MG2, 3 * (t + 1) // 2)):
                    if g + 3 < MG2:
                        load_mod(g + 3)
                if t < NT:
                    act.wait_ge(mn.h, mn.at(t + 1))
                    act.activation(sm[:, t % 2, 4:7, :], sm[:, t % 2, 1:4, :], ACT.Exp).then_inc(wx.h, 1)
                    act.wait_ge(yb.h, yb.at(t + 1))
                    if t >= 1:
                        act.wait_ge(sqs.h, sqs.at(nth["y", t - 1]))
                    act.activation(junk[:, 0, 0:H1 * HD], ybn[:, t % 2, :], ACT.Square,
                                   accum_out=stt[:, t, 0:1]).then_inc(sqs.h, 1)
                    act.wait_ge(tm.h, tm.at(t + 1))
                    if t >= 2:
                        act.wait_ge(mmd.h, mmd.at(2 * (t - 1)))
                    act.activation(ybT[:, t % 2, :, :], pT[0][:, :].rearrange("p (a b) -> p a b", b=P), ACT.Copy)\
                       .then_inc(tc.h, 1)
                if t >= 2:
                    v = t - 2
                    if v == 0:
                        act.wait_ge(ra.h, ra.at(1))
                    act.wait_ge(mmd.h, mmd.at(2 * v + 1))
                    if v >= 2:
                        act.wait_ge(hs[v % 2].h, hs[v % 2].at(16 * (v // 2)))
                    for half in range(2):
                        act.activation(mix[:, v % 2, half * CH:(half + 1) * CH], pA[half][:, :], ACT.Copy,
                                       scale=rst[:, 1, v:v + 1]).then_inc(pa.h, 1)
                    act.wait_ge(pb.h, pb.at(2 * v + 2))
                    if v >= 1:
                        act.wait_ge(sqs.h, sqs.at(nth["m", v - 1]))
                    act.activation(junk[:, 1, :], mix[:, v % 2, :], ACT.Square, accum_out=stt[:, v, 3:4]).then_inc(sqs.h, 1)

        @block.vector
        def _(dve):
            link = Link(dve, env.sem("dve_chain"))
            dve.tensor_scalar(rst[:, 0, :], sumsq[:, :], 1.0 / DREC, EPS, ALU.mult, ALU.add).then_inc(pw_in.h, 1)
            dve.wait_ge(env.sem("wo_loaded").h, 16)
            for k in range(KT):
                g = env.cols("norm_rec", 4) if k < 4 else env.cols("norm_att", 4)
                ins = dve.tensor_scalar(wo[:, k, :], wo[:, k, :], g[:, k % 4:k % 4 + 1], None, ALU.mult)
            ins.then_inc(env.sem("wo_scaled").h, 1)
            for t in range(NT + 2):
                if t < NT:
                    b = t % 2
                    R, s = r[:, t % NB, :, :], sm[:, b, :, :]
                    o = H1 * HD
                    dve.wait_ge(ld[t % NB].h, ld[t % NB].at(64 * (t // NB + 1)))
                    link(dve.tensor_tensor(s[:, 0, :], R[:, 0, o:o + H1], R[:, 1, o:o + H1], ALU.min))
                    link(dve.tensor_tensor(s[:, 0, :], s[:, 0, :], R[:, 2, o:o + H1], ALU.min))
                    dve.tensor_tensor(s[:, 1:4, :], s[:, 0:1, :].to_broadcast([P, 3, H1]), R[:, :, o:o + H1],
                                      ALU.subtract).then_inc(mn.h, 1)
                    dve.wait_ge(wx.h, wx.at(t + 1))
                    link(dve.tensor_tensor(s[:, 7:10, :], s[:, 4:7, :], R[:, :, o + H1:o + 2 * H1], ALU.mult))
                    link(dve.tensor_tensor(s[:, 10, :], s[:, 7, :], s[:, 8, :], ALU.add))
                    link(dve.tensor_tensor(s[:, 10, :], s[:, 10, :], s[:, 9, :], ALU.add))
                    link(dve.reciprocal(s[:, 10, :], s[:, 10, :]))
                    link(dve.tensor_tensor(s[:, 7:10, :], s[:, 4:7, :], s[:, 10:11, :].to_broadcast([P, 3, H1]), ALU.mult))
                    for p in range(3):
                        ins = dve.tensor_tensor(R[:, p, 0:o].rearrange("p (h e) -> p h e", e=HD),
                                                R[:, p, 0:o].rearrange("p (h e) -> p h e", e=HD),
                                                s[:, 7 + p, :, None].to_broadcast([P, H1, HD]), ALU.mult)
                    link(ins)
                    link(dve.tensor_tensor(R[:, 0, 0:o], R[:, 0, 0:o], R[:, 1, 0:o], ALU.add))
                    link(dve.tensor_tensor(R[:, 0, 0:o], R[:, 0, 0:o], R[:, 2, 0:o], ALU.add))
                    if t >= 2:
                        dve.wait_ge(tm.h, tm.at(t - 1))
                    dve.tensor_tensor(ybn[:, b, :], R[:, 0, 0:o], gb[:, t % NB, :], ALU.mult).then_inc(yb.h, 1)
                    dve.wait_ge(sqs.h, sqs.at(nth["y", t]))
                    dve.tensor_scalar(stt[:, t, 1:2], stt[:, t, 0:1], 1.0 / (H1 * HD), EPS, ALU.mult, ALU.add)\
                       .then_inc(pw_in.h, 1)
                if t >= 2:
                    v = t - 2
                    dve.wait_ge(pw.h, pw.at(nth["y", v]))
                    dve.wait_ge(mmd.h, mmd.at(2 * v + 2))
                    dve.wait_ge(pa.h, pa.at(2 * v + 2))
                    for half in range(2):
                        sl = slice(half * CH, (half + 1) * CH)
                        dve.scalar_tensor_tensor(out=mix[:, v % 2, sl], in0=pB[v % 2][half][:, :], scalar=stt[:, v, 2:3],
                                                 in1=mix[:, v % 2, sl], op0=ALU.mult, op1=ALU.add).then_inc(pb.h, 1)
                    dve.wait_ge(sqs.h, sqs.at(nth["m", v]))
                    dve.tensor_scalar(stt[:, v, 4:5], stt[:, v, 3:4], 1.0 / D, EPS, ALU.mult, ALU.add).then_inc(pw_in.h, 1)
                    dve.wait_ge(pw.h, pw.at(nth["m", v]))
                    dve.wait_ge(xld[v % NB].h, xld[v % NB].at(16 * (v // NB + 1)))
                    link(dve.scalar_tensor_tensor(out=mix[:, v % 2, :], in0=mix[:, v % 2, :], scalar=stt[:, v, 5:6],
                                                  in1=gate[:, :], op0=ALU.mult, op1=ALU.mult))
                    dve.tensor_tensor(mix[:, v % 2, :], mix[:, v % 2, :], xr[:, v % NB, :], ALU.add).then_inc(st.h, 1)
            dve.wait_ge(mu.h, mu.at(MG2))
            bt, bo = env.place["b_mod_2"]
            link(dve.tensor_tensor(mc[:, :, :, :], pM[:, 0:96].rearrange("p (l m v) -> p l m v", l=2, v=2),
                                   env.vcols[:, bt, bo:bo + 48].rearrange("p (l m) -> p l m", l=2)[:, :, :, None]
                                   .to_broadcast([P, 2, 24, 2]), ALU.add))
            gt, go = env.place["norm_g_2"]
            for l in range(2):
                gain = env.vcols[:, gt, go + 8 * l:go + 8 * l + 8]
                for v in range(2):
                    mods = env.mods[f"l{l}"]
                    link(dve.tensor_copy(mods[:, v, 1, :], mc[:, l, 0:8, v]))
                    link(dve.scalar_tensor_tensor(out=mods[:, v, 0, :], in0=mc[:, l, 8:16, v], scalar=1.0, in1=gain,
                                                  op0=ALU.add, op1=ALU.mult))
            dve.tensor_copy(gcol[:, :, :, :], mc[:, :, 16:24, :].rearrange("p l m v -> p l v m")).then_inc(gcs.h, 1)
            dve.wait_ge(gtn.h, gtn.at(1))
            dve.tensor_copy(grow[:, :], pM[0:4 * KT, 2 * P:3 * P]).then_inc(gcs.h, 1)
            link.close()
    for s_, c_ in ((yb, NT), (tm, NT), (tc, NT), (mmd, 2 * NT), (st, NT), (ra, 1), (pa, 2 * NT), (pb, 2 * NT), (mn, NT),
                   (wx, NT), (sqs, 2 * NT), (pw_in, 2 * NT + 1), (pw, 2 * NT), (hs[0], 16 * (NT // 2)), (hs[1], 16 * (NT // 2)),
                   (mu, MG2), (gcs, 2), (gtn, 1), (gdn, 64), *((x, 16 * MG2 // 4) for x in md),
                   *((ld[i], 64 * len(range(i, NT, NB))) for i in range(NB)),
                   *((xld[i], 16 * len(range(i, NT, NB))) for i in range(NB))):
        s_.base += c_


CTX = 256
W = S + CTX
WT = W // P
CHUNKS = [(q * CH, CH) for q in range(S // CH)] + [(S, CTX)]


class Split:

    def __init__(self, env, ctx, hT, jobs, KS, NB):
        self.KS, self.NB = KS, NB
        self.env, self.hT, self.jobs, self.g0 = env, hT, jobs, env.next_group
        KS = self.KS
        self.fh = env.sb(ctx, "features_high", [P, NB, KS, CH], F32R)
        self.fl = env.sb(ctx, "features_low", [P, NB, KS, CH], F32R)
        self.wh = env.sb(ctx, "weights_high", [P, KT, GC], F32R)
        self.wl = env.sb(ctx, "weights_low", [P, KT, GC], F32R)
        self.ps = env.banks(ctx, "ps_proj", 8)
        names = ("features_high", "features_low", "weights_high", "weights_low", "step_mm")
        self.fhs, self.fls, self.whs, self.wls, self.stp = (env.sem(n) for n in names)
        self.out = {e: env.sem(f"product_out_{e}") for e in ("act", "dve")}
        self.chunks = [(g, c) for g, (form, chunks, e) in enumerate(jobs) for c in chunks]
        self.steps = [(x, k0) for x in range(len(self.chunks)) for k0 in range(0, KT, KS)]
        self.first = [min(x for x, (g, _) in enumerate(self.chunks) if g == gg) * (KT // KS) for gg in range(len(jobs))]

    def taken(self, x):
        e = self.jobs[self.chunks[x][0]][2]
        return self.out[e], sum(1 for g, _ in self.chunks[:x + 1] if self.jobs[g][2] == e)

    def parts(self, x):
        g, (c0, n) = self.chunks[x]
        return [self.ps[4 * (x % 2) + i] for i in range(2 if self.jobs[g][0] == "t" else n // P)]

    def tensor(self, pe):
        env, KS, NB = self.env, self.KS, self.NB
        for s, (x, k0) in enumerate(self.steps):
            g, (c0, n) = self.chunks[x]
            if k0 % (KT // 2) == 0 and x * (KT // KS) == self.first[g]:
                pe.wait_ge(self.wls.h, self.wls.at(2 * g + 1 + k0 // (KT // 2)))
            if k0 == 0 and x >= 2:
                sem, count = self.taken(x - 2)
                pe.wait_ge(sem.h, sem.at(count))
            pe.wait_ge(self.fls.h, self.fls.at(s + 1))
            fh, fl = self.fh[:, s % NB, :, :], self.fl[:, s % NB, :, :]
            wh, wl = self.wh, self.wl
            for i, bank in enumerate(self.parts(x)):
                for k in range(KS):
                    for a, (f_, w_) in enumerate(((fh, wh), (fh, wl), (fl, wh))):
                        start, stop = k0 + k == 0 and a == 0, k0 + k == KT - 1 and a == 2
                        if self.jobs[g][0] == "t":
                            mm = pe.matmul(bank[:, 0:n], w_[:, k0 + k, i * P:(i + 1) * P], f_[:, k, 0:n], start=start, stop=stop)
                        else:
                            mm = pe.matmul(bank[:, 0:GC], f_[:, k, i * P:(i + 1) * P], w_[:, k0 + k, :], start=start, stop=stop)
            mm.then_inc(self.stp.h, 1)
            if s + 1 == len(self.steps) or s + 1 in self.first:
                pe.wait_ge(self.stp.h, self.stp.at(s + 1))
                pe.sem_inc(env.sem("w_used").h, 1)

    def scalar(self, act, take):
        env, KS, NB = self.env, self.KS, self.NB

        def weights(g):
            w = env.group_here(act, self.g0 + g)
            if g >= 1:
                act.wait_ge(self.stp.h, self.stp.at(self.first[g]))
            for half in range(2):
                ks = slice(half * KT // 2, (half + 1) * KT // 2)
                act.activation(self.wh[:, ks, :], w[:, ks, :], ACT.Copy).then_inc(self.whs.h, 1)

        def high(s):
            x, k0 = self.steps[s]
            c0, n = self.chunks[x][1]
            if s >= NB:
                act.wait_ge(self.stp.h, self.stp.at(s - NB + 1))
            act.activation(self.fh[:, s % NB, :, 0:n], self.hT[:, k0:k0 + KS, c0:c0 + n], ACT.Copy).then_inc(self.fhs.h, 1)

        weights(0)
        for s in range(NB):
            high(s)
        for s, (x, k0) in enumerate(self.steps):
            g = self.chunks[x][0]
            if s + NB < len(self.steps):
                high(s + NB)
            if s + 1 in self.first:
                weights(g + 1)
            if k0 + KS == KT and self.jobs[g][2] == "act":
                act.wait_ge(self.stp.h, self.stp.at(s + 1))
                take(act, g, self.chunks[x][1], self.parts(x)).then_inc(self.out["act"].h, 1)

    def vector(self, dve, take, beside=None):
        env, KS, NB = self.env, self.KS, self.NB

        def weights(g):
            w = env.wring[:, (self.g0 + g) % 2, :, :]
            if g >= 1:
                dve.wait_ge(self.stp.h, self.stp.at(self.first[g]))
            for half in range(2):
                ks = slice(half * KT // 2, (half + 1) * KT // 2)
                dve.wait_ge(self.whs.h, self.whs.at(2 * g + half + 1))
                dve.tensor_tensor(self.wl[:, ks, :], w[:, ks, :], self.wh[:, ks, :].bitcast(F32), ALU.subtract)\
                   .then_inc(self.wls.h, 1)

        def low(s):
            x, k0 = self.steps[s]
            c0, n = self.chunks[x][1]
            dve.wait_ge(self.fhs.h, self.fhs.at(s + 1))
            if s >= NB:
                dve.wait_ge(self.stp.h, self.stp.at(s - NB + 1))
            dve.tensor_tensor(self.fl[:, s % NB, :, 0:n], self.hT[:, k0:k0 + KS, c0:c0 + n],
                              self.fh[:, s % NB, :, 0:n].bitcast(F32), ALU.subtract).then_inc(self.fls.h, 1)

        weights(0)
        for s in range(NB):
            low(s)
        for s, (x, k0) in enumerate(self.steps):
            g = self.chunks[x][0]
            if s + NB < len(self.steps):
                low(s + NB)
            if beside:
                beside(g, x, k0)
            if s + 1 in self.first:
                weights(g + 1)
            if k0 + KS == KT and self.jobs[g][2] == "dve":
                dve.wait_ge(self.stp.h, self.stp.at(s + 1))
                take(dve, g, self.chunks[x][1], self.parts(x)).then_inc(self.out["dve"].h, 1)

    def close(self):
        n, g = len(self.steps), len(self.jobs)
        for s_, c_ in ((self.fhs, n), (self.fls, n), (self.whs, 2 * g), (self.wls, 2 * g), (self.stp, n)):
            s_.base += c_
        for e, s_ in self.out.items():
            s_.base += sum(1 for gg, _ in self.chunks if self.jobs[gg][2] == e)
        self.env.next_group += g


def stage_hgrn_in(env, hT, qT, vN, zT, zchunks):
    nc = env.nc
    with ExitStack() as ctx:
        proj = Split(env, ctx, hT, [("t", CHUNKS, "act"), ("n", CHUNKS, "act"), ("t", zchunks, "act")], 2, 3)
        block = ctx.enter_context(nc.Block())

        def take(act, g, chunk, banks):
            c0, n = chunk
            for i, bank in enumerate(banks):
                if g == 1:
                    ins = act.activation(vN[:, c0 // P + i, :], bank[:, 0:GC], ACT.Copy)
                else:
                    ins = act.activation((qT, None, zT)[g][:, i, c0:c0 + n], bank[:, 0:n], ACT.Silu)
            return ins

        @block.sync
        def _(sp):
            env.load_groups(sp, proj.g0 + 3 + 1)

        @block.tensor
        def _(pe):
            proj.tensor(pe)

        @block.scalar
        def _(act):
            proj.scalar(act, take)

        @block.vector
        def _(dve):
            proj.vector(dve, None)
    proj.close()


def stage_hgrn_scan(env, layer, d, hT, qT, vN, oT, out_ctx):
    nc, A = env.nc, env.A
    g = env.next_group
    lat = [(S // CH - 1 - q if d else q) for q in range(S // CH)]
    steps = [(S, 2)] + [(q * CH, 4) for q in lat]
    NSTEP = len(steps)
    LV = 8
    pj, fk, fl = env.sem("f_mm"), env.sem("f_done"), env.sem("f_bounded")
    qi, up, sc, cp = env.sem("qf_start"), env.sem("level_up"), env.sem("score_lv"), env.sem("score_kept")
    tm, tc, um, su, om, oc = (env.sem(n) for n in ("kb_turned", "kb_copied", "state_mm", "state_up", "o_mm", "o_out"))
    qh, kh = (0, 1) if d else (1, 0)
    NU = 2 * LV
    with ExitStack() as ctx:
        f = env.sb(ctx, "f", [P, 2, CH])
        kb = env.sb(ctx, "kb", [P, 2, CH])
        qf = env.sb(ctx, "qf", [P, 2, CH])
        fn = env.sb(ctx, "f_next", [P, 2, CH])
        kn = env.sb(ctx, "k_next", [P, 2, CH])
        pp = env.sb(ctx, "products", [P, 2, CH])
        sT = env.sb(ctx, "scores_t", [P, 2, 2, CH])
        kbn = env.sb(ctx, "kb_rows", [P, 2, CH])
        st = env.sb(ctx, "state", [P, 2, 2, P])
        poff = [0] * 8
        for l in range(1, 8):
            poff[l] = poff[l - 1] + (CH >> (l - 1) if l > 1 else 0)
        pf = env.banks(ctx, "ps_f", 2)
        pS = [env.banks(ctx, f"ps_s{i}", 2) for i in range(2)]
        pO = env.banks(ctx, "ps_o", 2)
        block = ctx.enter_context(nc.Block())

        def prod(pr, l, n):
            return f[:, pr, 0:n * P] if l == 0 else pp[:, pr, poff[l]:poff[l] + (n * P >> l)]

        @block.sync
        def _(sp):
            env.load_groups(sp, g + 1 + 1)

        @block.tensor
        def _(pe):
            w = env.group_here(pe, g)

            def project(s, pr, k):
                col, n = steps[s]
                if k == 0 and s >= 1:
                    pe.wait_ge(fk.h, fk.at(4 * (s - 1) + 2 * pr + 2))
                mm = pe.matmul(pf[pr][:, 0:n * P], w[:, k, pr * P:(pr + 1) * P], hT[:, k, col:col + n * P],
                               start=(k == 0), stop=(k == KT - 1))
                if k == KT - 1:
                    mm.then_inc(pj.h, 1)

            for pr in range(2):
                for k in range(KT):
                    project(0, pr, k)
            for s, (col, n) in enumerate(steps):
                for lv in range(LV):
                    for pr in range(2):
                        if lv < 2:
                            pe.wait_ge(qi.h, qi.at(4 * s + 2 * pr + 2))
                        else:
                            pe.wait_ge(up.h, up.at(14 * s + 2 * (lv - 2) + pr + 1))
                        if lv >= 1:
                            pe.wait_ge(cp.h, cp.at(2 * (NU * s + 2 * (lv - 1) + pr) + 2))
                        elif s >= 1:
                            pe.wait_ge(su.h, su.at(sum(2 * m for _, m in steps[:s])))
                            pe.wait_ge(tc.h, tc.at(2 * s))
                        for h in range(2):
                            lo = HD * h
                            for i in range(n):
                                cs = slice(i * P, (i + 1) * P)
                                rhs = qT[lo:lo + HD, pr, col + i * P:col + (i + 1) * P] if lv == 0 else qf[lo:lo + HD, pr, cs]
                                mm = pe.matmul(pS[pr][h][:, cs], kb[lo:lo + HD, pr, cs], rhs, start=True, stop=True)
                        mm.then_inc(sc.h, 1)
                        if s + 1 < NSTEP:
                            project(s + 1, pr, lv)
                for pr in range(2):
                    pe.wait_ge(up.h, up.at(14 * s + 12 + pr + 1))
                    pe.wait_ge(cp.h, cp.at(2 * (NU * s + 2 * (LV - 1) + pr) + 2))
                    for i in range(n):
                        mm = pe.transpose(pS[pr][0][:, i * P:(i + 1) * P], kb[:, pr, i * P:(i + 1) * P], env.ident[:, :])
                    mm.then_inc(tm.h, 1)
                for pr in range(2):
                    pe.wait_ge(tc.h, tc.at(2 * s + pr + 1))
                    for i in range(n):
                        mm = pe.matmul(pS[pr][1][:, i * P:(i + 1) * P], kbn[:, pr, i * P:(i + 1) * P],
                                       vN[:, col // P + i, pr * P:(pr + 1) * P], start=True, stop=True)
                    mm.then_inc(um.h, 1)
                order = range(n - 1, -1, -1) if d else range(n)
                for x, i in enumerate(order):
                    n_done = sum(m for _, m in steps[:s]) + x
                    for pr in range(2):
                        cs = slice(i * P, (i + 1) * P)
                        if x == 0 and s >= 1:
                            pe.wait_ge(oc.h, oc.at(2 * (s - 1) + pr + 1))
                        for h in range(2):
                            pe.matmul(pO[pr][HD * h:HD * (h + 1), cs],
                                      vN[:, col // P + i, pr * P + h * HD:pr * P + (h + 1) * HD],
                                      sT[:, pr, h, cs], start=True, stop=False)
                        if n_done >= 1:
                            pe.wait_ge(su.h, su.at(2 * (n_done - 1) + pr + 1))
                        for h in range(2):
                            lo = slice(HD * h, HD * (h + 1))
                            mm = pe.matmul(pO[pr][lo, cs], st[lo, pr, n_done % 2, lo], qf[lo, pr, cs],
                                           start=False, stop=True)
                        mm.then_inc(om.h, 1)
            pe.wait_ge(om.h, om.at(2 * WT))
            pe.sem_inc(env.sem("w_used").h, 1)

        @block.scalar
        def _(act):
            def sigmoids(s):
                n = steps[s][1]
                for pr in range(2):
                    act.wait_ge(pj.h, pj.at(2 * s + pr + 1))
                    if s >= 1:
                        act.wait_ge(qi.h, qi.at(4 * (s - 1) + 4))
                    act.activation(fn[:, pr, 0:n * P], pf[pr][:, 0:n * P], ACT.Sigmoid).then_inc(fk.h, 1)
                    act.activation(kn[:, pr, 0:n * P], pf[pr][:, 0:n * P], ACT.Sigmoid, scale=-1.0).then_inc(fk.h, 1)

            sigmoids(0)
            for s, (col, n) in enumerate(steps):
                if s + 1 < NSTEP:
                    sigmoids(s + 1)
                for pr in range(2):
                    act.wait_ge(tm.h, tm.at(2 * s + pr + 1))
                    if s >= 1:
                        act.wait_ge(um.h, um.at(2 * (s - 1) + pr + 1))
                    act.activation(kbn[:, pr, 0:n * P], pS[pr][0][:, 0:n * P], ACT.Copy).then_inc(tc.h, 1)
                if d == 0:
                    for pr in range(2):
                        act.wait_ge(om.h, om.at(2 * sum(m for _, m in steps[:s + 1])))
                        act.activation(oT[:, pr, col:col + n * P], pO[pr][:, 0:n * P], ACT.Copy).then_inc(oc.h, 1)

        if layer == 1:
            @block.gpsimd
            def _(pool):
                for s, (col, n) in enumerate(steps):
                    for pr in range(2):
                        pool.wait_ge(fk.h, fk.at(4 * s + 2 * pr + 2))
                        lo, hi = env.lb[:, 0, d, pr:pr + 1], env.lb[:, 1, d, pr:pr + 1]
                        pool.tensor_scalar(fn[:, pr, 0:n * P], fn[:, pr, 0:n * P], hi, lo, ALU.mult, ALU.add).then_inc(fl.h, 1)
                        pool.tensor_scalar(kn[:, pr, 0:n * P], kn[:, pr, 0:n * P], hi, None, ALU.mult).then_inc(fl.h, 1)

        @block.vector
        def _(dve):
            link = Link(dve, env.sem("dve_chain"))
            link(dve.memset(st[:, :, :, :], 0.0))

            def halves(ap, h):
                return ap.rearrange("p (b a x) -> p b a x", a=2, x=h)

            for s, (col, n) in enumerate(steps):
                w = n * P
                ready, done = (fl, 4) if layer == 1 else (fk, 4)
                for pr in range(2):
                    dve.wait_ge(ready.h, ready.at(4 * s + 2 * pr + 2))
                    if s >= 1:
                        dve.wait_ge(tm.h, tm.at(2 * (s - 1) + pr + 1))
                        dve.wait_ge(om.h, om.at(2 * sum(m for _, m in steps[:s])))
                    dve.tensor_copy(f[:, pr, 0:w], fn[:, pr, 0:w])
                    dve.tensor_copy(kb[:, pr, 0:w], kn[:, pr, 0:w]).then_inc(qi.h, 1)
                    dve.tensor_tensor(qf[:, pr, 0:w], qT[:, pr, col:col + w], fn[:, pr, 0:w], ALU.mult).then_inc(qi.h, 1)
                dve.wait_ge(qi.h, qi.at(4 * s + 4))
                for lv in range(LV):
                    l = lv - 1
                    for pr in range(2):
                        dve.wait_ge(sc.h, sc.at(NU * s + 2 * lv + pr + 1))
                        if lv >= 1:
                            h = 1 << l
                            q2, k2 = halves(qf[:, pr, 0:w], h), halves(kb[:, pr, 0:w], h)
                            if lv >= 2:
                                dve.wait_ge(up.h, up.at(14 * s + 2 * (l - 1) + pr + 1))
                            p2 = prod(pr, l, n).rearrange("p (b a) -> p b a", a=2)
                            nb = w // (2 * h)
                            dve.tensor_tensor(q2[:, :, qh, :], q2[:, :, qh, :],
                                              p2[:, :, kh, None].to_broadcast([P, nb, h]), ALU.mult)
                            dve.tensor_tensor(k2[:, :, kh, :], k2[:, :, kh, :],
                                              p2[:, :, qh, None].to_broadcast([P, nb, h]), ALU.mult)
                            dve.tensor_tensor(prod(pr, l + 1, n), p2[:, :, 0], p2[:, :, 1], ALU.mult).then_inc(up.h, 1)
                        for h in range(2):
                            src = pS[pr][h][:, 0:w].rearrange("p (i x) -> p i x", x=P)
                            dst = sT[:, pr, h, 0:w].rearrange("p (i x) -> p i x", x=P)
                            if lv == 0:
                                dve.tensor_tensor(dst, src, env.ident[:, None, :].to_broadcast([P, n, P]), ALU.mult)\
                                   .then_inc(cp.h, 1)
                            else:
                                dve.wait_ge(cp.h, cp.at(2 * (NU * s + 2 * (lv - 1) + pr) + h + 1))
                                dve.copy_predicated(dst, env.levmask[:, 8 * d + l, None, :].to_broadcast([P, n, P]), src)\
                                   .then_inc(cp.h, 1)
                order = range(n - 1, -1, -1) if d else range(n)
                for x, i in enumerate(order):
                    n_done = sum(m for _, m in steps[:s]) + x
                    for pr in range(2):
                        if x == 0:
                            dve.wait_ge(um.h, um.at(2 * s + pr + 1))
                            dve.wait_ge(up.h, up.at(14 * s + 12 + pr + 1))
                        if n_done >= 1:
                            dve.wait_ge(om.h, om.at(2 * (n_done - 1) + pr + 1))
                            dve.wait_ge(su.h, su.at(2 * (n_done - 1) + pr + 1))
                        for h in range(2):
                            lo = slice(HD * h, HD * (h + 1))
                            ins = dve.scalar_tensor_tensor(
                                out=st[lo, pr, (n_done + 1) % 2, HD * h:HD * (h + 1)],
                                in0=st[lo, pr, n_done % 2, HD * h:HD * (h + 1)],
                                scalar=pp[lo, pr, poff[7] + i:poff[7] + i + 1],
                                in1=pS[pr][1][lo, i * P + HD * h:i * P + HD * (h + 1)], op0=ALU.mult, op1=ALU.add)
                        ins.then_inc(su.h, 1)
                if d == 1:
                    for pr in range(2):
                        dve.wait_ge(om.h, om.at(2 * sum(m for _, m in steps[:s + 1])))
                        dve.tensor_tensor(oT[:, pr, col:col + w], oT[:, pr, col:col + w], pO[pr][:, 0:w], ALU.add)\
                           .then_inc(oc.h, 1)
            link.close()
    for s_, c_ in ((pj, 2 * NSTEP), (fk, 4 * NSTEP), (fl, 4 * NSTEP if layer == 1 else 0), (qi, 4 * NSTEP), (up, 14 * NSTEP),
                   (sc, NU * NSTEP), (cp, 2 * NU * NSTEP), (tm, 2 * NSTEP), (tc, 2 * NSTEP), (um, 2 * NSTEP),
                   (su, 2 * WT), (om, 2 * WT), (oc, 2 * NSTEP)):
        s_.base += c_
    env.next_group += 1


def stage_hgrn_norm(env, layer, oT, zT, chunks):
    nc = env.nc
    units = [(pr, c) for pr in range(2) for c in chunks]
    sq, mm_, rt, rc, sd, yo = (env.sem(n) for n in ("o_squared", "o_mean", "o_root", "o_recip", "o_scaled", "o_gated"))
    with ExitStack() as ctx:
        o2 = env.sb(ctx, "o_sq", [P, 2, CH])
        rr = env.sb(ctx, "o_rms", [P, 2, CH])
        ps = env.banks(ctx, "ps_on", 2)
        block = ctx.enter_context(nc.Block())
        gains = env.cols("hgrn_norm_g_2", 4)

        @block.scalar
        def _(act):
            for u in range(len(units) + 1):
                if u < len(units):
                    pr, (c0, n) = units[u]
                    if u >= 2:
                        act.wait_ge(mm_.h, mm_.at(u - 1))
                    act.activation(o2[:, u % 2, 0:n], oT[:, pr, c0:c0 + n], ACT.Square).then_inc(sq.h, 1)
                if u >= 1:
                    v = u - 1
                    n = units[v][1][1]
                    act.wait_ge(mm_.h, mm_.at(v + 1))
                    if v >= 2:
                        act.wait_ge(sd.h, sd.at(v - 1))
                    act.activation(rr[:, v % 2, 0:n], ps[v % 2][:, 0:n], ACT.Sqrt, bias=env.eps[:, :]).then_inc(rt.h, 1)

        @block.tensor
        def _(pe):
            for u, (pr, (c0, n)) in enumerate(units):
                pe.wait_ge(sq.h, sq.at(u + 1))
                if u >= 2:
                    pe.wait_ge(rt.h, rt.at(u - 1))
                pe.matmul(ps[u % 2][:, 0:n], env.headmean[:, :], o2[:, u % 2, 0:n], start=True, stop=True).then_inc(mm_.h, 1)

        @block.vector
        def _(dve):
            for u, (pr, (c0, n)) in enumerate(units):
                o = oT[:, pr, c0:c0 + n]
                dve.wait_ge(rt.h, rt.at(u + 1))
                dve.reciprocal(rr[:, u % 2, 0:n], rr[:, u % 2, 0:n]).then_inc(rc.h, 1)
                dve.wait_ge(rc.h, rc.at(u + 1))
                dve.scalar_tensor_tensor(out=o, in0=o, scalar=gains[:, 2 * layer + pr:2 * layer + pr + 1],
                                         in1=rr[:, u % 2, 0:n], op0=ALU.mult, op1=ALU.mult).then_inc(sd.h, 1)

        @block.gpsimd
        def _(pool):
            for u, (pr, (c0, n)) in enumerate(units):
                o = oT[:, pr, c0:c0 + n]
                pool.wait_ge(sd.h, sd.at(u + 1))
                pool.tensor_tensor(o, o, zT[:, pr, c0:c0 + n], ALU.mult).then_inc(yo.h, 1)
    for s_ in (sq, mm_, rt, rc, sd, yo):
        s_.base += len(units)


def stage_qkv2(env, layer, hT, QT, keys, VN, aT, qtiles, zchunks):
    nc, A = env.nc, env.A
    g0 = env.next_group
    units = [(0, t, 4) for t in range(qtiles)] + [(1, t, 2) for t in range(WT)]
    zun = [(m, c) for m in range(2) for c in zchunks]
    NU = len(units)
    mmd, nrm, rp, st = env.sem("proj_mm"), env.sem("qk_normed"), env.sem("rope_read"), env.sem("rope_sum")
    sq, mn, pw, vv = env.sem("qk_sq"), env.sem("qk_mean"), env.sem("qk_rstd"), env.sem("v_kept")
    tq, tc = env.sem("qk_turned"), env.sem("qk_copied")
    zm, ze = env.sem("az_mm"), env.sem("az_out")
    NV = sum(1 for u in units if u[0] == 1)
    with ExitStack() as ctx:
        s2 = env.sb(ctx, "qk_square", [P, 2, GC])
        ss = env.sb(ctx, "qk_stats", [P, 3, NU, 4])
        nn = env.sb(ctx, "qk_rows", [P, 2, GC])
        ta = env.sb(ctx, "rope_a", [P, 2, GC])
        tb = env.sb(ctx, "rope_b", [P, 2, GC])
        nat = env.sb(ctx, "rope_rows", [P, 2, GC])
        cs = env.sb(ctx, "axial", [P, 2, NT, 32])
        gn = env.sb(ctx, "qk_gain", [P, 2, HD])
        ps = env.banks(ctx, "ps_proj", 4)
        pt = env.banks(ctx, "ps_qk", 2)
        pz = env.banks(ctx, "ps_az", 2)
        block = ctx.enter_context(nc.Block())
        ld = env.sem("axial_loaded")

        @block.sync
        def _(sp):
            sp.dma_start(cs[:, :, :, :], A["k_axial"]).then_inc(ld.h, 16)
            sp.dma_start(gn[:, 0, :], A["q_norm_g_2"][layer:layer + 1, :].to_broadcast([P, HD])).then_inc(ld.h, 16)
            sp.dma_start(gn[:, 1, :], A["k_norm_g_2"][layer:layer + 1, :].to_broadcast([P, HD])).then_inc(ld.h, 16)
            env.load_groups(sp, g0 + 3 + 1)

        def turned(u):
            return sum(2 if g == 0 else 1 for g, _, _ in units[:u + 1])

        @block.tensor
        def _(pe):
            def turn(u):
                g, t, nh = units[u]
                pe.wait_ge(st.h, st.at(u + 1))
                for x in range(nh // 2):
                    n = turned(u - 1) + x
                    if n >= 2:
                        pe.wait_ge(tc.h, tc.at(n - 1))
                    pe.transpose(pt[n % 2][:, 0:P], nat[:, u % 2, x * P:(x + 1) * P], env.ident[:, :]).then_inc(tq.h, 1)

            for u, (g, t, nh) in enumerate(units):
                w = env.group_here(pe, g0 + g)
                if u >= 4:
                    pe.wait_ge(nrm.h, nrm.at(u - 3))
                    pe.wait_ge(sq.h, sq.at(u - 3))
                    if units[u - 4][0] == 1:
                        pe.wait_ge(vv.h, vv.at(units[u - 4][1] + 1))
                for k in range(KT):
                    mm = pe.matmul(ps[u % 4][:, 0:GC], hT[:, k, t * P:(t + 1) * P], w[:, k, :],
                                   start=(k == 0), stop=(k == KT - 1))
                mm.then_inc(mmd.h, 1)
                if u + 1 == NU or units[u + 1][0] != g:
                    pe.wait_ge(mmd.h, mmd.at(u + 1))
                    pe.sem_inc(env.sem("w_used").h, 1)
                if u >= 3:
                    turn(u - 3)
            w = env.group_here(pe, g0 + 2)
            for z, (m, (c0, n)) in enumerate(zun):
                if z >= 2:
                    pe.wait_ge(ze.h, ze.at(z - 1))
                for k in range(KT):
                    mm = pe.matmul(pz[z % 2][:, 0:n], w[:, k, m * P:(m + 1) * P], hT[:, k, c0:c0 + n],
                                   start=(k == 0), stop=(k == KT - 1))
                mm.then_inc(zm.h, 1)
                if z < 3:
                    turn(NU - 3 + z)
            pe.wait_ge(zm.h, zm.at(len(zun)))
            pe.sem_inc(env.sem("w_used").h, 1)

        @block.scalar
        def _(act):
            def copy_turned(u):
                g, t, nh = units[u]
                for x in range(nh // 2):
                    n = turned(u - 1) + x
                    act.wait_ge(tq.h, tq.at(n + 1))
                    ts = slice(t * P, (t + 1) * P)
                    if g == 0:
                        ins = act.activation(QT[:, x, ts], pt[n % 2][:, 0:P], ACT.Copy)
                    else:
                        for kv in range(2):
                            lo = slice(HD * kv, HD * (kv + 1))
                            ins = act.activation(keys[kv][lo, ts], pt[n % 2][lo, 0:P], ACT.Copy)
                    ins.then_inc(tc.h, 1)

            for u, (g, t, nh) in enumerate(units):
                act.wait_ge(mmd.h, mmd.at(u + 1))
                if u >= 2:
                    act.wait_ge(mn.h, mn.at(u - 1))
                act.activation(s2[:, u % 2, 0:nh * HD], ps[u % 4][:, 0:nh * HD], ACT.Square).then_inc(sq.h, 1)
                if g == 1:
                    act.activation(VN[:, t, :], ps[u % 4][:, P:2 * P], ACT.Copy).then_inc(vv.h, 1)
                if u >= 4:
                    copy_turned(u - 4)
            for z, (m, (c0, n)) in enumerate(zun):
                if z < 4:
                    copy_turned(NU - 4 + z)
                act.wait_ge(zm.h, zm.at(z + 1))
                act.activation(aT[:, m, c0:c0 + n], pz[z % 2][:, 0:n], ACT.Silu).then_inc(ze.h, 1)

        @block.vector
        def _(dve):
            link = Link(dve, env.sem("dve_chain"))
            for kv in range(2):
                link(dve.memset(keys[kv][HD * (1 - kv):HD * (2 - kv), :], 0.0))
            dve.wait_ge(ld.h, ld.at(48))

            def mean(u):
                nh = units[u][2]
                dve.wait_ge(sq.h, sq.at(u + 1))
                link(dve.tensor_reduce(ss[:, 0, u, 0:nh], s2[:, u % 2, 0:nh * HD].rearrange("p (h e) -> p h e", e=HD),
                                       AXX, ALU.add))
                dve.tensor_scalar(ss[:, 1, u, 0:nh], ss[:, 0, u, 0:nh], 1.0 / HD, EPS, ALU.mult, ALU.add).then_inc(mn.h, 1)

            mean(0)
            for u, (g, t, nh) in enumerate(units):
                if u + 1 < NU:
                    mean(u + 1)
                w = nh * HD
                v3 = lambda a: a[:, u % 2, 0:w].rearrange("p (h e) -> p h e", e=HD)
                v4 = lambda a: a[:, u % 2, 0:w].rearrange("p (h j x) -> p h j x", j=32, x=2)
                dve.wait_ge(pw.h, pw.at(u + 1))
                if u >= 2:
                    dve.wait_ge(st.h, st.at(u - 1))
                if g == 1:
                    dve.wait_ge(vv.h, vv.at(t + 1))
                dve.tensor_tensor(v3(nn), ps[u % 4][:, 0:w].rearrange("p (h e) -> p h e", e=HD),
                                  ss[:, 2, u, 0:nh, None].to_broadcast([P, nh, HD]), ALU.mult).then_inc(nrm.h, 1)
                dve.wait_ge(nrm.h, nrm.at(u + 1))
                if t >= NT:
                    dve.tensor_tensor(v3(ta), v3(nn), gn[:, g, None, :].to_broadcast([P, nh, HD]), ALU.mult)
                    dve.memset(tb[:, u % 2, 0:w], 0.0).then_inc(rp.h, 1)
                    continue
                link(dve.tensor_tensor(v3(nn), v3(nn), gn[:, g, None, :].to_broadcast([P, nh, HD]), ALU.mult))
                cosv, sinv = (cs[:, i, t, None, :].to_broadcast([P, nh, 32]) for i in range(2))
                for x in range(2):
                    dve.tensor_tensor(v4(ta)[:, :, :, x], v4(nn)[:, :, :, x], cosv, ALU.mult)
                dve.scalar_tensor_tensor(out=v4(tb)[:, :, :, 0], in0=v4(nn)[:, :, :, 1], scalar=-1.0, in1=sinv,
                                         op0=ALU.mult, op1=ALU.mult)
                dve.tensor_tensor(v4(tb)[:, :, :, 1], v4(nn)[:, :, :, 0], sinv, ALU.mult).then_inc(rp.h, 1)
            link.close()

        @block.gpsimd
        def _(pool):
            def add(u):
                g, t, nh = units[u]
                w = nh * HD
                pool.wait_ge(rp.h, rp.at(u + 1))
                if u >= 2:
                    pool.wait_ge(tq.h, tq.at(turned(u - 2)))
                if g == 0:
                    dst = nat[:, u % 2, 0:w].rearrange("p (i v e) -> p v i e", v=2, e=HD)
                    a, b = (x[:, u % 2, 0:w].rearrange("p (v i e) -> p v i e", v=2, e=HD) for x in (ta, tb))
                else:
                    dst, a, b = (x[:, u % 2, 0:w] for x in (nat, ta, tb))
                pool.tensor_tensor(dst, a, b, ALU.add).then_inc(st.h, 1)

            for u, (g, t, nh) in enumerate(units):
                pool.wait_ge(mn.h, mn.at(u + 1))
                pool.tensor_tensor(ss[:, 2, u, 0:nh], ss[:, 1, u, 0:nh], env.mhalf[:, :].to_broadcast([P, nh]), ALU.pow)\
                    .then_inc(pw.h, 1)
                if u >= 1:
                    add(u - 1)
            add(NU - 1)
    T = turned(NU - 1)
    for s_, c_ in ((mmd, NU), (nrm, NU), (rp, NU), (st, NU), (sq, NU), (mn, NU), (pw, NU), (vv, NV), (tq, T), (tc, T),
                   (zm, len(zun)), (ze, len(zun)), (ld, 48)):
        s_.base += c_
    env.next_group += 3


def stage_attend(env, QT, keys, VN, aT, qtiles):
    nc = env.nc
    units = []
    for t in range(qtiles):
        k0, nk = (0, WT) if t < NT else (NT, WT - NT)
        for h in range(4):
            units.append((t, h, k0, nk))
    U = len(units)
    nch = [-(-nk // 4) for _, _, _, nk in units]
    na = [-(-n // 2) for n in nch]
    nd = [n // 2 for n in nch]
    NC = max(nch)
    NPR = 7
    smm, mx, nb, ex = env.sem("score_mm"), env.sem("max_part"), env.sem("max_ready"), env.sem("prob_exp")
    tA, tD, cA, cD = (env.sem(n) for n in ("turn_a", "turn_d", "prob_copied_act", "prob_copied_dve"))
    pvm, nr, at, ac = (env.sem(n) for n in ("pv_mm", "att_normed", "att_turned", "att_gated"))
    with ExitStack() as ctx:
        pr = env.sb(ctx, "probs", [P, NPR, CH])
        pT = env.sb(ctx, "probs_t", [P, 4, CH])
        st = env.sb(ctx, "soft", [P, 2, 2, NC + 2])
        an = env.sb(ctx, "att_rows", [P, 2, GC])
        ps = env.banks(ctx, "ps_scores", NC)
        pt = env.banks(ctx, "ps_pt", 2)
        pv = env.banks(ctx, "ps_pv", 1)[0]
        block = ctx.enter_context(nc.Block())

        def tiles(u, c):
            return min(4, units[u][3] - 4 * c)

        def before(u, c=0):
            return sum(nch[:u]) + c

        @block.tensor
        def _(pe):
            def scores(u, c):
                if u >= U or c >= nch[u]:
                    return
                t, h, k0, nk = units[u]
                kv, i = divmod(h, 2)
                n = tiles(u, c)
                if u >= 1:
                    pe.wait_ge(ex.h, ex.at(before(u - 1, min(c + 1, nch[u - 1]))))
                pe.matmul(ps[c][:, 0:n * P], QT[:, i, t * P:(t + 1) * P],
                          keys[kv][:, (k0 + 4 * c) * P:(k0 + 4 * c + n) * P], start=True, stop=True).then_inc(smm.h, 1)

            def turn(u, c):
                if u < 0 or c >= nch[u]:
                    return
                pe.wait_ge(ex.h, ex.at(before(u, c + 1)))
                if c % 2 == 0:
                    i = sum(na[:u]) + c // 2
                    if i >= 1:
                        pe.wait_ge(cA.h, cA.at(i))
                else:
                    i = sum(nd[:u]) + c // 2
                    if i >= 1:
                        pe.wait_ge(cD.h, cD.at(i))
                for j in range(tiles(u, c)):
                    mm = pe.transpose(pt[c % 2][:, j * P:(j + 1) * P], pr[:, before(u, c) % NPR, j * P:(j + 1) * P],
                                      env.ident[:, :])
                mm.then_inc((tA, tD)[c % 2].h, 1)

            def values(u, c):
                if u < 0 or c >= nch[u]:
                    return
                t, h, k0, nk = units[u]
                kv = h // 2
                if c % 2 == 0:
                    pe.wait_ge(cA.h, cA.at(sum(na[:u]) + c // 2 + 1))
                else:
                    pe.wait_ge(cD.h, cD.at(sum(nd[:u]) + c // 2 + 1))
                if c == 0 and u >= 1:
                    pe.wait_ge(nr.h, nr.at(u))
                    if h == 0:
                        pe.wait_ge(ac.h, ac.at(u // 4))
                for j in range(tiles(u, c)):
                    k = 4 * c + j
                    mm = pe.matmul(pv[:, 0:HD], pT[:, before(u, c) % 4, j * P:(j + 1) * P],
                                   VN[:, k0 + k, kv * HD:(kv + 1) * HD], start=(k == 0), stop=(k == nk - 1))
                mm.then_inc(pvm.h, 1)

            def rows(v):
                pe.wait_ge(nr.h, nr.at(v + 1))
                for x in range(2):
                    mm = pe.transpose(pv[:, P + x * P:2 * P + x * P], an[:, (v // 4) % 2, x * P:(x + 1) * P],
                                      env.ident[:, :])
                mm.then_inc(at.h, 1)

            for u in range(U + 1):
                v = u - 1
                turn(v, 0)
                scores(u, 0)
                turn(v, 1)
                scores(u, 1)
                scores(u, 2)
                if v % 4 == 0 and v >= 4:
                    rows(v - 1)
                values(v, 0)
                turn(v, 2)
                scores(u, 3)
                values(v, 1)
                turn(v, 3)
                scores(u, 4)
                values(v, 2)
                turn(v, 4)
                values(v, 3)
                values(v, 4)
            rows(U - 1)

        @block.scalar
        def _(act):
            def copy(v, c):
                if c < nch[v]:
                    n = tiles(v, c)
                    i = before(v, c)
                    act.wait_ge(tA.h, tA.at(sum(na[:v]) + c // 2 + 1))
                    if i >= 4:
                        act.wait_ge(pvm.h, pvm.at(i - 3))
                    act.activation(pT[:, i % 4, 0:n * P], pt[0][:, 0:n * P], ACT.Copy).then_inc(cA.h, 1)

            def exp(u, c):
                if c < nch[u]:
                    b, n = u % 2, tiles(u, c)
                    if c == 0:
                        act.wait_ge(nb.h, nb.at(u + 1))
                        if u >= 2:
                            act.wait_ge(nr.h, nr.at(u - 1))
                    i = before(u, c)
                    if i >= NPR:
                        act.wait_ge(pvm.h, pvm.at(i - NPR + 1))
                    act.activation(pr[:, i % NPR, 0:n * P], ps[c][:, 0:n * P], ACT.Exp,
                                   bias=st[:, b, 0, NC + 1:NC + 2], scale=HD ** -0.5,
                                   accum_out=st[:, b, 1, c:c + 1]).then_inc(ex.h, 1)

            for u in range(U):
                exp(u, 0)
                exp(u, 1)
                copy(u, 0)
                exp(u, 2)
                exp(u, 3)
                exp(u, 4)
                copy(u, 2)
                copy(u, 4)

        @block.vector
        def _(dve):
            link = Link(dve, env.sem("dve_chain"))

            def maximum(u, c):
                if u < U and c < nch[u]:
                    dve.wait_ge(smm.h, smm.at(before(u, c + 1)))
                    dve.tensor_reduce(st[:, u % 2, 0, c:c + 1], ps[c][:, 0:tiles(u, c) * P], AXX, ALU.max).then_inc(mx.h, 1)

            def bias(u):
                b = u % 2
                dve.wait_ge(mx.h, mx.at(before(u + 1)))
                if u >= 2:
                    dve.wait_ge(ex.h, ex.at(before(u - 1)))
                link(dve.tensor_reduce(st[:, b, 0, NC:NC + 1], st[:, b, 0, 0:nch[u]], AXX, ALU.max))
                dve.tensor_scalar(st[:, b, 0, NC + 1:NC + 2], st[:, b, 0, NC:NC + 1], -(HD ** -0.5), None, ALU.mult)\
                   .then_inc(nb.h, 1)

            def copy(v, c):
                if v >= 0 and c < nch[v]:
                    n = tiles(v, c)
                    i = before(v, c)
                    dve.wait_ge(tD.h, tD.at(sum(nd[:v]) + c // 2 + 1))
                    if i >= 4:
                        dve.wait_ge(pvm.h, pvm.at(i - 3))
                    dve.tensor_copy(pT[:, i % 4, 0:n * P], pt[1][:, 0:n * P]).then_inc(cD.h, 1)

            def finish(v):
                t, h, k0, nk = units[v]
                b = v % 2
                dve.wait_ge(ex.h, ex.at(before(v + 1)))
                link(dve.tensor_reduce(st[:, b, 1, NC:NC + 1], st[:, b, 1, 0:nch[v]], AXX, ALU.add))
                link(dve.reciprocal(st[:, b, 1, NC + 1:NC + 2], st[:, b, 1, NC:NC + 1]))
                if h == 0 and v >= 8:
                    dve.wait_ge(at.h, at.at(v // 4 - 1))
                dve.wait_ge(pvm.h, pvm.at(before(v + 1)))
                dve.tensor_scalar(an[:, (v // 4) % 2, h * HD:(h + 1) * HD], pv[:, 0:HD], st[:, b, 1, NC + 1:NC + 2], None,
                                  ALU.mult).then_inc(nr.h, 1)

            def gate(v):
                t = units[v][0]
                dve.wait_ge(at.h, at.at(v // 4 + 1))
                y = aT[:, :, t * P:(t + 1) * P]
                dve.tensor_tensor(y, y, pv[:, P:3 * P].rearrange("p (m x) -> p m x", x=P), ALU.mult).then_inc(ac.h, 1)

            for u in range(U + 1):
                v = u - 1
                maximum(u, 0)
                copy(v, 1)
                maximum(u, 1)
                maximum(u, 2)
                if v % 4 == 0 and v >= 4:
                    gate(v - 1)
                maximum(u, 3)
                copy(v, 3)
                maximum(u, 4)
                if u < U:
                    bias(u)
                if v >= 0:
                    finish(v)
            gate(U - 1)
            link.close()
    T = sum(nch)
    for s_, c_ in ((smm, T), (mx, T), (nb, U), (ex, T), (tA, sum(na)), (tD, sum(nd)), (cA, sum(na)), (cD, sum(nd)),
                   (pvm, T), (nr, U), (at, U // 4), (ac, U // 4)):
        s_.base += c_


def stage_fourier(env, hT, uT, yT, with_ctx, zt_d):
    nc, A = env.nc, env.A
    g0 = env.next_group
    chunks = CHUNKS if with_ctx else CHUNKS[:-1]
    units = [(0, m, c, uT) for m in range(2) for c in chunks] + [(1, m, c, yT) for m in range(2) for c in chunks]
    mmd, ev = env.sem("proj_mm"), env.sem("proj_out")
    a_mm, a_ev, b_mm, b_ev = env.sem("ch_mm"), env.sem("ch_out"), env.sem("t1_mm"), env.sem("t1_out")
    c_mm, c_ev = env.sem("t2_mm"), env.sem("t2_out")
    a_ed = env.sem("ch_out_dve")
    ml = [env.sem(f"dft_loaded{i}") for i in range(3)]
    zs = [env.sem(f"z_stored{i}") for i in range(2)]
    zl = [env.sem(f"z_loaded{i}") for i in range(4)]
    cl = env.sem("dft_const")
    NB = 16
    NA = NB + (2 if with_ctx else 0)
    with ExitStack() as ctx:
        ch = env.sb(ctx, "dft_ch", [P, 3 * P])
        a = env.sb(ctx, "ch_rows", [P, 2, 3 * GC])
        m16 = env.sb(ctx, "dft_t1", [P, 3, 2, P])
        z = env.sb(ctx, "t1_rows", [P, 2, 2 * GC])
        zt = env.sb(ctx, "t2_rows", [P, 4, 2 * GC])
        m128 = env.sb(ctx, "dft_t2", [P, 2, P])
        mctx = env.sb(ctx, "dft_ctx", [P, 2, 2, CTX])
        ps = env.banks(ctx, "ps_in", 2)
        pa = env.banks(ctx, "ps_ch", 2)
        pb = env.banks(ctx, "ps_t1", 2)
        pc = env.banks(ctx, "ps_t2", 2)
        block = ctx.enter_context(nc.Block())

        @block.sync
        def _(sp):
            env.load_groups(sp, g0 + 2)
            sp.dma_start(ch[:, :], A["k_dft_ch"]).then_inc(cl.h, 16)
            sp.dma_start(m128[:, :, :], A["k_dft_128"]).then_inc(cl.h, 16)
            sp.dma_start(mctx[:, :, :, :], A["k_dft_ctx"]).then_inc(cl.h, 16)
            for b in range(NB):
                if b >= 3:
                    sp.wait_ge(b_mm.h, b_mm.at(b - 2))
                sp.dma_start(m16[:, b % 3, :, :], A["k_dft_16"][b]).then_inc(ml[b % 3].h, 16)
                if b >= 1:
                    sp.wait_ge(b_ev.h, b_ev.at(b))
                    sp.dma_start(zt_d[8 * (b - 1):8 * b].rearrange("a k c -> (a k) c"), z[:, (b - 1) % 2, :])\
                        .then_inc(zs[(b - 1) % 2].h, 16)
            sp.wait_ge(b_ev.h, b_ev.at(NB))
            sp.dma_start(zt_d[8 * (NB - 1):8 * NB].rearrange("a k c -> (a k) c"), z[:, (NB - 1) % 2, :])\
                .then_inc(zs[(NB - 1) % 2].h, 16)
            for i in range(2):
                sp.wait_ge(zs[i].h, zs[i].at(16 * NB // 2))
            for k in range(NB):
                if k >= 4:
                    sp.wait_ge(c_mm.h, c_mm.at(k - 3))
                sp.dma_start(zt[:, k % 4, :], zt_d[:, k, :]).then_inc(zl[k % 4].h, 16)
            env.load_groups(sp, g0 + 3)

        @block.tensor
        def _(pe):
            def project(u):
                g, m, (c0, n), dst = units[u]
                w = env.group_here(pe, g0 + g)
                if u >= 2:
                    pe.wait_ge(ev.h, ev.at(u - 1))
                for k in range(KT):
                    mm = pe.matmul(ps[u % 2][:, 0:n], w[:, k, m * P:(m + 1) * P], hT[:, k, c0:c0 + n],
                                   start=(k == 0), stop=(k == KT - 1))
                mm.then_inc(mmd.h, 1)
                if u + 1 == len(units) or units[u + 1][0] != g:
                    pe.wait_ge(mmd.h, mmd.at(u + 1))
                    pe.sem_inc(env.sem("w_used").h, 1)

            def channels(b):
                if b >= 1:
                    pe.wait_ge(a_ev.h, a_ev.at(b))
                    pe.wait_ge(a_ed.h, a_ed.at(b))
                for m in range(2):
                    if b < NB:
                        lhs = uT[:, m, b * P:(b + 1) * P]
                    else:
                        lhs = uT[:, m, S + (b - NB) * P:S + (b - NB + 1) * P]
                    mm = pe.matmul(pa[m][:, 0:3 * P], lhs, ch[:, :], start=True, stop=True)
                mm.then_inc(a_mm.h, 1)

            def first_points(b):
                pe.wait_ge(a_ev.h, a_ev.at(b + 1))
                pe.wait_ge(a_ed.h, a_ed.at(b + 1))
                pe.wait_ge(ml[b % 3].h, ml[b % 3].at(16 * (b // 3 + 1)))
                if b >= 2:
                    pe.wait_ge(b_ev.h, b_ev.at(b - 1))
                pe.matmul(pb[b % 2][:, :], m16[:, b % 3, 0, :], a[:, b % 2, GC:3 * GC], start=True, stop=False)
                pe.matmul(pb[b % 2][:, :], m16[:, b % 3, 1, :], a[:, b % 2, 0:2 * GC], start=False, stop=True).then_inc(b_mm.h, 1)

            half = len(units) // 2
            for u in range(half):
                project(u)
            pe.wait_ge(ev.h, ev.at(half))
            pe.wait_ge(cl.h, cl.at(48))
            channels(0)
            nxt = half
            for b in range(NB):
                if nxt < len(units) and b % 2:
                    project(nxt)
                    nxt += 1
                if b + 1 < NB:
                    channels(b + 1)
                first_points(b)
            for u in range(nxt, len(units)):
                project(u)
            for k in range(NB):
                pe.wait_ge(zl[k % 4].h, zl[k % 4].at(16 * (k // 4 + 1)))
                if k % 4 == 0 and k >= 4:
                    pe.wait_ge(c_ev.h, c_ev.at(2 * (k // 4)))
                for m in range(2):
                    for part in range(2):
                        mm = pe.matmul(pc[m][:, (k % 4) * P:(k % 4 + 1) * P], zt[:, k % 4, part * GC + m * P:part * GC + (m + 1) * P],
                                       m128[:, part, :], start=(part == 0), stop=(part == 1))
                mm.then_inc(c_mm.h, 1)
            if with_ctx:
                pe.wait_ge(c_ev.h, c_ev.at(8))
                for j in range(2):
                    channels(NB + j)
                pe.wait_ge(a_ev.h, a_ev.at(NB + 2))
                pe.wait_ge(a_ed.h, a_ed.at(NB + 2))
                for m in range(2):
                    for j in range(2):
                        for part in range(2):
                            mm = pe.matmul(pc[m][:, 0:CTX], a[:, j, (1 + part) * GC + m * P:(1 + part) * GC + (m + 1) * P],
                                           mctx[:, j, part, :], start=(j == 0 and part == 0), stop=(j == 1 and part == 1))
                mm.then_inc(c_mm.h, 1)

        def ch_view(b, m):
            return a[:, b % 2, :].rearrange("p (s c) -> p s c", s=3)[:, :, m * P:(m + 1) * P]

        @block.scalar
        def _(act):
            def project_out(u):
                g, m, (c0, n), dst = units[u]
                act.wait_ge(mmd.h, mmd.at(u + 1))
                out, src = dst[:, m, c0:c0 + n], ps[u % 2][:, 0:n]
                if g == 0 and c0 < S:
                    out = dst[:, m, 0:S].rearrange("p (b t a) -> p t b a", b=NB, a=8)[:, c0 // P:(c0 + n) // P]
                    src = src.rearrange("p (t b a) -> p t b a", b=NB, a=8)
                act.activation(out, src, ACT.Copy if g == 0 else ACT.Silu).then_inc(ev.h, 1)

            def channels_out(b):
                act.wait_ge(a_mm.h, a_mm.at(b + 1))
                if 2 <= b < NB:
                    act.wait_ge(b_mm.h, b_mm.at(b - 1))
                act.activation(ch_view(b, 0), pa[0][:, 0:3 * P].rearrange("p (s c) -> p s c", s=3), ACT.Copy).then_inc(a_ev.h, 1)

            half = len(units) // 2
            for u in range(half):
                project_out(u)
            nxt = half
            channels_out(0)
            for b in range(NB):
                if nxt < len(units) and b % 2:
                    project_out(nxt)
                    nxt += 1
                if b + 1 < NB:
                    channels_out(b + 1)
                act.wait_ge(b_mm.h, b_mm.at(b + 1))
                if b >= 2:
                    act.wait_ge(zs[b % 2].h, zs[b % 2].at(16 * (b // 2)))
                act.activation(z[:, b % 2, :], pb[b % 2][:, :], ACT.Copy).then_inc(b_ev.h, 1)
            for u in range(nxt, len(units)):
                project_out(u)
            if with_ctx:
                for j in range(2):
                    channels_out(NB + j)

        @block.vector
        def _(dve):
            for b in range(NB):
                dve.wait_ge(a_mm.h, a_mm.at(b + 1))
                if b >= 2:
                    dve.wait_ge(b_mm.h, b_mm.at(b - 1))
                dve.tensor_copy(ch_view(b, 1), pa[1][:, 0:3 * P].rearrange("p (s c) -> p s c", s=3)).then_inc(a_ed.h, 1)
            dve.wait_ge(ev.h, ev.at(len(units)))
            for q in range(NB // 4):
                dve.wait_ge(c_mm.h, c_mm.at(4 * (q + 1)))
                for m in range(2):
                    y = yT[:, m, 0:S].rearrange("p (b a) -> p a b", a=NB)[:, 4 * q:4 * q + 4, :]
                    dve.tensor_tensor(y, y, pc[m][:, :].rearrange("p (a b) -> p a b", b=P), ALU.mult).then_inc(c_ev.h, 1)
            if with_ctx:
                for j in range(2):
                    dve.wait_ge(a_mm.h, a_mm.at(NB + j + 1))
                    dve.tensor_copy(ch_view(NB + j, 1), pa[1][:, 0:3 * P].rearrange("p (s c) -> p s c", s=3)).then_inc(a_ed.h, 1)
                dve.wait_ge(c_mm.h, c_mm.at(NB + 1))
                for m in range(2):
                    dve.tensor_tensor(yT[:, m, S:W], yT[:, m, S:W], pc[m][:, 0:CTX], ALU.mult).then_inc(c_ev.h, 1)
    x = 1 if with_ctx else 0
    for s_, c_ in ((mmd, len(units)), (ev, len(units)), (a_mm, NA), (a_ev, NA), (a_ed, NA), (b_mm, NB), (b_ev, NB),
                   (c_mm, NB + x), (c_ev, 8 + 2 * x), (cl, 48)):
        s_.base += c_
    for i in range(3):
        ml[i].base += 16 * len(range(i, NB, 3))
    for i in range(2):
        zs[i].base += 16 * NB // 2
    for i in range(4):
        zl[i].base += 16 * NB // 4
    env.next_group += 2


def stage_conv(env, layer, hT, yT, with_ctx):
    nc = env.nc
    chunks = CHUNKS if with_ctx else CHUNKS[:-1]
    N = len(chunks)
    gt = env.sem("conv_gated")
    w3 = env.cols("conv_w_2", 12)
    with ExitStack() as ctx:
        edge = env.sb(ctx, "left_edges", [P, 2, N])
        tmp = env.sb(ctx, "taps", [P, 2, CH])
        zb = env.sb(ctx, "cz_silu", [P, 2, CH])
        proj = Split(env, ctx, hT, [("t", chunks, "act"), ("t", chunks, "dve"), ("t", chunks, "dve"), ("t", chunks, "act")], 2, 2)
        act_out, dve_out = proj.out["act"], proj.out["dve"]
        block = ctx.enter_context(nc.Block())

        @block.sync
        def _(sp):
            env.load_groups(sp, proj.g0 + 4)

        @block.tensor
        def _(pe):
            proj.tensor(pe)

        @block.scalar
        def _(act):
            def take(act, g, chunk, banks):
                c0, n = chunk
                x = chunks.index(chunk)
                if g == 3 and x >= 1:
                    act.wait_ge(gt.h, gt.at(x))
                for m, bank in enumerate(banks):
                    if g == 0:
                        ins = act.activation(yT[:, m, c0:c0 + n], bank[:, 0:n], ACT.Copy)
                    else:
                        ins = act.activation(zb[:, m, 0:n], bank[:, 0:n], ACT.Silu)
                return ins

            proj.scalar(act, take)

        @block.gpsimd
        def _(pool):
            for x, (c0, n) in enumerate(chunks):
                pool.wait_ge(act_out.h, act_out.at(N + x + 1))
                pool.wait_ge(dve_out.h, dve_out.at(N + x + 1))
                y = yT[:, :, c0:c0 + n]
                pool.tensor_tensor(y, y, zb[:, :, 0:n], ALU.mult).then_inc(gt.h, 1)

        @block.vector
        def _(dve):
            link = Link(dve, env.sem("dve_chain"))

            def take(dve, g, chunk, banks):
                c0, n = chunk
                if g == 1:
                    dve.wait_ge(act_out.h, act_out.at(chunks.index(chunk) + 1))
                for m, bank in enumerate(banks):
                    y = yT[:, m, c0:c0 + n]
                    ins = dve.tensor_tensor(y, y if g == 1 else tmp[:, m, 0:n], bank[:, 0:n], ALU.mult)
                return ins

            def taps(g, x, k0):
                if g != 2 or k0 % 4:
                    return
                x -= 2 * N
                c0, n = chunks[x]
                if x == 0 and k0 == 0:
                    dve.wait_ge(dve_out.h, dve_out.at(N))
                    for j in range(1, N):
                        c = chunks[j][0]
                        ins = dve.tensor_copy(edge[:, :, j:j + 1], yT[:, :, c - 1:c])
                    link(ins)
                if x >= 1:
                    dve.wait_ge(dve_out.h, dve_out.at(N + x))
                m = k0 // 4
                y, t = yT[:, m, :], tmp[:, m, :]
                wc = lambda k: w3[:, (layer * 3 + k) * 2 + m:(layer * 3 + k) * 2 + m + 1]
                link(dve.tensor_scalar(t[:, 0:n], y[:, c0:c0 + n], wc(1), None, ALU.mult))
                link(dve.scalar_tensor_tensor(out=t[:, 1:n], in0=y[:, c0:c0 + n - 1], scalar=wc(0), in1=t[:, 1:n],
                                              op0=ALU.mult, op1=ALU.add))
                if c0 not in (0, S):
                    link(dve.scalar_tensor_tensor(out=t[:, 0:1], in0=edge[:, m, x:x + 1], scalar=wc(0), in1=t[:, 0:1],
                                                  op0=ALU.mult, op1=ALU.add))
                r = n if c0 + n not in (S, W) else n - 1
                link(dve.scalar_tensor_tensor(out=t[:, 0:r], in0=y[:, c0 + 1:c0 + 1 + r], scalar=wc(2), in1=t[:, 0:r],
                                              op0=ALU.mult, op1=ALU.add))

            proj.vector(dve, take, taps)
            link.close()
    gt.base += N
    proj.close()


def stage_output2(env, yT, w_ap, pieces, final):
    nc, A = env.nc, env.A
    tiles = [(src, dst, t, col0 + t * P, gi) for gi, (src, dst, n, col0, _) in enumerate(pieces) for t in range(n)]
    NTI = len(tiles)
    wl, gl = [env.sem(f"wo_loaded{i}") for i in range(4)], env.sem("gate_loaded")
    xl = [env.sem(f"o2_x{i}") for i in range(2)]
    hs = [env.sem(f"o2_stored{i}") for i in range(2)]
    mmd, gd, ad, sq, ms, pw, fn = (env.sem(n) for n in ("out_mm", "out_gated", "out_added", "fin_sq", "fin_mean", "fin_rstd", "fin_done"))
    last = fn if final else ad
    whs, wls, yhs, yls = (env.sem(n) for n in ("w_high", "w_low", "y_high", "y_low"))
    with ExitStack() as ctx:
        g_ = env.sb(ctx, "gates", [P, len(pieces), D])
        x = env.sb(ctx, "x_res", [P, 2, D])
        t_ = env.sb(ctx, "gated", [P, D])
        junk = env.sb(ctx, "junk", [P, D]) if final else None
        fg = env.sb(ctx, "final_gain", [P, D]) if final else None
        yh = env.sb(ctx, "y_high", [P, 2, KT, P], F32R)
        yl = env.sb(ctx, "y_low", [P, 2, KT, P], F32R)
        whi = env.sb(ctx, "w_out_high", [P, KT, D], F32R)
        wlo = env.sb(ctx, "w_out_low", [P, KT, D], F32R)
        raw = env.wring.rearrange("p a k c -> p (a k c)").rearrange("p (s c) -> p s c", s=4)
        st = env.sb(ctx, "fin_stat", [P, 3, NTI])
        ps = [env.banks(ctx, f"ps_o{i}", 2) for i in range(2)]
        block = ctx.enter_context(nc.Block())

        @block.sync
        def _(sp):
            for k in range(KT):
                if k >= 4:
                    sp.wait_ge(wls.h, wls.at(k - 3))
                sp.dma_start(raw[:, k % 4, :], w_ap[k * P:(k + 1) * P, :]).then_inc(wl[k % 4].h, 16)
            for i, (_, _, _, _, gd_) in enumerate(pieces):
                sp.dma_start(g_[:, i, :], gd_.to_broadcast([P, D])).then_inc(gl.h, 16)
            if final:
                sp.dma_start(fg[:, :], A["final_g_2"].rearrange("(a d) -> a d", a=1).to_broadcast([P, D])).then_inc(gl.h, 16)
            for i in range(NTI + 1):
                if i < NTI:
                    src, dst, t, col, gi = tiles[i]
                    if i >= 2:
                        sp.wait_ge(hs[i % 2].h, hs[i % 2].at(16 * (i // 2)))
                    sp.dma_start(x[:, i % 2, :], src[t * P:(t + 1) * P, :]).then_inc(xl[i % 2].h, 16)
                if i >= 1:
                    v = i - 1
                    src, dst, t, col, gi = tiles[v]
                    sp.wait_ge(last.h, last.at(v + 1))
                    sp.dma_start(dst[t * P:(t + 1) * P, :], x[:, v % 2, :]).then_inc(hs[v % 2].h, 16)
            for i in range(2):
                sp.wait_ge(hs[i].h, hs[i].at(16 * len(range(i, NTI, 2))))

        @block.tensor
        def _(pe):
            for i, (src, dst, t, col, gi) in enumerate(tiles):
                if i >= 2:
                    pe.wait_ge(gd.h, gd.at(i - 1))
                pe.wait_ge(yls.h, yls.at(i + 1))
                for half in range(2):
                    sl = slice(half * CH, (half + 1) * CH)
                    for k in range(KT):
                        if i == 0 and half == 0:
                            pe.wait_ge(wls.h, wls.at(k + 1))
                        for n, (y, w) in enumerate(((yh, whi), (yh, wlo), (yl, whi))):
                            mm = pe.matmul(ps[i % 2][half][:, :], y[:, i % 2, k, :], w[:, k, sl],
                                           start=(k == 0 and n == 0), stop=(k == KT - 1 and n == 2))
                mm.then_inc(mmd.h, 1)

        @block.vector
        def _(dve):
            link = Link(dve, env.sem("dve_chain"))
            def low(i):
                col = tiles[i][3]
                dve.wait_ge(yhs.h, yhs.at(i + 1))
                if i >= 2:
                    dve.wait_ge(mmd.h, mmd.at(i - 1))
                dve.tensor_tensor(yl[:, i % 2, :, :], yT[:, :, col:col + P], yh[:, i % 2, :, :].bitcast(F32), ALU.subtract)\
                   .then_inc(yls.h, 1)

            for k in range(KT):
                dve.wait_ge(whs.h, whs.at(k + 1))
                dve.tensor_tensor(wlo[:, k, :], raw[:, k % 4, :], whi[:, k, :].bitcast(F32), ALU.subtract).then_inc(wls.h, 1)
                if k == 0:
                    low(0)
            dve.wait_ge(gl.h, gl.at(16 * (len(pieces) + (1 if final else 0))))
            for i, (src, dst, t, col, gi) in enumerate(tiles):
                if i + 1 < NTI:
                    low(i + 1)
                dve.wait_ge(mmd.h, mmd.at(i + 1))
                if i >= 1:
                    dve.wait_ge(ad.h, ad.at(i))
                for half in range(2):
                    sl = slice(half * CH, (half + 1) * CH)
                    ins = dve.tensor_tensor(t_[:, sl], ps[i % 2][half][:, :], g_[:, gi, sl], ALU.mult)
                ins.then_inc(gd.h, 1)
                dve.wait_ge(gd.h, gd.at(i + 1))
                dve.wait_ge(xl[i % 2].h, xl[i % 2].at(16 * (i // 2 + 1)))
                dve.tensor_tensor(x[:, i % 2, :], x[:, i % 2, :], t_[:, :], ALU.add).then_inc(ad.h, 1)
                if final:
                    dve.wait_ge(sq.h, sq.at(i + 1))
                    dve.tensor_scalar(st[:, 1, i:i + 1], st[:, 0, i:i + 1], 1.0 / D, EPS, ALU.mult, ALU.add).then_inc(ms.h, 1)
                    dve.wait_ge(pw.h, pw.at(i + 1))
                    dve.scalar_tensor_tensor(out=x[:, i % 2, :], in0=x[:, i % 2, :], scalar=st[:, 2, i:i + 1], in1=fg[:, :],
                                             op0=ALU.mult, op1=ALU.mult).then_inc(fn.h, 1)
            link.close()

        @block.scalar
        def _(act):
            def high(i):
                col = tiles[i][3]
                if i >= 2:
                    act.wait_ge(mmd.h, mmd.at(i - 1))
                act.activation(yh[:, i % 2, :, :], yT[:, :, col:col + P], ACT.Copy).then_inc(yhs.h, 1)

            high(0)
            for k in range(KT):
                act.wait_ge(wl[k % 4].h, wl[k % 4].at(16 * (k // 4 + 1)))
                act.activation(whi[:, k, :], raw[:, k % 4, :], ACT.Copy).then_inc(whs.h, 1)
            for i in range(NTI):
                if i + 1 < NTI:
                    high(i + 1)
                if final:
                    act.wait_ge(ad.h, ad.at(i + 1))
                    if i >= 1:
                        act.wait_ge(sq.h, sq.at(i))
                    act.activation(junk[:, :], x[:, i % 2, :], ACT.Square, accum_out=st[:, 0, i:i + 1]).then_inc(sq.h, 1)

        if final:
            @block.gpsimd
            def _(pool):
                for i in range(NTI):
                    pool.wait_ge(ms.h, ms.at(i + 1))
                    pool.tensor_tensor(st[:, 2, i:i + 1], st[:, 1, i:i + 1], env.mhalf[:, :], ALU.pow).then_inc(pw.h, 1)
    f = NTI if final else 0
    for s_, c_ in (*((x, 32) for x in wl), (whs, KT), (wls, KT), (yhs, NTI), (yls, NTI), (gl, 16 * (len(pieces) + (1 if final else 0))), (mmd, NTI), (gd, NTI), (ad, NTI), (sq, f), (ms, f),
                   (pw, f), (fn, f)):
        s_.base += c_
    for i in range(2):
        n = 16 * len(range(i, NTI, 2))
        xl[i].base += n
        hs[i].base += n


def stage_gqa(env, layer, hT, QT, KTt, VN, aT, qtiles, zchunks):
    with ExitStack() as ctx:
        keys = [KTt, env.sb(ctx, "k_second", [P, W])]
        stage_qkv2(env, layer, hT, QT, keys, VN, aT, qtiles, zchunks)
        stage_attend(env, QT, keys, VN, aT, qtiles)


def program(nc, A, upto=99, layers=(0, 1)):
    env = Env(nc, A)
    env.next_group = 0
    with env.stack:
        top = env.stack
        env.cols = lambda key, n: env.vcols[:, env.place[key][0], env.place[key][1]:env.place[key][1] + n]
        env.ident = env.sb(top, "ident", [P, P])
        env.vcols = env.sb(top, "vcols", [P, 2, P])
        env.ones = env.sb(top, "ones", [P, P])
        env.mhalf = env.sb(top, "minus_half", [P, 1])
        env.mask1 = env.sb(top, "mask1", [P, 2 * P])
        env.levmask = env.sb(top, "level_masks", [P, 16, P], mybir.dt.uint8)
        env.headmean = env.sb(top, "head_mean", [P, P])
        env.eps = env.sb(top, "eps", [P, 1])
        env.lb = env.sb(top, "lower_bounds", [P, 3, 2, 2])
        env.invf = env.sb(top, "inv_freq", [P, 32])
        env.sp = env.sb(top, "softplus", [P, 5, 4])
        env.nsp = env.sb(top, "decay_scale", [P, 4])
        env.csilu = env.sb(top, "c_silu", [P, 24])
        env.wring = env.sb(top, "weight_ring", [P, 2, KT, GC])
        env.mods = {t: env.sb(top, f"mod_{t}", [P, 2, 2, KT]) for t in ("one", "l0", "l1")}
        v_d = nc.dram_tensor("v_rows", [S, H1 * HD], F32, kind="Internal").ap()
        gb_d = nc.dram_tensor("gb_rows", [S, H1 * HD], F32, kind="Internal").ap()
        res_d = [nc.dram_tensor(f"res{p}", [S, RW], F32, kind="Internal").ap() for p in range(3)]
        gate_d = [[nc.dram_tensor(f"gate{l}{v}", [1, D], F32, kind="Internal").ap() for v in range(2)] for l in range(2)]
        h_d = A["out"] if upto == 1 else nc.dram_tensor("h_rows", [S, D], F32, kind="Internal").ap()
        env.groups += [(A["w_in"][0], c) for c in (0, 512, 256, 768, 2048, 2304, 2560, 2816, 1024, 1280, 1536, 1792)]
        for l in layers:
            env.groups += [(A["w_in_2"][l], c) for c in (1792, 2560, 2816, 2048, 2304, 1024, 1280, 1536, 3072, 3328, 256, 512, 0, 768)]
        with ExitStack() as one:
            gate = env.sb(one, "gate1", [P, D])
            yaT = env.sb(one, "ya_t", [P, CT, S])
            sumsq = env.sb(one, "ya_sumsq", [P, NT])
            with ExitStack() as pr:
                hT = env.sb(pr, "h_t", [P, KT, S])
                with ExitStack() as tables:
                    env.cosF = env.sb(tables, "cos", [P, NT, 2, 32])
                    env.sinF = env.sb(tables, "sin", [P, NT, 2, 32])
                    slots = [hT[:, :, i * MC:(i + 1) * MC] for i in range(4)]
                    slots += [yaT[:, 2 * i:2 * i + 2, :].rearrange("p a (b c) -> p (a b) c", c=MC) for i in range(2)]
                    stage_vectors(env, slots)
                    stage_mod(env, slots, gate)
                    env.retire("gate_row", "mod_row", "mod_turned", "mod_w_used", *(f"mod_w{g}" for g in range(MG)))
                    m = env.mods["one"]
                    stage_norm(env, hT, [(A["x"][0], NT, 0, (m[:, 0, 0, :], m[:, 0, 1, :]))])
                    stage_recurrent(env, hT, yaT, sumsq)
                    with ExitStack() as qk:
                        QT = env.sb(qk, "q_t", [P, 4, S])
                        KTt = env.sb(qk, "k_t", [P, 4, S])
                        stage_qkvg(env, hT, QT, KTt, v_d, gb_d)
                        stage_dilated(env, hT, QT, KTt, v_d, res_d)
            stage_output1(env, yaT, sumsq, res_d, gb_d, gate, h_d, gate_d)
        if upto == 1:
            return
        env.retire("mod2_w0", "mod2_w1", "mod2_w2", "mod2_w3", "mod2_used", "mod2_gate_cols", "mod2_gate_turned",
                   "gate_stored", "xa_out", "ga_out", "conv_done", "gate_mm", "gate_act", "xa_mm", "ga_mm", "decay_done",
                   "decay_sq",
                   "root_done", "gated_in", "score_mm", "score_min", "prob_exp", "prob_turned",
                   "prob_copied_act", "prob_copied_dve", "pv_mm", "pv_copied")
        zt_d = nc.dram_tensor("t2_rows", [P, 16, 2 * GC], F32, kind="Internal").ap()
        h1_d = nc.dram_tensor("h1_rows", [S, D], F32, kind="Internal").ap()
        c1_d = nc.dram_tensor("c1_rows", [CTX, D], F32, kind="Internal").ap()
        rows = [(h_d, A["ctx_2"][0]), (h1_d, c1_d)]
        for l in layers:
            tag = f"l{l}"
            h_in, c_in = rows[l]
            with ExitStack() as lay:
                yT = env.sb(lay, "y_t", [P, KT, W])
                feat = ExitStack()
                hT = env.sb(feat, "h_t", [P, KT, W])
                m = env.mods[tag]
                stage_norm(env, hT, [(h_in, NT, 0, (m[:, 0, 0, :], m[:, 0, 1, :])),
                                     (c_in, CTX // P, S, (m[:, 1, 0, :], m[:, 1, 1, :]))])
                with_ctx = l == 0
                chunks = CHUNKS if with_ctx else CHUNKS[:-1]
                qtiles = WT if with_ctx else NT
                vN = yT[:, 2:4, :].rearrange("p a (t c) -> p (a t) c", c=GC)
                stage_hgrn_in(env, hT, yT[:, 0:2, :], vN, yT[:, 6:8, :], chunks)
                for d in range(2):
                    stage_hgrn_scan(env, l, d, hT, yT[:, 0:2, :], vN, yT[:, 4:6, :], with_ctx)
                stage_hgrn_norm(env, l, yT[:, 4:6, :], yT[:, 6:8, :], chunks)
                stage_gqa(env, l, hT, yT[:, 0:2, :], yT[:, 6, :], yT[:, 7, :].rearrange("p (t c) -> p t c", c=P),
                          yT[:, 2:4, :], qtiles, chunks)
                stage_fourier(env, hT, yT[:, 0:2, :], yT[:, 6:8, :], with_ctx, zt_d)
                stage_conv(env, l, hT, yT[:, 0:2, :], with_ctx)
                feat.close()
                pieces = [(h_in, A["out"] if l == 1 else h1_d, NT, 0, gate_d[l][0])]
                if with_ctx:
                    pieces.append((c_in, c1_d, CTX // P, S, gate_d[l][1]))
                stage_output2(env, yT, A["w_out_2"][l], pieces, final=l == 1)


def constants():
    i = np.arange(P)
    ident = np.eye(P, dtype=np.float32)
    mask1 = np.zeros((P, 2 * P), np.float32)
    mask1[:, :P][i[None, :] < i[:, None]] = BIG
    mask1[:, P:][i[None, :] > i[:, None]] = BIG
    invf = (np.float32(10000.0) ** (-np.arange(32, dtype=np.float32) / np.float32(32))).astype(np.float32)[None]
    lev = np.zeros((P, 16, P), np.float32)
    for l in range(7):
        same = (i[:, None] >> (l + 1)) == (i[None, :] >> (l + 1))
        kb, qb = (i[:, None] >> l) & 1, (i[None, :] >> l) & 1
        lev[:, l, :] = same & (kb == 0) & (qb == 1)
        lev[:, 8 + l, :] = same & (kb == 1) & (qb == 0)
    lev[:, 7, :] = lev[:, 15, :] = np.eye(P)
    headmean = np.kron(np.eye(2), np.full((HD, HD), 1.0 / HD)).astype(np.float32)
    tok = np.arange(S)
    fr = (np.float32(10000.0) ** (-np.arange(16, dtype=np.float32) / np.float32(16))).astype(np.float32)
    ang = np.concatenate([(tok // 64).astype(np.float32)[:, None] * fr, (tok % 64).astype(np.float32)[:, None] * fr], -1)
    axial = np.stack([np.cos(ang.astype(np.float64)), np.sin(ang.astype(np.float64))], 0).astype(np.float32)
    axial = np.ascontiguousarray(axial.reshape(2, NT, P, 32).transpose(2, 0, 1, 3))
    c64 = 2 * np.pi * np.outer(np.arange(HD), np.arange(HD)) / HD
    two = lambda m: np.kron(np.eye(2), m)
    dft_ch = np.concatenate([two(np.sin(c64)), two(np.cos(c64)), two(-np.sin(c64))], 1).astype(np.float32)
    dft_16 = np.zeros((16, P, 2, P))
    t1, a, k1 = np.arange(16)[:, None], np.arange(8), np.arange(16)[None, :]
    for b in range(16):
        for aa in a:
            th = 2 * np.pi * (t1 * k1 / 16 + (8 * b + aa) * k1 / S)
            dft_16[b][np.ix_(t1[:, 0] * 8 + aa, [0], aa * 16 + k1[0])] = np.cos(th)[:, None, :]
            dft_16[b][np.ix_(t1[:, 0] * 8 + aa, [1], aa * 16 + k1[0])] = -np.sin(th)[:, None, :]
    scale = 1 / np.sqrt(S * HD)
    ph = 2 * np.pi * np.outer(i, i) / P
    dft_128 = np.stack([np.cos(ph), np.sin(ph)], 1) * scale
    tc = np.arange(CTX)
    pc = 2 * np.pi * np.outer(tc, tc) / CTX
    dft_ctx = (np.stack([np.cos(pc), np.sin(pc)], 1) / np.sqrt(CTX * HD)).reshape(2, P, 2, CTX).transpose(1, 0, 2, 3)
    f = lambda x: np.ascontiguousarray(x, dtype=np.float32)
    return {"k_ident": ident, "k_mask1": mask1, "k_invf": invf, "k_levmask": lev, "k_headmean": headmean, "k_axial": axial,
            "k_dft_ch": f(dft_ch), "k_dft_16": f(dft_16), "k_dft_128": f(dft_128), "k_dft_ctx": f(dft_ctx)}


INPUTS = ["x", "c", "positions", "w_ada", "b_ada", "norm_pre", "norm_post", "w_in", "conv_w", "conv_b", "w_rg_a", "b_rg_a",
          "w_rg_x", "b_rg_x", "lru_lambda", "norm_rec", "norm_att", "w_out", "c_2", "ctx_2", "c_ctx_2", "norm_g_2",
          "w_mod_2", "b_mod_2", "w_in_2", "conv_w_2", "q_norm_g_2", "k_norm_g_2", "hgrn_lb_2", "hgrn_norm_g_2",
          "w_out_2", "final_g_2"]


def kernel(**inputs):
    import concourse.bacc as bacc
    from concourse.bass_utils import run_bass_kernel_spmd as _run

    nc = bacc.Bacc("TRN2", target_bir_lowering=False, num_devices=1)
    given = {name: inputs[name] for name in INPUTS}
    given.update(constants())
    arrays, A = {}, {}
    for name, value in given.items():
        a = np.ascontiguousarray(value)
        arrays[f"in_{name}_dram"] = a
        A[name] = nc.dram_tensor(f"in_{name}_dram", a.shape, mybir.dt.from_np(a.dtype), kind="ExternalInput").ap()
    A["out"] = nc.dram_tensor("out_dram", (S, D), F32, kind="ExternalOutput").ap()
    program(nc, A)
    r = _run(nc, [arrays], core_ids=[0])
    return r.results[0]["out_dram"].reshape(1, S, D)
```
